# Optimizing a Trainium2 kernel written in Bass

```python
import math
import jax, jax.numpy as jnp
from jax import lax
import numpy as np

D_MODEL = 1024
BATCH = 1
SEQ = 256
DEPTH = 1

HEAD_DIM = 64
N_HEADS_DIL = 8
N_HEADS_SB = 8
D_DIL = N_HEADS_DIL * HEAD_DIM
D_SB = N_HEADS_SB * HEAD_DIM
D_MIX = D_DIL + D_SB
DIL_PATTERNS = ((128, 1), (512, 4), (2048, 16))
Q_BLOCK = 128
ROPE_THETA = 500000.0
ROPE_DIM = HEAD_DIM // 4
N_MEM = 256
MEM_HEADS = 4
MEM_HEAD_DIM = 128
D_MEM_ATTN = MEM_HEADS * MEM_HEAD_DIM
PEER_HEADS = 8
PEER_NKEYS = 128
PEER_N_EXPERTS = PEER_NKEYS * PEER_NKEYS
PEER_DKEY = 256
PEER_TOPK = 16
PEER_TOKEN_BLOCK = 128
EPS = 1e-6
POS_OFFSET_MAX = 1024

kernel_name = "hybrid_dilated_stickbreaking_peer_block"

def rmsnorm(x, g):
    xf = x.astype(jnp.float32)
    y = xf * lax.rsqrt(jnp.mean(xf * xf, axis=-1, keepdims=True) + EPS)
    return (y * g.astype(jnp.float32)).astype(x.dtype)

def partial_rope(x, positions):
    inv_freq = ROPE_THETA ** (-jnp.arange(0, ROPE_DIM, 2, dtype=jnp.float32) / ROPE_DIM)
    ang = positions.astype(jnp.float32)[:, None, :, None] * inv_freq
    cos, sin = jnp.cos(ang), jnp.sin(ang)
    xf = x.astype(jnp.float32)
    x1 = xf[..., :ROPE_DIM // 2]
    x2 = xf[..., ROPE_DIM // 2:ROPE_DIM]
    out = jnp.concatenate([x1 * cos - x2 * sin, x2 * cos + x1 * sin, xf[..., ROPE_DIM:]], axis=-1)
    return out.astype(x.dtype)

def split_heads(t, n_heads, head_dim):
    b, s, _ = t.shape
    return t.reshape(b, s, n_heads, head_dim).transpose(0, 2, 1, 3)

def merge_heads(t):
    b, h, s, d = t.shape
    return t.transpose(0, 2, 1, 3).reshape(b, s, h * d)

def dilated_window_attention(q, k, v):
    b, h, s, dh = q.shape
    scale = dh ** -0.5
    n_blocks = s // Q_BLOCK

    def block(i):
        start = i * Q_BLOCK
        qb = lax.dynamic_slice_in_dim(q, start, Q_BLOCK, axis=2)
        t = start + jnp.arange(Q_BLOCK)
        outs, lses = [], []
        for window, dilation in DIL_PATTERNS:
            n_k = window // dilation + 1
            idx = t[:, None] - dilation * jnp.arange(n_k)[None, :]
            valid = idx >= 0
            idx = jnp.maximum(idx, 0)
            kg = jnp.take(k, idx, axis=2)
            vg = jnp.take(v, idx, axis=2)
            sc = jnp.einsum('bhqd,bhqjd->bhqj', qb, kg).astype(jnp.float32) * scale
            sc = jnp.where(valid, sc, -jnp.inf)
            m = jnp.max(sc, axis=-1, keepdims=True)
            p = jnp.exp(sc - m)
            den = jnp.sum(p, axis=-1, keepdims=True)
            o = jnp.einsum('bhqj,bhqjd->bhqd', p, vg.astype(jnp.float32)) / den
            outs.append(o)
            lses.append(m + jnp.log(den))
        lse = jnp.concatenate(lses, axis=-1)
        w = jax.nn.softmax(lse, axis=-1)
        o = jnp.einsum('bhqp,bhqpd->bhqd', w, jnp.stack(outs, axis=-2))
        return o.astype(q.dtype)

    out = lax.map(block, jnp.arange(n_blocks))
    return jnp.moveaxis(out, 0, 2).reshape(b, h, s, dh)

def stick_breaking_attention(q, k, v):
    b, h, s, dh = q.shape
    scale = dh ** -0.5
    n_blocks = s // Q_BLOCK
    key_pos = jnp.arange(s)
    vf = v.astype(jnp.float32)

    def block(i):
        start = i * Q_BLOCK
        qb = lax.dynamic_slice_in_dim(q, start, Q_BLOCK, axis=2)
        t = start + jnp.arange(Q_BLOCK)
        z = jnp.einsum('bhqd,bhkd->bhqk', qb, k).astype(jnp.float32) * scale
        causal = key_pos[None, :] < t[:, None]
        log_1m = jnp.where(causal, jax.nn.log_sigmoid(-z), 0.0)
        after = lax.cumsum(log_1m, axis=3, reverse=True) - log_1m
        a = jnp.where(causal, jnp.exp(jax.nn.log_sigmoid(z) + after), 0.0)
        o = jnp.einsum('bhqk,bhkd->bhqd', a, vf)
        return o.astype(q.dtype)

    out = lax.map(block, jnp.arange(n_blocks))
    return jnp.moveaxis(out, 0, 2).reshape(b, h, s, dh)

def memory_cross_attention(h_n, mem_n, w_q, w_kv, g_q, g_k, w_o):
    q = split_heads(h_n @ w_q, MEM_HEADS, MEM_HEAD_DIM)
    kv = mem_n @ w_kv
    k = split_heads(kv[..., :D_MEM_ATTN], MEM_HEADS, MEM_HEAD_DIM)
    v = split_heads(kv[..., D_MEM_ATTN:], MEM_HEADS, MEM_HEAD_DIM)
    q = rmsnorm(q, g_q)
    k = rmsnorm(k, g_k)
    sc = jnp.einsum('bhsd,bhmd->bhsm', q, k).astype(jnp.float32) * (MEM_HEAD_DIM ** -0.5)
    p = jax.nn.softmax(sc, axis=-1)
    o = jnp.einsum('bhsm,bhmd->bhsd', p, v.astype(jnp.float32)).astype(h_n.dtype)
    return merge_heads(o) @ w_o

def peer_ffn(x_n, w_q, sub_keys, u, v):
    b, s, d = x_n.shape
    n_blocks = (b * s) // PEER_TOKEN_BLOCK
    xb = x_n.reshape(n_blocks, PEER_TOKEN_BLOCK, d)

    def block(xc):
        q = (xc @ w_q).reshape(PEER_TOKEN_BLOCK, PEER_HEADS, 2, PEER_DKEY // 2)
        sc = jnp.einsum('thpc,hpnc->thpn', q, sub_keys).astype(jnp.float32)
        top_s, top_i = lax.top_k(sc, PEER_TOPK)
        cand_s = top_s[:, :, 0, :, None] + top_s[:, :, 1, None, :]
        cand_i = top_i[:, :, 0, :, None] * PEER_NKEYS + top_i[:, :, 1, None, :]
        cand_s = cand_s.reshape(PEER_TOKEN_BLOCK, PEER_HEADS, PEER_TOPK * PEER_TOPK)
        cand_i = cand_i.reshape(PEER_TOKEN_BLOCK, PEER_HEADS, PEER_TOPK * PEER_TOPK)
        best_s, best_pos = lax.top_k(cand_s, PEER_TOPK)
        experts = jnp.take_along_axis(cand_i, best_pos, axis=-1)
        g = jax.nn.softmax(best_s, axis=-1)
        ue = jnp.take(u, experts, axis=0)
        ve = jnp.take(v, experts, axis=0)
        act = jax.nn.gelu(jnp.einsum('td,thkd->thk', xc, ue).astype(jnp.float32), approximate=False)
        y = jnp.einsum('thk,thkd->td', (g * act).astype(ve.dtype), ve)
        return y

    y = lax.map(block, xb)
    return y.reshape(b, s, d)

def setup_inputs(seed: int = 0) -> dict:
    key = jax.random.key(seed)
    ks = jax.random.split(key, 24)
    f32 = jnp.float32

    def nrm(k, shape, scale):
        return jax.random.normal(k, shape, f32) * scale

    def gain(k, shape):
        return 1.0 + 0.02 * jax.random.normal(k, shape, f32)

    x = jax.random.normal(ks[0], (BATCH, SEQ, D_MODEL), f32)
    mem = jax.random.normal(ks[1], (BATCH, N_MEM, D_MODEL), f32)
    offset = jax.random.randint(ks[2], (BATCH, 1), 0, POS_OFFSET_MAX, dtype=jnp.int32)
    positions = (offset + jnp.arange(SEQ, dtype=jnp.int32)[None, :]).astype(jnp.int32)
    return {
        "x": x,
        "mem": mem,
        "positions": positions,
        "norm_mix_g": gain(ks[3], (DEPTH, D_MODEL)),
        "w_in": nrm(ks[4], (DEPTH, D_MODEL, 3 * D_MIX), D_MODEL ** -0.5),
        "qnorm_g_dil": gain(ks[5], (DEPTH, HEAD_DIM)),
        "knorm_g_dil": gain(ks[6], (DEPTH, HEAD_DIM)),
        "out_norm_g_dil": gain(ks[7], (DEPTH, D_DIL)),
        "out_norm_g_sb": gain(ks[8], (DEPTH, D_SB)),
        "w_out": nrm(ks[9], (DEPTH, D_MIX, D_MODEL), D_MIX ** -0.5),
        "norm_mem_g": gain(ks[10], (DEPTH, D_MODEL)),
        "norm_memtok_g": gain(ks[11], (DEPTH, D_MODEL)),
        "w_q_mem": nrm(ks[12], (DEPTH, D_MODEL, D_MEM_ATTN), D_MODEL ** -0.5),
        "w_kv_mem": nrm(ks[13], (DEPTH, D_MODEL, 2 * D_MEM_ATTN), D_MODEL ** -0.5),
        "qnorm_g_mem": gain(ks[14], (DEPTH, MEM_HEAD_DIM)),
        "knorm_g_mem": gain(ks[15], (DEPTH, MEM_HEAD_DIM)),
        "w_o_mem": nrm(ks[16], (DEPTH, D_MEM_ATTN, D_MODEL), D_MEM_ATTN ** -0.5),
        "norm_ffn_g": gain(ks[17], (DEPTH, D_MODEL)),
        "w_q_peer": nrm(ks[18], (DEPTH, D_MODEL, PEER_HEADS * PEER_DKEY), D_MODEL ** -0.5),
        "peer_sub_keys": nrm(ks[19], (DEPTH, PEER_HEADS, 2, PEER_NKEYS, PEER_DKEY // 2), (PEER_DKEY // 2) ** -0.5),
        "peer_u": nrm(ks[20], (DEPTH, PEER_N_EXPERTS, D_MODEL), D_MODEL ** -0.5),
        "peer_v": nrm(ks[21], (DEPTH, PEER_N_EXPERTS, D_MODEL), 0.25),
    }

def reference(x, mem, positions, norm_mix_g, w_in, qnorm_g_dil, knorm_g_dil, out_norm_g_dil,
              out_norm_g_sb, w_out, norm_mem_g, norm_memtok_g, w_q_mem, w_kv_mem, qnorm_g_mem,
              knorm_g_mem, w_o_mem, norm_ffn_g, w_q_peer, peer_sub_keys, peer_u, peer_v):
    h = x
    for l in range(DEPTH):
        h_n = rmsnorm(h, norm_mix_g[l])
        proj = h_n @ w_in[l]
        q_a = proj[..., 0 * D_DIL:1 * D_DIL]
        k_a = proj[..., 1 * D_DIL:2 * D_DIL]
        v_a = proj[..., 2 * D_DIL:3 * D_DIL]
        off = 3 * D_DIL
        q_b = proj[..., off + 0 * D_SB:off + 1 * D_SB]
        k_b = proj[..., off + 1 * D_SB:off + 2 * D_SB]
        v_b = proj[..., off + 2 * D_SB:off + 3 * D_SB]

        qa = partial_rope(rmsnorm(split_heads(q_a, N_HEADS_DIL, HEAD_DIM), qnorm_g_dil[l]), positions)
        ka = partial_rope(rmsnorm(split_heads(k_a, N_HEADS_DIL, HEAD_DIM), knorm_g_dil[l]), positions)
        va = split_heads(v_a, N_HEADS_DIL, HEAD_DIM)
        o_a = merge_heads(dilated_window_attention(qa, ka, va))

        qb = split_heads(q_b, N_HEADS_SB, HEAD_DIM)
        kb = split_heads(k_b, N_HEADS_SB, HEAD_DIM)
        vb = split_heads(v_b, N_HEADS_SB, HEAD_DIM)
        o_b = merge_heads(stick_breaking_attention(qb, kb, vb))

        mixed = jnp.concatenate([rmsnorm(o_a, out_norm_g_dil[l]), rmsnorm(o_b, out_norm_g_sb[l])], axis=-1)
        h = h + mixed @ w_out[l]

        h_n = rmsnorm(h, norm_mem_g[l])
        mem_n = rmsnorm(mem, norm_memtok_g[l])
        h = h + memory_cross_attention(h_n, mem_n, w_q_mem[l], w_kv_mem[l], qnorm_g_mem[l],
                                       knorm_g_mem[l], w_o_mem[l])

        h_n = rmsnorm(h, norm_ffn_g[l])
        h = h + peer_ffn(h_n, w_q_peer[l], peer_sub_keys[l], peer_u[l], peer_v[l])
    return h


_drawn_inputs = setup_inputs


def setup_inputs(seed=0):
    import zlib

    import numpy as np

    out = dict(_drawn_inputs(seed))
    spreads = {}
    factors = {'qnorm_g_dil': 4.009,
     'knorm_g_dil': 4.029,
     'out_norm_g_dil': 4.088,
     'out_norm_g_sb': 4.352,
     'norm_mem_g': 8.0,
     'norm_memtok_g': 8.0,
     'qnorm_g_mem': 8.0,
     'knorm_g_mem': 8.0,
     'norm_ffn_g': 30.22}
    for name, (base, spread) in spreads.items():
        noise = np.random.default_rng([zlib.crc32(name.encode()), seed]).standard_normal(out[name].shape)
        drawn = base * np.exp(spread * noise) if base else spread * noise
        out[name] = __import__('jax').numpy.asarray(drawn.astype(out[name].dtype))
    for name, factor in factors.items():
        out[name] = (out[name] * factor).astype(out[name].dtype)
    return out
```

```python
from contextlib import ExitStack

import numpy as np
import concourse.bass as bass
import concourse.mybir as mybir

F32 = mybir.dt.float32
F32R = mybir.dt.float32r
I32 = mybir.dt.int32
U32 = mybir.dt.uint32
ALU = mybir.AluOpType
ACT = mybir.ActivationFunctionType
AX = mybir.AxisListType.X

P = 128
D = 1024
SEQ = 256
NT = SEQ // P
KD = D // P
HD = 64
NH = 8
ROPE = HD // 4
HALF = ROPE // 2
MH, MHD = 4, 128
PH, TOPK = 8, 16
NKEY = 128
NBLK = 2 * PH
EPS = 1e-6
CAND = [TOPK // (a + 1) for a in range(TOPK)]
NCAND = sum(CAND)
TAPS = (128, 512, 2048), (1, 4, 16)
WSLOTS = 7
WHALF = 2048
(Q_A, K_A, Q_B, K_B, V_B, V_A, K_MEM, V_MEM, OUT0, OUT1, Q_MEM, O_MEM, PEER0) = range(13)
PEER_UNITS = 4
KEYS_HALF = 2 * (PEER0 + PEER_UNITS)
LOWEST = -3.0e38
MASKED = -1.0e30
TWO_PI_PARTS = (6.28125, 0.0019340515136718750, float(2 * np.pi - 6.28125 - 0.0019340515136718750))
MAGIC = 1.5 * 2.0 ** 23
PI_SAFE = 3.1415925


class Signal:

    def __init__(self, sem):
        self.sem, self.n = sem, 0

    def on(self, ins, by=1):
        ins.then_inc(self.sem, by)
        self.n += by
        return self.n


def hybrid_layer(nc, x, mem, pos, weights, cols, head_gains, u_t, v_t, out):
    inv_freq = np.float32(500000.0) ** (-np.arange(0, ROPE, 2, dtype=np.float32) / np.float32(ROPE))
    with ExitStack() as ctx:
        def sb(name, shape, dt=F32):
            return ctx.enter_context(nc.sbuf_tensor(name, shape, dt))

        def sem(name):
            return ctx.enter_context(nc.semaphore(name))

        big = sb("big", [P, NKEY * SEQ])
        ring = [big[:, s * WHALF:(s + 1) * WHALF] for s in range(WSLOTS)]
        S0 = WSLOTS * WHALF

        def scratch(at, n):
            return big[:, S0 + at:S0 + at + n]

        xt = scratch(0, 2048).rearrange("p (k t) -> p k t", k=KD)
        memt = scratch(2048, 2048).rearrange("p (k t) -> p k t", k=KD)
        mixed = scratch(2048, 2048).rearrange("p (t n) -> p t n", t=NT)
        qk_a = scratch(4096, 2048).rearrange("p (t w n) -> p t w n", t=NT, w=2)
        q_mem = scratch(4096, 1024).rearrange("p (t n) -> p t n", t=NT)
        sq_mem = scratch(5120, 1024).rearrange("p (t n) -> p t n", t=NT)
        q_at = scratch(6144, 1024).rearrange("p (b t) -> p b t", b=4)
        k_at = scratch(7168, 1024).rearrange("p (b t) -> p b t", b=4)
        q_bt = scratch(8192, 1024).rearrange("p (b t) -> p b t", b=4)
        k_bt = scratch(9216, 1024).rearrange("p (b t) -> p b t", b=4)
        v_a = scratch(10240, 1024).rearrange("p (t n) -> p t n", t=NT)
        v_b = scratch(11264, 1024).rearrange("p (t n) -> p t n", t=NT)
        k_mem = scratch(12288, 1024).rearrange("p (t n) -> p t n", t=NT)
        v_mem = scratch(13312, 1024).rearrange("p (t n) -> p t n", t=NT)
        k_memt = scratch(14336, 1024).rearrange("p (b t) -> p b t", b=4)
        sticks = scratch(15360, 3072).rearrange("p (h c) -> p h c", h=NH)
        q_peert = scratch(2048, 4096).rearrange("p (b t) -> p b t", b=NBLK)
        scores = scratch(6144, 4096).rearrange("p (t b n) -> p t b n", t=NT, b=NBLK)
        chosen = scratch(2048, 6 * P).rearrange("p (n k) -> p n k", n=6)
        top_val = scratch(2816, 512).rearrange("p (t b k) -> p t b k", t=NT, b=NBLK)
        top_pos = scratch(3328, 512).bitcast(U32).rearrange("p (t b k) -> p t b k", t=NT, b=NBLK)
        top_id = scratch(3840, 512).rearrange("p (t b k) -> p t b k", t=NT, b=NBLK)
        cand_val = scratch(4352, PH * NCAND).rearrange("p (h c) -> p h c", h=PH)
        cand_id = scratch(4752, PH * NCAND).rearrange("p (h c) -> p h c", h=PH)
        best = scratch(5152, P).rearrange("p (h k) -> p h k", h=PH)
        best_pos = scratch(5280, P).bitcast(U32).rearrange("p (h k) -> p h k", h=PH)
        best_at = scratch(5408, P).rearrange("p (h k) -> p h k", h=PH)
        expert = scratch(5536, P)
        expert_i = scratch(5664, P).bitcast(I32)
        digit = scratch(5792, 2 * P).bitcast(I32)
        match = scratch(10240, PH * TOPK * NCAND).rearrange("p (h k c) -> p h k c", h=PH, k=TOPK)

        h = sb("h", [P, NT, D])
        tmp = sb("tmp", [P, 6144])
        t1, t2 = tmp[:, 0:3072], tmp[:, 3072:6144]
        raw = tmp[:, 0:4096].rearrange("p (s n) -> p s n", s=4)
        hot_i = tmp[:, 4096:5120].rearrange("p (s q n) -> p s q n", s=2, q=4)
        hot_j = tmp[:, 5120:6144].rearrange("p (s q n) -> p s q n", s=2, q=4)
        part_hi = sb("part_hi", [P, 2, D], F32R)
        part_lo = sb("part_lo", [P, 2, D], F32R)
        x_hi = sb("x_hi", [P, KD, SEQ], F32R)
        x_lo = sb("x_lo", [P, KD, SEQ], F32R)
        a_hi = sb("a_hi", [P, 2, SEQ], F32R)
        a_lo = sb("a_lo", [P, 2, SEQ], F32R)
        ident = sb("ident", [P, P])
        taps = sb("taps", [P, SEQ])
        untapped = sb("untapped", [P, SEQ])
        tri_neg = sb("tri_neg", [P, P])
        ones_neg = sb("ones_neg", [P, P])
        iota_key = sb("iota_key", [P, P])
        iota_cand = sb("iota_cand", [P, NCAND])
        gain = sb("gain", [P, 42])
        hgain = sb("hgain", [P, 2, HD])
        posi = sb("posi", [P, NT], I32)
        posf = sb("posf", [P, NT])
        freq = sb("freq", [P, HALF])
        cossin = sb("cossin", [P, 2, NT, HALF])
        stat = sb("stat", [P, 5, 32])
        route_t = sb("route_t", [P, 3, SEQ])
        ps = ctx.enter_context(nc.psum_tensor("ps", [P, 8, 512], F32))

        def bank(b, n=1):
            return ps[:, b:b + n, :].rearrange("p b n -> p (b n)")

        loaded_x, loaded_mem, loaded_c = sem("loaded_x"), sem("loaded_mem"), sem("loaded_c")
        w_loaded = [sem(f"w_loaded{s}") for s in range(WSLOTS)]
        w_used = sem("w_used")
        ident_ready, masks_ready = sem("ident_ready"), sem("masks_ready")
        pool_step = sem("pool_step")
        sumsq, mean_ready, root_ready = sem("sumsq"), sem("mean_ready"), sem("root_ready")
        rows_normed, xt_psum, xt_ready = sem("rows_normed"), sem("xt_psum"), (sem("xt_lower"), sem("xt_upper"))
        a_mixed, b_taken, h_ready = sem("a_mixed"), sem("b_taken"), sem("h_ready")
        taken = [sem(f"taken{u}") for u in range(PEER0 + PEER_UNITS)]
        qk_normed, at_psum, at_ready = sem("qk_normed"), sem("at_psum"), sem("at_ready")
        a_scores, a_max, a_exp, a_weighted, a_turned, a_prob_t, a_out = (
            sem("a_scores"), sem("a_max"), sem("a_exp"), sem("a_weighted"), sem("a_turned"), sem("a_prob_t"), sem("a_out"))
        b_scores, b_abs, b_log, b_soft, b_soft_masked, b_summed, b_stick, b_stick_masked, b_out = (
            sem("b_scores"), sem("b_abs"), sem("b_log"), sem("b_soft"), sem("b_soft_masked"), sem("b_summed"),
            sem("b_stick"), sem("b_stick_masked"), sem("b_out"))
        mixed_ready, b_evens = sem("mixed_ready"), sem("b_evens")
        m_normed, m_psum, m_ready = sem("m_normed"), sem("m_psum"), sem("m_ready")
        m_scores, m_max, m_exp, m_weighted, m_turned, m_prob_t, m_out, m_out_ready = (
            sem("m_scores"), sem("m_max"), sem("m_exp"), sem("m_weighted"), sem("m_turned"), sem("m_prob_t"),
            sem("m_out"), sem("m_out_ready"))
        angles, sines = sem("angles"), sem("sines")
        x_hi_ready, x_lo_ready = sem("x_hi_ready"), sem("x_lo_ready")
        key_scores, key_scores_taken = sem("key_scores"), sem("key_scores_taken")
        best_centred, gates_exp = sem("best_centred"), sem("gates_exp")
        routed, route_psum, route_ready = sem("routed"), sem("route_psum"), sem("route_ready")
        u_loaded = [sem(f"u_loaded{s}") for s in range(4)]
        u_hi, u_lo, h_done, gelu_done = sem("u_hi"), sem("u_lo"), sem("h_done"), sem("gelu_done")
        hot_ready, g_done, g_applied = sem("hot_ready"), sem("g_done"), sem("g_applied")
        v_loaded = [sem(f"v_loaded{s}") for s in range(4)]
        v_hi, v_lo, a_hi_s, a_lo_s, y_done = sem("v_hi"), sem("v_lo"), sem("act_hi"), sem("act_lo"), sem("y_done")
        out_ready, stored = sem("out_ready"), sem("stored")
        dve_step, act_step = sem("dve_step"), sem("act_step")

        block = ctx.enter_context(nc.Block())

        G_MIX, G_TOK, G_MEM, G_FFN, G_OUT, G_QM, G_KM = 0, 8, 16, 24, 32, 40, 41
        NORMS = 4
        XT_BANK = (0, 4, 4, 4)

        @block.sync
        def _(sp):
            sp.dma_start(h[:], x.rearrange("(t p) n -> p t n", p=P)).then_inc(loaded_x, 16)
            sp.dma_start(t2[:, 0:2048].rearrange("p (t n) -> p t n", t=NT),
                         mem.rearrange("(t p) n -> p t n", p=P)).then_inc(loaded_mem, 16)
            sp.dma_start(gain[:], cols).then_inc(loaded_c, 16)
            sp.dma_start(hgain[:], head_gains.partition_broadcast(P)).then_inc(loaded_c, 16)
            sp.dma_start(posi[:], pos).then_inc(loaded_c, 16)
            for n in range(KEYS_HALF + 1):
                if n >= WSLOTS:
                    sp.wait_ge(w_used, n - WSLOTS + 1)
                sp.dma_start(ring[n % WSLOTS], weights[n]).then_inc(w_loaded[n % WSLOTS], 16)

            sp.wait_ge(xt_psum, 4 * NORMS)
            for s in range(4):
                sp.dma_start(raw[:, s, :], u_t[s]).then_inc(u_loaded[s], 16)
            with sp.Fori(1, NKEY // 4) as g:
                for s in range(4):
                    sp.wait_ge(u_lo, g * 4 + (s - 3))
                    sp.dma_start(raw[:, s, :], u_t[g * 4 + s]).then_inc(u_loaded[s], 16)
            sp.wait_ge(u_lo, NKEY)
            for s in range(4):
                sp.dma_start(raw[:, s, :], v_t[s]).then_inc(v_loaded[s], 16)
            with sp.Fori(1, NKEY // 4) as g:
                for s in range(4):
                    sp.wait_ge(v_lo, g * 4 + (s - 3))
                    sp.dma_start(raw[:, s, :], v_t[g * 4 + s]).then_inc(v_loaded[s], 16)
            sp.wait_ge(out_ready, 1)
            sp.dma_start(out.rearrange("(t p) n -> p t n", p=P), h[:]).then_inc(stored, 16)
            sp.wait_ge(stored, 16)

        @block.gpsimd
        def _(pool):
            step = Signal(pool_step)

            def chain(ins):
                pool.wait_ge(pool_step, step.on(ins))

            chain(pool.memset(ident[:], 0.0))
            pool.affine_select(ident[:], ident[:], [[-1, P]], ALU.not_equal, 1.0, base=0,
                               channel_multiplier=1).then_inc(ident_ready, 1)
            pool.iota(untapped[:].bitcast(I32), [[-1, SEQ]], base=P, channel_multiplier=1).then_inc(masks_ready, 1)
            chain(pool.memset(tri_neg[:], -1.0))
            pool.affine_select(tri_neg[:], tri_neg[:], [[-1, P]], ALU.is_ge, 0.0, base=0,
                               channel_multiplier=1).then_inc(masks_ready, 1)
            pool.memset(ones_neg[:], -1.0).then_inc(masks_ready, 1)
            pool.iota(iota_key[:], [[1, P]], base=0, channel_multiplier=0,
                      allow_small_or_imprecise_dtypes=True).then_inc(masks_ready, 1)
            pool.iota(iota_cand[:], [[1, NCAND]], base=0, channel_multiplier=0,
                      allow_small_or_imprecise_dtypes=True).then_inc(masks_ready, 1)
            for g in range(2):
                soft = t2[:, 1536:3072]
                pool.wait_ge(b_soft, g + 1)
                for at, n in ((0, SEQ), (1024, P)):
                    part = soft[:, at:at + 4 * n].rearrange("p (h t) -> p h t", h=4)[:, :, 0:P]
                    pool.affine_select(part, part, [[0, 4], [1, P]], ALU.is_gt, 0.0, base=0,
                                       channel_multiplier=-1).then_inc(b_soft_masked, 1)
                pool.wait_ge(b_stick, 2 * (g + 1))
                for at in (0, SEQ):
                    part = sticks[:, 4 * g:4 * g + 4, at:at + P]
                    pool.affine_select(part, part, [[0, 4], [1, P]], ALU.is_gt, 0.0, base=0,
                                       channel_multiplier=-1).then_inc(b_stick_masked, 1)

        def b_head(g, j):
            return 4 * g + (0, 2, 1, 3)[j]

        @block.tensor
        def _(pe):
            def turn(n):
                src = (t1, t2, t1, t1)[n][:, 0:2048].rearrange("p (t n) -> p t n", t=NT)
                for t in range(NT):
                    pe.wait_ge(rows_normed, NT * n + t + 1)
                    for k in range(KD):
                        ins = pe.transpose(ps[:, XT_BANK[n] + k // 2, (k % 2) * SEQ + t * P:][:, 0:P],
                                           src[:, t, k * P:(k + 1) * P], ident[:])
                        if t == NT - 1 and k % 2:
                            ins.then_inc(xt_psum, 1)

            def turned_taken(n):
                pe.wait_ge(xt_ready[0], 4 * (n + 1))
                pe.wait_ge(xt_ready[1], 4 * (n + 1))

            def arrived(n):
                pe.wait_ge(w_loaded[n % WSLOTS], 16 * (n // WSLOTS + 1))

            def project_rows(u, b, src):
                for a in range(2):
                    arrived(2 * u + a)
                    w = ring[(2 * u + a) % WSLOTS].rearrange("p (k n) -> p k n", k=4)
                    for t in range(NT):
                        for k in range(4):
                            ins = pe.matmul(bank(b + t), src[:, 4 * a + k, t * P:(t + 1) * P], w[:, k, :],
                                            start=(a == 0 and k == 0), stop=(a == 1 and k == 3))
                    ins.then_inc(w_used, 1)

            def project_cols(u, b, src):
                arrived(2 * u)
                arrived(2 * u + 1)
                for c in range(4):
                    for k in range(KD):
                        w = ring[(2 * u + k // 4) % WSLOTS].rearrange("p (k n) -> p k n", k=4)
                        ins = pe.matmul(ps[:, b + c // 2, (c % 2) * SEQ:][:, 0:SEQ],
                                        w[:, k % 4, c * P:(c + 1) * P], src[:, k, :],
                                        start=(k == 0), stop=(k == KD - 1))
                        if c == 3 and k % 4 == 3:
                            ins.then_inc(w_used, 1)

            pe.wait_ge(ident_ready, 1)
            turn(0)
            turn(1)
            turned_taken(0)
            project_rows(Q_A, 0, xt)
            project_rows(K_A, 2, xt)
            turned_taken(1)
            project_cols(Q_B, 4, xt)
            project_cols(K_B, 6, xt)
            pe.wait_ge(taken[Q_A], 1)
            project_rows(V_B, 0, xt)
            pe.wait_ge(taken[K_A], 1)
            project_rows(V_A, 2, xt)

            pe.wait_ge(taken[Q_B], 1)
            pe.wait_ge(taken[K_B], 1)
            pe.wait_ge(qk_normed, 1)
            for w in range(2):
                for c in range(4):
                    for t in range(NT):
                        ins = pe.transpose(ps[:, 4 + 2 * w + c // 2, (c % 2) * SEQ + t * P:][:, 0:P],
                                           qk_a[:, t, w, c * P:(c + 1) * P], ident[:])
                ins.then_inc(at_psum, 1)
            pe.wait_ge(taken[V_B], 1)
            pe.wait_ge(taken[V_A], 1)
            pe.wait_ge(at_ready, 2)
            for par in range(2):
                rows = slice(HD * par, HD * par + HD)
                for c in range(4):
                    pe.matmul(ps[:, par, c * P:(c + 1) * P], q_at[rows, c, 0:P], k_at[rows, c, 0:P],
                              start=True, stop=True)
                for c in range(4):
                    ins = pe.matmul(ps[:, 2 + 2 * par + c // 2, (c % 2) * SEQ:][:, 0:SEQ],
                                    q_at[rows, c, P:SEQ], k_at[rows, c, :], start=True, stop=True)
            ins.then_inc(a_scores, 1)
            project_rows(K_MEM, 6, memt)
            pe.wait_ge(taken[K_MEM], 1)
            project_rows(V_MEM, 6, memt)

            pe.wait_ge(a_weighted, 1)
            for n in range(24):
                ins = pe.transpose(ps[:, n // 4, (n % 4) * P:][:, 0:P], t2[:, n * P:(n + 1) * P], ident[:])
            ins.then_inc(a_turned, 1)
            pe.wait_ge(taken[V_MEM], 1)
            pe.wait_ge(a_prob_t, 2)
            for t in range(NT):
                for hh in range(NH):
                    slot = (hh % 2) * 4 + hh // 2
                    for sblk in range(t + 1):
                        at = slot * P if t == 0 else 1024 + slot * SEQ + sblk * P
                        ins = pe.matmul(ps[:, 6 + t, hh * HD:(hh + 1) * HD], t1[:, at:at + P],
                                        v_a[:, sblk, hh * HD:(hh + 1) * HD], start=(sblk == 0), stop=(sblk == t))
            ins.then_inc(a_out, 1)

            pe.wait_ge(masks_ready, 5)
            for g in range(2):
                for j in range(4):
                    hh = b_head(g, j)
                    rows = slice(HD * (hh % 2), HD * (hh % 2) + HD)
                    if j == 2:
                        pe.wait_ge(b_evens, g + 1)
                    pe.matmul(ps[:, 3 * g + j // 2, (j % 2) * SEQ:][:, 0:SEQ], k_bt[rows, hh // 2, 0:P],
                              q_bt[rows, hh // 2, :], start=(j % 2 == 0), stop=True, skip_group_check=True)
                    ins = pe.matmul(ps[:, 3 * g + 2, j * P:(j + 1) * P], k_bt[rows, hh // 2, P:SEQ],
                                    q_bt[rows, hh // 2, P:SEQ], start=(j == 0), stop=True, skip_group_check=True)
                    if j == 1:
                        ins.then_inc(b_evens, 1)
                ins.then_inc(b_scores, 1)
            for g in range(2):
                soft = t2[:, 1536:3072]
                pe.wait_ge(b_soft_masked, 2 * (g + 1))
                for j in range(4):
                    s0 = soft[:, j * SEQ:(j + 1) * SEQ]
                    s1 = soft[:, 1024 + j * P:1024 + (j + 1) * P]
                    z0 = ps[:, 3 * g + j // 2, (j % 2) * SEQ:][:, 0:SEQ]
                    pe.matmul(z0, tri_neg[:], s0, start=False, stop=False, skip_group_check=True)
                    pe.matmul(z0[:, P:SEQ], ones_neg[:], s1, start=False, stop=True, skip_group_check=True)
                    ins = pe.matmul(ps[:, 3 * g + 2, j * P:(j + 1) * P], tri_neg[:], s1, start=False, stop=True,
                                    skip_group_check=True)
                ins.then_inc(b_summed, 1)
            pe.wait_ge(b_stick_masked, 4)
            pe.wait_ge(a_mixed, 1)
            for t in range(NT):
                for hh in range(NH):
                    for sblk in range(t + 1):
                        g, j = hh // 4, (0, 2, 1, 3)[hh % 4]
                        st = sticks[:, 4 * g + j, :]
                        at = t * P if sblk == 0 else SEQ
                        ins = pe.matmul(ps[:, 6 + t, hh * HD:(hh + 1) * HD], st[:, at:at + P],
                                        v_b[:, sblk, hh * HD:(hh + 1) * HD], start=(sblk == 0), stop=(sblk == t))
            ins.then_inc(b_out, 1)

            for t in range(NT):
                pe.wait_ge(mixed_ready, t + 1)
                for k in range(KD):
                    ins = pe.transpose(ps[:, k // 2, (k % 2) * SEQ + t * P:][:, 0:P],
                                       mixed[:, t, k * P:(k + 1) * P], ident[:])
            ins.then_inc(at_psum, 1)
            pe.wait_ge(at_ready, 4)
            project_rows(OUT0, 4, xt)
            project_rows(OUT1, 6, xt)

            pe.wait_ge(m_normed, 1)
            for c in range(MH):
                for t in range(NT):
                    ins = pe.transpose(ps[:, c // 2, (c % 2) * SEQ + t * P:][:, 0:P],
                                       k_mem[:, t, c * P:(c + 1) * P], ident[:])
            ins.then_inc(m_psum, 1)
            pe.wait_ge(h_ready, 2)
            turn(2)
            turned_taken(2)
            project_rows(Q_MEM, 2, xt)
            pe.wait_ge(m_ready, 1)
            pe.wait_ge(m_normed, 2)
            for c in range(MH):
                for t in range(NT):
                    ins = pe.transpose(ps[:, c // 2, (c % 2) * SEQ + t * P:][:, 0:P],
                                       q_mem[:, t, c * P:(c + 1) * P], ident[:])
            ins.then_inc(m_psum, 1)
            pe.wait_ge(m_ready, 2)
            for t in range(NT):
                for c in range(MH):
                    ins = pe.matmul(ps[:, 4 + 2 * t + c // 2, (c % 2) * SEQ:][:, 0:SEQ],
                                    q_at[:, c, t * P:(t + 1) * P], k_memt[:, c, :], start=True, stop=True)
            ins.then_inc(m_scores, 1)
            pe.wait_ge(m_weighted, 1)
            for t in range(NT):
                for c in range(MH):
                    for m in range(2):
                        ins = pe.transpose(ps[:, c, m * SEQ + t * P:][:, 0:P],
                                           t2[:, (t * MH + c) * SEQ + m * P:][:, 0:P], ident[:])
            ins.then_inc(m_turned, 1)
            pe.wait_ge(m_prob_t, 2)
            for c in range(MH):
                for m in range(2):
                    ins = pe.matmul(ps[:, 4 + c // 2, (c % 2) * SEQ:][:, 0:SEQ], v_mem[:, m, c * P:(c + 1) * P],
                                    t1[:, (c * 2 + m) * SEQ:][:, 0:SEQ], start=(m == 0), stop=(m == 1))
            ins.then_inc(m_out, 1)
            pe.wait_ge(m_out_ready, 1)
            for a in range(2):
                arrived(2 * O_MEM + a)
                w = ring[(2 * O_MEM + a) % WSLOTS].rearrange("p (k n) -> p k n", k=2)
                for t in range(NT):
                    for n in range(2):
                        for k in range(2):
                            ins = pe.matmul(bank(2 * t + n), k_at[:, 2 * a + k, t * P:(t + 1) * P],
                                            w[:, k, n * 512:(n + 1) * 512],
                                            start=(a == 0 and k == 0), stop=(a == 1 and k == 1))
                ins.then_inc(w_used, 1)

            turn(3)
            turned_taken(3)
            pe.wait_ge(h_ready, 3)
            for n in range(PEER_UNITS):
                project_cols(PEER0 + n, 2 * n, xt)
            arrived(KEYS_HALF)
            keys = ring[KEYS_HALF % WSLOTS].rearrange("p (b n) -> p b n", b=NBLK)
            for n in range(PEER_UNITS):
                pe.wait_ge(taken[PEER0 + n], 1)
            for t in range(NT):
                for b in range(NBLK):
                    ins = pe.matmul(ps[:, 4 * t + b // 4, (b % 4) * P:][:, 0:P], q_peert[:, b, t * P:(t + 1) * P],
                                    keys[:, b, :], start=True, stop=True)
                ins.then_inc(key_scores, 1)
            pe.wait_ge(key_scores_taken, NT)
            pe.wait_ge(routed, NT)
            for w in range(3):
                for t in range(NT):
                    src = chosen[:, t * 3 + w, :]
                    ins = pe.transpose(ps[:, w // 2, (w % 2) * SEQ + t * P:][:, 0:P], src, ident[:])
            ins.then_inc(route_psum, 1)
            pe.wait_ge(route_ready, 1)

            def hidden(g, s, first):
                i = g * 4 + s
                pe.wait_ge(u_lo, i + 1)
                if not first:
                    pe.wait_ge(gelu_done, i - 3)
                part = s % 2
                for k in range(KD):
                    for n, (w, r) in enumerate(((part_hi, x_hi), (part_hi, x_lo), (part_lo, x_hi))):
                        ins = pe.matmul(ps[:, s, 0:SEQ], w[:, part, k * P:(k + 1) * P], r[:, k, :],
                                        start=(k == 0 and n == 0), stop=(k == KD - 1 and n == 2))
                ins.then_inc(h_done, 1)

            pe.wait_ge(x_lo_ready, 1)
            for s in range(4):
                hidden(0, s, True)
            with pe.Fori(1, NKEY // 4) as g:
                for s in range(4):
                    hidden(g, s, False)

            def gate_matrix(g, s, first):
                n = g * 2 + s
                pe.wait_ge(hot_ready, n + 1)
                if not first:
                    pe.wait_ge(g_applied, n - 1)
                for q in range(4):
                    ins = pe.matmul(ps[:, 4 + s, q * P:(q + 1) * P], hot_j[:, s, q, :], hot_i[:, s, q, :],
                                    start=True, stop=True)
                ins.then_inc(g_done, 1)

            for s in range(2):
                gate_matrix(0, s, True)
            with pe.Fori(1, SEQ // 8) as g:
                for s in range(2):
                    gate_matrix(g, s, False)

            def mix(g, s, first):
                i = g * 4 + s
                pe.wait_ge(v_lo, i + 1)
                pe.wait_ge(a_lo_s, i + 1)
                b = s % 2
                for t in range(NT):
                    for n, (w, r) in enumerate(((a_hi, part_hi), (a_hi, part_lo), (a_lo, part_hi))):
                        for c in range(2):
                            ins = pe.matmul(bank(2 * t + c), w[:, b, t * P:(t + 1) * P],
                                            r[:, b, c * 512:(c + 1) * 512],
                                            start=(first and s == 0 and n == 0), stop=False,
                                            skip_group_check=True)
                ins.then_inc(y_done, 1)

            pe.wait_ge(gelu_done, NKEY)
            for s in range(4):
                mix(0, s, True)
            with pe.Fori(1, NKEY // 4) as g:
                for s in range(4):
                    mix(g, s, False)

        @block.scalar
        def _(act):
            step = Signal(act_step)

            def chain(ins):
                act.wait_ge(act_step, step.on(ins))

            def sums_of_squares(n):
                src = h if n != 1 else t2[:, 0:2048].rearrange("p (t n) -> p t n", t=NT)
                junk = (scratch(15360, 2048) if n < 2 else t1[:, 0:2048]).rearrange("p (t n) -> p t n", t=NT)
                for t in range(NT):
                    act.activation(junk[:, t, :], src[:, t, :], ACT.Square,
                                   accum_out=stat[:, 0, 2 * n + t:2 * n + t + 1]).then_inc(sumsq, 1)

            def root(n, cols):
                act.wait_ge(mean_ready, n + 1)
                act.activation(stat[:, 2, cols], stat[:, 1, cols], ACT.Sqrt).then_inc(root_ready, 1)

            def take_turned(n):
                base = (G_MIX, G_TOK, G_MEM, G_FFN)[n]
                dst = memt if n == 1 else xt
                for k in range(4, 8):
                    if k % 2 == 0:
                        act.wait_ge(xt_psum, 4 * n + k // 2 + 1)
                    act.activation(dst[:, k, :], ps[:, XT_BANK[n] + k // 2, (k % 2) * SEQ:][:, 0:SEQ], ACT.Copy,
                                   scale=gain[:, base + k:base + k + 1]).then_inc(xt_ready[1], 1)

            act.wait_ge(loaded_x, 16)
            sums_of_squares(0)
            act.wait_ge(loaded_mem, 16)
            act.wait_ge(sumsq, 2)
            sums_of_squares(1)
            root(0, slice(0, 2))
            root(1, slice(2, 4))
            act.wait_ge(loaded_c, 48)
            take_turned(0)
            take_turned(1)
            for w in range(2):
                act.wait_ge(w_used, 2 * (w + 1))
                act.activation(qk_a[:, :, w, :], ps[:, 2 * w:2 * w + 2, :], ACT.Copy).then_inc(taken[(Q_A, K_A)[w]], 1)
            root(2, slice(0, 32))
            act.wait_ge(angles, 1)
            act.activation(cossin[:].rearrange("p w t f -> p (w t f)"),
                           cossin[:].rearrange("p w t f -> p (w t f)"), ACT.Sin).then_inc(sines, 1)
            act.wait_ge(w_used, 6)
            act.activation(q_bt.rearrange("p b t -> p (b t)"), bank(4, 2), ACT.Copy,
                           scale=HD ** -0.5).then_inc(taken[Q_B], 1)
            act.wait_ge(w_used, 10)
            act.activation(v_b.rearrange("p t n -> p (t n)"), bank(0, 2), ACT.Copy).then_inc(taken[V_B], 1)
            act.wait_ge(at_psum, 2)
            act.activation(k_at.rearrange("p b t -> p (b t)"), bank(6, 2), ACT.Copy).then_inc(at_ready, 1)
            act.wait_ge(w_used, 14)
            act.activation(k_mem.rearrange("p t n -> p (t n)"), bank(6, 2), ACT.Copy).then_inc(taken[K_MEM], 1)
            act.wait_ge(a_max, 1)
            for n in range(16):
                part = t2[:, n * P:(n + 1) * P] if n < 8 else t2[:, 1024 + (n - 8) * SEQ:][:, 0:SEQ]
                act.activation(part, part, ACT.Exp, bias=stat[:, 3, n:n + 1], scale=HD ** -0.5).then_inc(a_exp, 1)
            act.wait_ge(w_used, 16)
            act.activation(v_mem.rearrange("p t n -> p (t n)"), bank(6, 2), ACT.Copy).then_inc(taken[V_MEM], 1)
            act.wait_ge(a_turned, 1)
            act.activation(t1[:, 0:1536], bank(0, 3), ACT.Copy).then_inc(a_prob_t, 1)
            for g in range(2):
                act.wait_ge(b_scores, g + 1)
                act.wait_ge(a_turned, 1)
                if g:
                    act.wait_ge(b_soft, g)
                e = t2[:, 0:1536]
                chain(act.activation(e, bank(3 * g, 3), ACT.Abs))
                chain(act.activation(e, e, ACT.Exp, scale=-1.0))
                act.activation(e, e, ACT.Ln, bias=1.0).then_inc(b_log, 1)
            for g in range(2):
                act.wait_ge(b_summed, g + 1)
                act.activation(sticks[:, 4 * g:4 * g + 4, 0:SEQ],
                               bank(3 * g, 2).rearrange("p (h t) -> p h t", h=4), ACT.Exp).then_inc(b_stick, 1)
                act.activation(sticks[:, 4 * g:4 * g + 4, SEQ:SEQ + P],
                               bank(3 * g + 2).rearrange("p (h t) -> p h t", h=4), ACT.Exp).then_inc(b_stick, 1)
            act.wait_ge(b_out, 1)
            act.activation(mixed[:, :, 512:1024], ps[:, 6:8, :], ACT.Copy).then_inc(b_taken, 1)
            act.wait_ge(a_mixed, 1)
            act.wait_ge(b_taken, 1)
            for t in range(NT):
                for w in range(2):
                    act.activation(t1[:, (2 * t + w) * 512:(2 * t + w + 1) * 512],
                                   mixed[:, t, w * 512:(w + 1) * 512], ACT.Square,
                                   accum_out=stat[:, 0, 2 * t + w:2 * t + w + 1]).then_inc(sumsq, 1)
            root(3, slice(0, 4))
            act.wait_ge(at_psum, 3)
            for k in range(4, 8):
                ins = act.activation(xt[:, k, :], ps[:, k // 2, (k % 2) * SEQ:][:, 0:SEQ], ACT.Copy,
                                     scale=gain[:, G_OUT + k:G_OUT + k + 1])
            ins.then_inc(at_ready, 1)
            root(4, slice(8, 16))
            act.wait_ge(h_ready, 2)
            act.wait_ge(sumsq, 8)
            sums_of_squares(2)
            root(5, slice(4, 6))
            take_turned(2)
            act.wait_ge(w_used, 22)
            act.activation(q_mem.rearrange("p t n -> p (t n)"), bank(2, 2), ACT.Copy).then_inc(taken[Q_MEM], 1)
            root(6, slice(16, 24))
            act.wait_ge(m_max, 1)
            for n in range(8):
                act.activation(t2[:, n * SEQ:(n + 1) * SEQ], bank(4, 4)[:, n * SEQ:(n + 1) * SEQ], ACT.Exp,
                               bias=stat[:, 3, n:n + 1], scale=MHD ** -0.5,
                               accum_out=stat[:, 4, n:n + 1]).then_inc(m_exp, 1)
            act.wait_ge(m_turned, 1)
            act.activation(t1[:, 0:1024], bank(0, 2), ACT.Copy).then_inc(m_prob_t, 1)
            act.wait_ge(m_out, 1)
            act.activation(k_at.rearrange("p b t -> p (b t)"), bank(4, 2), ACT.Copy).then_inc(m_out_ready, 1)
            act.wait_ge(h_ready, 3)
            sums_of_squares(3)
            root(7, slice(6, 8))
            take_turned(3)
            act.wait_ge(xt_ready[0], 16)
            act.wait_ge(xt_ready[1], 16)
            act.activation(x_hi[:], xt, ACT.Copy).then_inc(x_hi_ready, 1)
            for n in range(PEER_UNITS):
                act.wait_ge(w_used, 2 * (PEER0 + n + 1))
                act.activation(q_peert[:, 4 * n:4 * n + 4, :].rearrange("p b t -> p (b t)"), bank(2 * n, 2),
                               ACT.Copy).then_inc(taken[PEER0 + n], 1)
            for t in range(NT):
                act.wait_ge(key_scores, t + 1)
                act.activation(scores[:, t].rearrange("p b n -> p (b n)"), bank(4 * t, 4),
                               ACT.Copy).then_inc(key_scores_taken, 1)
            for t in range(NT):
                act.wait_ge(best_centred, t + 1)
                part = chosen[:, t * 3 + 2, :]
                act.activation(part, part, ACT.Exp).then_inc(gates_exp, 1)

            def high_u(g, s, first):
                i = g * 4 + s
                act.wait_ge(u_loaded[s], 16 * (g + 1))
                if not (first and s < 2):
                    act.wait_ge(h_done, i - 1)
                act.activation(part_hi[:, s % 2, :], raw[:, s, :], ACT.Copy).then_inc(u_hi, 1)

            def gelu(i, s):
                act.wait_ge(h_done, i + 1)
                act.activation(big[:, bass.ds(i * SEQ, SEQ)], ps[:, s, 0:SEQ], ACT.Gelu).then_inc(gelu_done, 1)

            act.wait_ge(route_ready, 1)
            for s in range(4):
                high_u(0, s, True)
                if s:
                    gelu(s - 1, s - 1)
            with act.Fori(1, NKEY // 4) as g:
                for s in range(4):
                    high_u(g, s, False)
                    gelu(g * 4 + (s - 1), (s - 1) % 4)
            gelu(NKEY - 1, 3)

            def high_v(g, s, first):
                i = g * 4 + s
                act.wait_ge(v_loaded[s], 16 * (g + 1))
                if not (first and s < 2):
                    act.wait_ge(y_done, i - 1)
                act.activation(part_hi[:, s % 2, :], raw[:, s, :], ACT.Copy).then_inc(v_hi, 1)
                act.activation(a_hi[:, s % 2, :], big[:, bass.ds(i * SEQ, SEQ)], ACT.Copy).then_inc(a_hi_s, 1)

            act.wait_ge(g_applied, SEQ // 4)
            for s in range(4):
                high_v(0, s, True)
            with act.Fori(1, NKEY // 4) as g:
                for s in range(4):
                    high_v(g, s, False)

        @block.vector
        def _(dve):
            step = Signal(dve_step)

            def chain(ins):
                dve.wait_ge(dve_step, step.on(ins))

            def mean(n, cols, waits, width):
                if waits:
                    dve.wait_ge(sumsq, waits)
                dve.tensor_scalar(stat[:, 1, cols], stat[:, 0, cols], 1.0 / width, EPS, ALU.mult,
                                  ALU.add).then_inc(mean_ready, 1)

            def inverse(n, cols):
                dve.wait_ge(root_ready, n + 1)
                chain(dve.reciprocal(stat[:, 2, cols], stat[:, 2, cols]))

            def norm_rows(n, mean_no, col):
                src = h if n != 1 else t2[:, 0:2048].rearrange("p (t n) -> p t n", t=NT)
                dst = (t1, t2, t1, t1)[n][:, 0:2048].rearrange("p (t n) -> p t n", t=NT)
                for t in range(NT):
                    dve.tensor_scalar(dst[:, t, :], src[:, t, :], stat[:, 2, col + t:col + t + 1], None,
                                      ALU.mult).then_inc(rows_normed, 1)

            def take_turned(n):
                base = (G_MIX, G_TOK, G_MEM, G_FFN)[n]
                dst = memt if n == 1 else xt
                for k in range(4):
                    if k % 2 == 0:
                        dve.wait_ge(xt_psum, 4 * n + k // 2 + 1)
                    dve.tensor_scalar(dst[:, k, :], ps[:, XT_BANK[n] + k // 2, (k % 2) * SEQ:][:, 0:SEQ],
                                      gain[:, base + k:base + k + 1], None, ALU.mult).then_inc(xt_ready[0], 1)

            mean(0, slice(0, 2), 2, D)
            inverse(0, slice(0, 2))
            norm_rows(0, 0, 0)
            mean(1, slice(2, 4), 4, D)
            inverse(1, slice(2, 4))
            norm_rows(1, 1, 2)

            dve.wait_ge(masks_ready, 5)
            off_i = untapped[:].bitcast(I32)
            w = [t1[:, 2048 + n * SEQ:2048 + (n + 1) * SEQ] for n in range(4)]
            chain(dve.tensor_copy(w[0], off_i))
            chain(dve.tensor_scalar(taps[:], w[0], float(TAPS[0][0]), None, ALU.is_le))
            for window, dilation in zip(TAPS[0][1:], TAPS[1][1:]):
                assert window >= SEQ
                chain(dve.tensor_scalar(w[1].bitcast(I32), off_i, dilation - 1, None, ALU.bitwise_and))
                chain(dve.tensor_copy(w[2], w[1].bitcast(I32)))
                chain(dve.scalar_tensor_tensor(taps[:], w[2], 0.0, taps[:], ALU.is_equal, ALU.add))
            chain(dve.scalar_tensor_tensor(taps[:], w[0], 0.0, taps[:], ALU.is_ge, ALU.mult))
            chain(dve.tensor_scalar(untapped[:], taps[:], 0.0, MASKED, ALU.is_equal, ALU.mult))

            dve.wait_ge(loaded_c, 48)
            chain(dve.tensor_copy(posf[:], posi[:]))
            for f in range(HALF):
                ins = dve.memset(freq[:, f:f + 1], float(inv_freq[f]))
                step.on(ins)
            dve.wait_ge(dve_step, step.n)
            ang, turns = cossin[:, 0], cossin[:, 1]
            for t in range(NT):
                chain(dve.tensor_scalar(w[3][:, t * HALF:(t + 1) * HALF], freq[:], posf[:, t:t + 1], None, ALU.mult))
            a16, n16, m16 = w[3][:, 0:16], w[3][:, 16:32], w[3][:, 32:48]
            for c in range(2):
                chain(dve.tensor_scalar(n16, a16, float(1 / (2 * np.pi)), 0.25 * (1 - c), ALU.mult, ALU.add))
                chain(dve.tensor_scalar(n16, n16, MAGIC, None, ALU.add))
                chain(dve.tensor_scalar(n16, n16, MAGIC, None, ALU.subtract))
                chain(dve.scalar_tensor_tensor(m16, n16, -TWO_PI_PARTS[0], a16, ALU.mult, ALU.add))
                chain(dve.scalar_tensor_tensor(m16, n16, -TWO_PI_PARTS[1], m16, ALU.mult, ALU.add))
                chain(dve.scalar_tensor_tensor(m16, n16, -TWO_PI_PARTS[2], m16, ALU.mult, ALU.add))
                chain(dve.tensor_scalar(m16, m16, float(np.pi / 2) * (1 - c), PI_SAFE, ALU.add, ALU.min))
                ins = dve.tensor_scalar(cossin[:, c].rearrange("p t f -> p (t f)"), m16, -PI_SAFE, None, ALU.max)
                if c:
                    ins.then_inc(angles, 1)
                else:
                    chain(ins)

            take_turned(0)
            take_turned(1)

            dve.wait_ge(taken[Q_A], 1)
            dve.wait_ge(taken[K_A], 1)
            flat = qk_a.rearrange("p t w n -> p (t w n)")
            by_head = qk_a.rearrange("p t w (h d) -> p (t w h) d", d=HD)
            sq = t1[:, 0:2048]
            dve.wait_ge(xt_psum, 4)
            chain(dve.tensor_tensor(sq, flat, flat, ALU.mult))
            chain(dve.tensor_reduce(stat[:, 0, :], sq.rearrange("p (g d) -> p g d", d=HD), AX, ALU.add))
            mean(2, slice(0, 32), 0, HD)
            inverse(2, slice(0, 32))
            chain(dve.tensor_tensor(by_head, by_head, stat[:, 2, :].unsqueeze(2).broadcast_to([P, 32, HD]), ALU.mult))
            for t in range(NT):
                for w_ in range(2):
                    part = qk_a[:, t, w_, :].rearrange("p (h d) -> p h d", d=HD)
                    ins = dve.tensor_tensor(part, part, hgain[:, w_, :].unsqueeze(1).broadcast_to([P, NH, HD]),
                                            ALU.mult)
                    step.on(ins)
            dve.wait_ge(dve_step, step.n)
            dve.wait_ge(sines, 1)
            for t in range(NT):
                part = qk_a[:, t].rearrange("p w (h d) -> p (w h) d", d=HD)
                x1, x2 = part[:, :, 0:HALF], part[:, :, HALF:ROPE]
                cos = cossin[:, 0, t, :].unsqueeze(1).broadcast_to([P, 2 * NH, HALF])
                sin = cossin[:, 1, t, :].unsqueeze(1).broadcast_to([P, 2 * NH, HALF])
                r = [t1[:, n * 128:(n + 1) * 128].rearrange("p (g f) -> p g f", f=HALF) for n in range(4 * t, 4 * t + 4)]
                for o, a, b in ((r[0], x1, cos), (r[1], x2, sin), (r[2], x2, cos), (r[3], x1, sin)):
                    step.on(dve.tensor_tensor(o, a, b, ALU.mult))
                dve.wait_ge(dve_step, step.n)
                step.on(dve.tensor_tensor(x1, r[0], r[1], ALU.subtract))
                ins = dve.tensor_tensor(x2, r[2], r[3], ALU.add)
            ins.then_inc(qk_normed, 1)

            dve.wait_ge(w_used, 8)
            dve.tensor_copy(k_bt.rearrange("p b t -> p (b t)"), bank(6, 2)).then_inc(taken[K_B], 1)
            dve.wait_ge(w_used, 12)
            dve.tensor_copy(v_a.rearrange("p t n -> p (t n)"), bank(2, 2)).then_inc(taken[V_A], 1)
            dve.wait_ge(at_psum, 1)
            dve.tensor_copy(q_at.rearrange("p b t -> p (b t)"), bank(4, 2)).then_inc(at_ready, 1)

            dve.wait_ge(a_scores, 1)
            dve.wait_ge(xt_psum, 8)
            p0 = t2[:, 0:1024].rearrange("p (h s) -> p h s", h=NH)
            p1 = t2[:, 1024:3072].rearrange("p (h s) -> p h s", h=NH)
            chain(dve.tensor_tensor(p0, bank(0, 2).rearrange("p (h s) -> p h s", h=NH),
                                    untapped[:, P:SEQ].unsqueeze(1).broadcast_to([P, NH, P]), ALU.add))
            chain(dve.tensor_tensor(p1, bank(2, 4).rearrange("p (h s) -> p h s", h=NH),
                                    untapped[:].unsqueeze(1).broadcast_to([P, NH, SEQ]), ALU.add))
            step.on(dve.tensor_reduce(stat[:, 3, 0:8], p0, AX, ALU.max))
            chain(dve.tensor_reduce(stat[:, 3, 8:16], p1, AX, ALU.max))
            dve.tensor_scalar(stat[:, 3, 0:16], stat[:, 3, 0:16], -HD ** -0.5, None, ALU.mult).then_inc(a_max, 1)
            dve.wait_ge(a_exp, 16)
            step.on(dve.tensor_tensor(p0, p0, taps[:, P:SEQ].unsqueeze(1).broadcast_to([P, NH, P]), ALU.mult))
            dve.tensor_tensor(p1, p1, taps[:].unsqueeze(1).broadcast_to([P, NH, SEQ]), ALU.mult).then_inc(a_weighted, 1)
            dve.wait_ge(a_weighted, 1)
            step.on(dve.tensor_reduce(stat[:, 4, 0:8], p0, AX, ALU.add))
            chain(dve.tensor_reduce(stat[:, 4, 8:16], p1, AX, ALU.add))
            chain(dve.reciprocal(stat[:, 4, 0:16], stat[:, 4, 0:16]))
            dve.wait_ge(a_turned, 1)
            dve.tensor_copy(t1[:, 1536:3072], bank(3, 3)).then_inc(a_prob_t, 1)
            dve.wait_ge(a_out, 1)
            dve.wait_ge(w_used, 16)
            for t in range(NT):
                for par in range(2):
                    ins = dve.tensor_tensor(
                        mixed[:, t, 0:512].rearrange("p (a r d) -> p a r d", r=2, d=HD)[:, :, par, :],
                        bank(6 + t).rearrange("p (a r d) -> p a r d", r=2, d=HD)[:, :, par, :],
                        stat[:, 4, 8 * t + 4 * par:8 * t + 4 * par + 4].unsqueeze(2).broadcast_to([P, 4, HD]),
                        ALU.mult)
            ins.then_inc(a_mixed, 1)
            for g in range(2):
                dve.wait_ge(b_log, g + 1)
                if g:
                    dve.wait_ge(b_summed, g)
                dve.scalar_tensor_tensor(t2[:, 1536:3072], bank(3 * g, 3), 0.0, t2[:, 0:1536], ALU.max,
                                         ALU.add).then_inc(b_soft, 1)
            mean(3, slice(0, 4), 8, 512)
            inverse(3, slice(0, 4))
            for t in range(NT):
                for w_ in range(2):
                    part = mixed[:, t, w_ * 512:(w_ + 1) * 512]
                    ins = dve.tensor_scalar(part, part, stat[:, 2, 2 * t + w_:2 * t + w_ + 1], None, ALU.mult)
                ins.then_inc(mixed_ready, 1)
            dve.wait_ge(at_psum, 3)
            for k in range(4):
                ins = dve.tensor_scalar(xt[:, k, :], ps[:, k // 2, (k % 2) * SEQ:][:, 0:SEQ],
                                        gain[:, G_OUT + k:G_OUT + k + 1], None, ALU.mult)
            ins.then_inc(at_ready, 1)
            dve.wait_ge(taken[K_MEM], 1)
            by_head = k_mem.rearrange("p t (h d) -> p (t h) d", d=MHD)
            chain(dve.tensor_tensor(sq_mem, k_mem, k_mem, ALU.mult))
            chain(dve.tensor_reduce(stat[:, 0, 8:16], sq_mem.rearrange("p t (h d) -> p (t h) d", d=MHD), AX, ALU.add))
            mean(4, slice(8, 16), 0, MHD)
            inverse(4, slice(8, 16))
            dve.tensor_tensor(by_head, by_head, stat[:, 2, 8:16].unsqueeze(2).broadcast_to([P, 8, MHD]),
                              ALU.mult).then_inc(m_normed, 1)
            for n in range(2):
                dve.wait_ge(w_used, 2 * (OUT0 + n + 1))
                part = h[:, :, n * 512:(n + 1) * 512]
                dve.tensor_tensor(part, part, ps[:, 4 + 2 * n:6 + 2 * n, :], ALU.add).then_inc(h_ready, 1)
            dve.wait_ge(m_psum, 1)
            dve.tensor_scalar(k_memt.rearrange("p b t -> p (b t)"), bank(0, 2), gain[:, G_KM:G_KM + 1], None,
                              ALU.mult).then_inc(m_ready, 1)
            mean(5, slice(4, 6), 10, D)
            inverse(5, slice(4, 6))
            norm_rows(2, 5, 4)
            take_turned(2)
            dve.wait_ge(taken[Q_MEM], 1)
            by_head = q_mem.rearrange("p t (h d) -> p (t h) d", d=MHD)
            chain(dve.tensor_tensor(sq_mem, q_mem, q_mem, ALU.mult))
            chain(dve.tensor_reduce(stat[:, 0, 16:24], sq_mem.rearrange("p t (h d) -> p (t h) d", d=MHD), AX, ALU.add))
            mean(6, slice(16, 24), 0, MHD)
            inverse(6, slice(16, 24))
            dve.tensor_tensor(by_head, by_head, stat[:, 2, 16:24].unsqueeze(2).broadcast_to([P, 8, MHD]),
                              ALU.mult).then_inc(m_normed, 1)
            dve.wait_ge(m_psum, 2)
            dve.tensor_scalar(q_at.rearrange("p b t -> p (b t)"), bank(0, 2), gain[:, G_QM:G_QM + 1], None,
                              ALU.mult).then_inc(m_ready, 1)
            dve.wait_ge(m_scores, 1)
            chain(dve.tensor_reduce(stat[:, 3, 0:8], bank(4, 4).rearrange("p (g m) -> p g m", g=8), AX, ALU.max))
            dve.tensor_scalar(stat[:, 3, 0:8], stat[:, 3, 0:8], -MHD ** -0.5, None, ALU.mult).then_inc(m_max, 1)
            dve.wait_ge(m_exp, 8)
            chain(dve.reciprocal(stat[:, 4, 0:8], stat[:, 4, 0:8]))
            part = t2[:, 0:2048].rearrange("p (g m) -> p g m", g=8)
            dve.tensor_tensor(part, part, stat[:, 4, 0:8].unsqueeze(2).broadcast_to([P, 8, SEQ]),
                              ALU.mult).then_inc(m_weighted, 1)
            dve.wait_ge(m_turned, 1)
            dve.tensor_copy(t1[:, 1024:2048], bank(2, 2)).then_inc(m_prob_t, 1)
            dve.wait_ge(w_used, 24)
            dve.tensor_tensor(h[:].rearrange("p t n -> p (t n)"), h[:].rearrange("p t n -> p (t n)"), bank(0, 4),
                              ALU.add).then_inc(h_ready, 1)
            mean(7, slice(6, 8), 12, D)
            inverse(7, slice(6, 8))
            norm_rows(3, 7, 6)
            take_turned(3)
            dve.wait_ge(x_hi_ready, 1)
            dve.tensor_tensor(x_lo[:], xt, x_hi[:].bitcast(F32), ALU.subtract).then_inc(x_lo_ready, 1)

            for t in range(NT):
                dve.wait_ge(key_scores_taken, NT)
                def each_block(emit):
                    for b in range(NBLK):
                        step.on(emit(b))
                    dve.wait_ge(dve_step, step.n)

                def each_head(emit):
                    for n in range(PH):
                        step.on(emit(n))
                    dve.wait_ge(dve_step, step.n)

                val, at, row = top_val[:, t], top_pos[:, t], scores[:, t]
                each_block(lambda b: dve.max(val[:, b, 0:8], row[:, b, :]))
                each_block(lambda b: dve.max_index(at[:, b, 0:8], val[:, b, 0:8], row[:, b, :]))
                each_block(lambda b: dve.match_replace(row[:, b, :], val[:, b, 0:8], row[:, b, :], LOWEST))
                each_block(lambda b: dve.max(val[:, b, 8:16], row[:, b, :]))
                each_block(lambda b: dve.max_index(at[:, b, 8:16], val[:, b, 8:16], row[:, b, :]))
                chain(dve.tensor_copy(top_id[:, t], at))
                first = top_id[:, t].rearrange("p (h w) k -> p h w k", w=2)[:, :, 0, :]
                chain(dve.tensor_scalar(first, first, float(NKEY), None, ALU.mult))
                for dst, src in ((cand_val, top_val[:, t]), (cand_id, top_id[:, t])):
                    pair = src.rearrange("p (h w) k -> p h w k", w=2)
                    c = 0
                    for a, n in enumerate(CAND):
                        if n == 1:
                            break
                        step.on(dve.tensor_tensor(dst[:, :, c:c + n], pair[:, :, 0, a:a + 1].broadcast_to([P, PH, n]),
                                                  pair[:, :, 1, 0:n], ALU.add))
                        c += n
                    step.on(dve.tensor_tensor(dst[:, :, c:NCAND], pair[:, :, 0, a:TOPK],
                                              pair[:, :, 1, 0:1].broadcast_to([P, PH, TOPK - a]), ALU.add))
                dve.wait_ge(dve_step, step.n)
                each_head(lambda n: dve.max(best[:, n, 0:8], cand_val[:, n, :]))
                each_head(lambda n: dve.max_index(best_pos[:, n, 0:8], best[:, n, 0:8], cand_val[:, n, :]))
                each_head(lambda n: dve.match_replace(cand_val[:, n, :], best[:, n, 0:8], cand_val[:, n, :], LOWEST))
                each_head(lambda n: dve.max(best[:, n, 8:16], cand_val[:, n, :]))
                each_head(lambda n: dve.max_index(best_pos[:, n, 8:16], best[:, n, 8:16], cand_val[:, n, :]))
                gate = chosen[:, t * 3 + 2, :].rearrange("p (h k) -> p h k", h=PH)
                dve.tensor_tensor(gate, best, best[:, :, 0:1].broadcast_to([P, PH, TOPK]),
                                  ALU.subtract).then_inc(best_centred, 1)
                chain(dve.tensor_copy(best_at, best_pos))
                flat_match = match.rearrange("p h k c -> p (h k) c")
                chain(dve.tensor_tensor(flat_match, iota_cand[:].unsqueeze(1).broadcast_to([P, P, NCAND]),
                                        best_at.rearrange("p h k -> p (h k)").unsqueeze(2).broadcast_to([P, P, NCAND]),
                                        ALU.is_equal))
                chain(dve.tensor_tensor(match, match, cand_id.unsqueeze(2).broadcast_to([P, PH, TOPK, NCAND]), ALU.mult))
                chain(dve.tensor_reduce(expert, flat_match, AX, ALU.add))
                chain(dve.tensor_copy(expert_i, expert))
                step.on(dve.tensor_scalar(digit[:, 0:P], expert_i, 7, None, ALU.arith_shift_right))
                chain(dve.tensor_scalar(digit[:, P:2 * P], expert_i, NKEY - 1, None, ALU.bitwise_and))
                chain(dve.tensor_copy(chosen[:, t * 3:t * 3 + 2, :].rearrange("p n k -> p (n k)"), digit))
                dve.wait_ge(gates_exp, t + 1)
                chain(dve.tensor_reduce(stat[:, 0, 0:PH], gate, AX, ALU.add))
                chain(dve.reciprocal(stat[:, 0, 0:PH], stat[:, 0, 0:PH]))
                dve.tensor_tensor(gate, gate, stat[:, 0, 0:PH].unsqueeze(2).broadcast_to([P, PH, TOPK]),
                                  ALU.mult).then_inc(routed, 1)
            dve.wait_ge(route_psum, 1)
            dve.tensor_copy(route_t[:].rearrange("p n t -> p (n t)"), bank(0, 2)[:, 0:3 * SEQ]).then_inc(route_ready, 1)

            def low_u(i, s):
                dve.wait_ge(u_hi, i + 1)
                dve.tensor_tensor(part_lo[:, s % 2, :], raw[:, s, :], part_hi[:, s % 2, :].bitcast(F32),
                                  ALU.subtract).then_inc(u_lo, 1)

            with dve.Fori(0, NKEY // 4) as g:
                for s in range(4):
                    low_u(g * 4 + s, s)

            wide = big[:].rearrange("p (i t) -> p i t", t=SEQ)

            def one_hots(n, s, first):
                if not first:
                    dve.wait_ge(g_done, n - 1)
                for q in range(4):
                    t = n * 4 + q
                    dve.tensor_scalar(hot_i[:, s, q, :], iota_key[:], route_t[:, 0, bass.ds(t, 1)], None,
                                      ALU.is_equal)
                    ins = dve.tensor_scalar(hot_j[:, s, q, :], iota_key[:], route_t[:, 1, bass.ds(t, 1)],
                                            route_t[:, 2, bass.ds(t, 1)], ALU.is_equal, ALU.mult)
                ins.then_inc(hot_ready, 1)

            def apply(n, s):
                dve.wait_ge(g_done, n + 1)
                part = wide[:, :, bass.ds(n * 4, 4)]
                dve.tensor_tensor(part, part, bank(4 + s).rearrange("p (q i) -> p i q", q=4),
                                  ALU.mult).then_inc(g_applied, 1)

            dve.wait_ge(gelu_done, NKEY)
            one_hots(0, 0, True)
            one_hots(1, 1, True)
            apply(0, 0)
            with dve.Fori(1, SEQ // 8) as g:
                one_hots(g * 2, 0, False)
                apply(g * 2 - 1, 1)
                one_hots(g * 2 + 1, 1, False)
                apply(g * 2, 0)
            apply(SEQ // 4 - 1, 1)

            dve.wait_ge(g_applied, SEQ // 4)

            def low_v(i, s):
                dve.wait_ge(v_hi, i + 1)
                dve.tensor_tensor(part_lo[:, s % 2, :], raw[:, s, :], part_hi[:, s % 2, :].bitcast(F32),
                                  ALU.subtract).then_inc(v_lo, 1)
                dve.wait_ge(a_hi_s, i + 1)
                dve.tensor_tensor(a_lo[:, s % 2, :], big[:, bass.ds(i * SEQ, SEQ)],
                                  a_hi[:, s % 2, :].bitcast(F32), ALU.subtract).then_inc(a_lo_s, 1)

            with dve.Fori(0, NKEY // 4) as g:
                for s in range(4):
                    low_v(g * 4 + s, s)
            dve.wait_ge(y_done, NKEY)
            dve.tensor_tensor(h[:].rearrange("p t n -> p (t n)"), h[:].rearrange("p t n -> p (t n)"), bank(0, 4),
                              ALU.add).then_inc(out_ready, 1)


def kernel(x, mem, positions, norm_mix_g, w_in, qnorm_g_dil, knorm_g_dil, out_norm_g_dil, out_norm_g_sb, w_out,
           norm_mem_g, norm_memtok_g, w_q_mem, w_kv_mem, qnorm_g_mem, knorm_g_mem, w_o_mem, norm_ffn_g, w_q_peer,
           peer_sub_keys, peer_u, peer_v):
    import concourse.bacc as bacc
    from concourse.bass_utils import run_bass_kernel_spmd

    def blocks(w, n):
        k, c = w.shape[0] // P, w.shape[1] // n
        return np.ascontiguousarray(w.reshape(k, P, n, c).transpose(2, 1, 0, 3))

    def halves(units):
        n, p, k, c = units.shape
        return units.reshape(n, p, 2, k // 2, c).transpose(0, 2, 1, 3, 4).reshape(2 * n, p, k * c // 2)

    w_in, w_out, w_q_peer = np.asarray(w_in)[0], np.asarray(w_out)[0], np.asarray(w_q_peer)[0]
    w_kv = np.asarray(w_kv_mem)[0]
    mix = blocks(w_in, 6)
    keys = np.asarray(peer_sub_keys)[0].reshape(NBLK, NKEY, P).transpose(2, 0, 1).reshape(1, P, WHALF)
    weights = np.concatenate(
        [halves(mix[[0, 1, 3, 4, 5, 2]]), halves(blocks(w_kv, 2)), halves(blocks(w_out, 2)),
         halves(blocks(np.asarray(w_q_mem)[0], 1)), halves(blocks(np.asarray(w_o_mem)[0], 1)),
         halves(blocks(w_q_peer, PEER_UNITS)), keys], axis=0)
    cols = np.ascontiguousarray(np.concatenate(
        [np.asarray(a)[0].reshape(-1, P) for a in (norm_mix_g, norm_memtok_g, norm_mem_g, norm_ffn_g,
                                                    out_norm_g_dil, out_norm_g_sb, qnorm_g_mem, knorm_g_mem)], axis=0).T)
    head_gains = np.concatenate([np.asarray(qnorm_g_dil), np.asarray(knorm_g_dil)], axis=0)
    u_t = np.ascontiguousarray(np.asarray(peer_u)[0].reshape(NKEY, NKEY, KD, P).transpose(0, 3, 2, 1)).reshape(NKEY, P, D)
    v_t = np.asarray(peer_v)[0].reshape(NKEY, P, D)
    pos = np.ascontiguousarray(np.asarray(positions).reshape(NT, P).T)
    arrays = {"x": np.asarray(x)[0], "mem": np.asarray(mem)[0], "pos": pos, "weights": weights, "cols": cols,
              "head_gains": head_gains, "u_t": u_t, "v_t": v_t}
    nc = bacc.Bacc("TRN2", target_bir_lowering=False, num_devices=1)
    args = [nc.dram_tensor(n, a.shape, mybir.dt.from_np(a.dtype), kind="ExternalInput").ap() for n, a in arrays.items()]
    out = nc.dram_tensor("out", (SEQ, D), F32, kind="ExternalOutput").ap()
    hybrid_layer(nc, *args, out)
    r = run_bass_kernel_spmd(nc, [arrays], core_ids=[0])
    return r.results[0]["out"].reshape(1, SEQ, D)
```

```python
from contextlib import ExitStack

import numpy as np
import concourse.bass as bass
import concourse.mybir as mybir

F32 = mybir.dt.float32
F32R = mybir.dt.float32r
I32 = mybir.dt.int32
U32 = mybir.dt.uint32
ALU = mybir.AluOpType
ACT = mybir.ActivationFunctionType
AX = mybir.AxisListType.X

P = 128
D = 1024
SEQ = 256
NT = SEQ // P
KD = D // P
HD = 64
NH = 8
ROPE = HD // 4
HALF = ROPE // 2
MH, MHD = 4, 128
PH, TOPK = 8, 16
NKEY = 128
NBLK = 2 * PH
EPS = 1e-6
CAND = [TOPK // (a + 1) for a in range(TOPK)]
NCAND = sum(CAND)
TAPS = (128, 512, 2048), (1, 4, 16)
WSLOTS = 5
WHALF = 2048
HI_SLOTS = 4
(Q_B, K_B, Q_A, K_A, V_B, V_A, K_MEM, V_MEM, OUT0, OUT1, Q_MEM, O_MEM, PEER0) = range(13)
PEER_UNITS = 4
KEYS_HALF = 2 * (PEER0 + PEER_UNITS)
SPLIT = [n for n in range(KEYS_HALF) if n // 2 != O_MEM]
(X_ROWS, MEM_ROWS, MIXED_ROWS, QUERY_ROWS, FFN_ROWS) = range(5)
GROUPS = NKEY // 4
TOP_GROUPS = 8
BEST_GROUPS = 2
MATCH_GROUPS = 8
G_CAND = TOP_GROUPS
G_BEST = G_CAND + 1
G_MATCH = G_BEST + BEST_GROUPS
G_GATES = G_MATCH + MATCH_GROUPS
G_ROUTE = G_GATES + 1
G_BUILD = G_ROUTE + 1
QUADS = SEQ // 4
PAIRS = (GROUPS - 1 - G_BUILD) // 2
PLACES = [p for p in range(16) if p % 4 != 3]
assert G_BUILD + 2 * PAIRS + 1 == GROUPS and PAIRS * len(PLACES) + 4 == QUADS
LOWEST = -3.0e38
MASKED = -1.0e30
TWO_PI_PARTS = (6.28125, 0.0019340515136718750, float(2 * np.pi - 6.28125 - 0.0019340515136718750))
MAGIC = 1.5 * 2.0 ** 23
PI_SAFE = 3.1415925


class Signal:

    def __init__(self, sem):
        self.sem, self.n = sem, 0

    def on(self, ins, by=1):
        ins.then_inc(self.sem, by)
        self.n += by
        return self.n


def hybrid_layer(nc, x, mem, pos, weights, row_gains, cols, head_gains, u_t, v_t, out, h_kept, gelu_kept):
    inv_freq = np.float32(500000.0) ** (-np.arange(0, ROPE, 2, dtype=np.float32) / np.float32(ROPE))
    with ExitStack() as ctx:
        def sb(name, shape, dt=F32):
            return ctx.enter_context(nc.sbuf_tensor(name, shape, dt))

        def sem(name):
            return ctx.enter_context(nc.semaphore(name))

        def room_twice(name, shape, parts):
            typed, end = [], 0
            with ExitStack() as room:
                for part, first, n in parts:
                    if first > end:
                        room.enter_context(nc.sbuf_tensor(f"before_{part}", [P, first - end], F32))
                    typed.append(room.enter_context(nc.sbuf_tensor(part, [P, n], F32R)))
                    end = first + n
            return sb(name, shape), typed

        S0 = WSLOTS * WHALF
        big, (*ring_lo, mem_hi, mem_lo, hi_slot) = room_twice(
            "big", [P, NKEY * SEQ],
            [(f"ring_lo{s}", s * WHALF, WHALF) for s in range(WSLOTS)]
            + [("mem_hi", S0, 2048), ("mem_lo", S0 + 2048, 2048), ("hi_slot", NKEY * SEQ - WHALF, WHALF)])
        ring = [big[:, s * WHALF:(s + 1) * WHALF] for s in range(WSLOTS)]

        def scratch(at, n):
            return big[:, S0 + at:S0 + at + n]

        mem_hi = mem_hi[:].rearrange("p (k t) -> p k t", k=KD)
        mem_lo = mem_lo[:].rearrange("p (k t) -> p k t", k=KD)
        mixed = scratch(4096, 2048).rearrange("p (t n) -> p t n", t=NT)
        qk_a = scratch(4096, 2048).rearrange("p (t w n) -> p t w n", t=NT, w=2)
        q_at = scratch(6144, 1024).rearrange("p (b t) -> p b t", b=4)
        k_at = scratch(7168, 1024).rearrange("p (b t) -> p b t", b=4)
        q_bt = scratch(8192, 1024).rearrange("p (b t) -> p b t", b=4)
        k_bt = scratch(9216, 1024).rearrange("p (b t) -> p b t", b=4)
        q_mem = scratch(8192, 1024).rearrange("p (t n) -> p t n", t=NT)
        sq_mem = scratch(9216, 1024).rearrange("p (t n) -> p t n", t=NT)
        v_a = scratch(10240, 1024).rearrange("p (t n) -> p t n", t=NT)
        v_b = scratch(11264, 1024).rearrange("p (t n) -> p t n", t=NT)
        k_mem = scratch(12288, 1024).rearrange("p (t n) -> p t n", t=NT)
        v_mem = scratch(13312, 1024).rearrange("p (t n) -> p t n", t=NT)
        k_memt = scratch(14336, 1024).rearrange("p (b t) -> p b t", b=4)
        sticks = scratch(15360, 3072).rearrange("p (h c) -> p h c", h=NH)
        taps = scratch(18432, SEQ)
        untapped = scratch(18688, SEQ)
        tri_neg = scratch(18944, P)
        ones_neg = scratch(19072, P)
        hgain = scratch(19200, 2 * HD).rearrange("p (w d) -> p w d", w=2)
        gain_row0 = scratch(19328, D)
        q_peert = scratch(2048, 4096).rearrange("p (b t) -> p b t", b=NBLK)

        at = [NKEY * SEQ]

        def tail(n):
            at[0] -= n
            return big[:, at[0]:at[0] + n]

        scores = tail(4096).rearrange("p (b n) -> p b n", b=NT * NBLK)
        top_val = tail(512).rearrange("p (b k) -> p b k", b=NT * NBLK)
        top_pos = tail(512).bitcast(U32).rearrange("p (b k) -> p b k", b=NT * NBLK)
        top_id = tail(512).rearrange("p (b k) -> p b k", b=NT * NBLK)
        cand_val = tail(NT * PH * NCAND).rearrange("p (h c) -> p h c", c=NCAND)
        cand_id = tail(NT * PH * NCAND).rearrange("p (h c) -> p h c", c=NCAND)
        best = tail(2 * P).rearrange("p (h k) -> p h k", k=TOPK)
        best_pos = tail(2 * P).bitcast(U32).rearrange("p (h k) -> p h k", k=TOPK)
        best_at = tail(2 * P).rearrange("p (h k) -> p h k", k=TOPK)
        expert = tail(2 * P).rearrange("p (h k) -> p h k", k=TOPK)
        expert_i = tail(2 * P).bitcast(I32)
        digit = tail(4 * P).bitcast(I32)
        chosen = tail(6 * P).rearrange("p (n k) -> p n k", n=6)
        match = tail(2 * TOPK * NCAND).rearrange("p (n k c) -> p n k c", n=2, k=TOPK)

        h = sb("h", [P, NT, D])
        tmp = sb("tmp", [P, 6144])
        t1, t2 = tmp[:, 0:3072], tmp[:, 3072:6144]
        raw = tmp[:, 0:4096].rearrange("p (s n) -> p s n", s=4)
        h_room = h[:].rearrange("p t n -> p (t n)")
        gelus = h_room[:, 0:1024].rearrange("p (s t) -> p s t", s=4)
        hot_i = [part[:, n * 512:(n + 1) * 512].rearrange("p (q n) -> p q n", q=4)
                 for part in (h_room[:, 1024:2048], tmp[:, 4096:5120]) for n in range(2)]
        hot_j, (hot_j_parts,) = room_twice("hot_j", [P, 4, 4, P], [("hot_j_parts", 0, WHALF)])
        h_back = hot_j[:].rearrange("p b q n -> p (b q n)")
        first_gelus = h_back.rearrange("p (g s t) -> p g s t", g=2, s=4)
        route_t = tmp[:, 5376:6144].rearrange("p (n t) -> p n t", n=3)
        part_hi = sb("part_hi", [P, 4, 512], F32R)
        part_lo = sb("part_lo", [P, 4, 512], F32R)
        x_hi = sb("x_hi", [P, KD, SEQ], F32R)
        x_lo = sb("x_lo", [P, KD, SEQ], F32R)
        v_hi = [part_hi, x_hi[:].rearrange("p (m k) t -> p m (k t)", m=4)]
        v_lo = [part_lo, x_lo[:].rearrange("p (m k) t -> p m (k t)", m=4)]
        acts_room, (acts_split,) = room_twice("acts_room", [P, 4, SEQ], [("acts_split", 0, 4 * SEQ)])
        a_hi, a_lo = (acts_split[:, w * 2 * SEQ:(w + 1) * 2 * SEQ].rearrange("p (b t) -> p b t", b=2) for w in range(2))
        gain_row = [gain_row0, acts_room[:].rearrange("p b t -> p (b t)")]
        hi_slots = [part_hi[:], part_lo[:], hot_j_parts[:].rearrange("p (k n) -> p k n", k=4),
                    hi_slot[:].rearrange("p (k n) -> p k n", k=4)]
        ident = sb("ident", [P, P])
        iota_key = sb("iota_key", [P, P])
        iota_cand = sb("iota_cand", [P, NCAND])
        gain = sb("gain", [P, 2])
        posi = sb("posi", [P, NT], I32)
        posf = sb("posf", [P, NT])
        freq = sb("freq", [P, HALF])
        cossin = sb("cossin", [P, 2, NT, HALF])
        one = sb("one", [P, 1])
        stat = sb("stat", [P, 5, 32])
        ps = ctx.enter_context(nc.psum_tensor("ps", [P, 8, 512], F32))

        def bank(b, n=1):
            return ps[:, b:b + n, :].rearrange("p b n -> p (b n)")

        loaded_x = [sem(f"loaded_x{t}") for t in range(NT)]
        loaded_mem, loaded_c = sem("loaded_mem"), sem("loaded_c")
        gain_loaded = [sem("gain_loaded0"), sem("gain_loaded1")]
        w_loaded = [sem(f"w_loaded{s}") for s in range(WSLOTS)]
        w_hi_ready, w_lo_ready = sem("w_hi_ready"), sem("w_lo_ready")
        w_used = sem("w_used")
        ident_ready, masks_ready = sem("ident_ready"), sem("masks_ready")
        pool_step, one_ready = sem("pool_step"), sem("one_ready")
        sumsq, mean_ready, root_ready = sem("sumsq"), sem("mean_ready"), sem("root_ready")
        rows_normed, x_psum = sem("rows_normed"), sem("x_psum")
        x_hi_ready, x_lo_ready = sem("x_hi_ready"), sem("x_lo_ready")
        b_taken = [sem(f"b_taken{t}") for t in range(NT)]
        a_mixed, out_projected, h_ready = sem("a_mixed"), sem("out_projected"), sem("h_ready")
        taken = [sem(f"taken{u}") for u in range(PEER0 + PEER_UNITS)]
        qk_normed, at_psum, q_at_ready, k_at_ready = sem("qk_normed"), sem("at_psum"), sem("q_at_ready"), sem("k_at_ready")
        a_scores, a_max, a_exp, a_weighted, a_turned, a_out = (
            sem("a_scores"), sem("a_max"), sem("a_exp"), sem("a_weighted"), sem("a_turned"), sem("a_out"))
        a_prob_t = sem("a_prob_t")
        b_scores, b_abs, b_log, b_soft, b_soft_masked, b_summed, b_stick, b_stick_masked, b_out = (
            sem("b_scores"), sem("b_abs"), sem("b_log"), sem("b_soft"), sem("b_soft_masked"), sem("b_summed"),
            sem("b_stick"), sem("b_stick_masked"), sem("b_out"))
        b_evens = sem("b_evens")
        mk_normed, mk_psum, mk_ready = sem("mk_normed"), sem("mk_psum"), sem("mk_ready")
        mq_projected, mq_taken = sem("mq_projected"), sem("mq_taken")
        mq_psum, mq_ready = sem("mq_psum"), sem("mq_ready")
        m_scores, m_max, m_exp, m_weighted, m_turned, m_out, m_out_ready, o_projected = (
            sem("m_scores"), sem("m_max"), sem("m_exp"), sem("m_weighted"), sem("m_turned"),
            sem("m_out"), sem("m_out_ready"), sem("o_projected"))
        m_prob_t = [sem(f"m_prob_t{t}") for t in range(NT)]
        angles, sines = sem("angles"), sem("sines")
        key_scores, key_scores_taken = sem("key_scores"), sem("key_scores_taken")
        best_centred, gates_exp = sem("best_centred"), sem("gates_exp")
        routed, route_psum, route_ready = sem("routed"), sem("route_psum"), sem("route_ready")
        raw_loaded = [sem(f"raw_loaded{s}") for s in range(4)]
        part_hi_ready, part_lo_ready, part_used = sem("part_hi_ready"), sem("part_lo_ready"), sem("part_used")
        gelu_done = sem("gelu_done")
        hots_ready, gated = sem("hots_ready"), sem("gated")
        g_done, g_taken, acts_ready = sem("g_done"), sem("g_taken"), sem("acts_ready")
        h_stored, h_back_loaded = sem("h_stored"), sem("h_back_loaded")
        gelu_stored = [sem(f"gelu_stored{s}") for s in range(4)]
        first_gelus_loaded = [sem("first_gelus_loaded0"), sem("first_gelus_loaded1")]
        gelu_loaded = [sem(f"gelu_loaded{s}") for s in range(4)]
        a_hi_ready, a_lo_ready = sem("a_hi_ready"), sem("a_lo_ready")
        top_step, best_step, at_ready = sem("top_step"), sem("best_step"), sem("at_ready")
        matched, match_ids, match_summed = sem("matched"), sem("match_ids"), sem("match_summed")
        out_ready, stored = sem("out_ready"), sem("stored")
        dve_step, act_step = sem("dve_step"), sem("act_step")

        block = ctx.enter_context(nc.Block())

        G_QM, G_KM = 0, 1
        rows1, rows2 = (part[:, 0:2048].rearrange("p (t n) -> p t n", t=NT) for part in (t1, t2))
        ROWS = rows1, rows2, mixed, rows1, rows1
        X_PARTS = (x_hi, x_lo), (mem_hi, mem_lo), (x_hi, x_lo), (x_hi, x_lo), (x_hi, x_lo)

        def hi_of(n):
            return hi_slots[SPLIT.index(n) % HI_SLOTS]

        def lo_of(n):
            return ring_lo[n % WSLOTS][:].rearrange("p (k n) -> p k n", k=4)

        def hi_free(n):
            m = SPLIT.index(n) - HI_SLOTS
            return SPLIT[m] + 1 if m >= 0 else 0

        @block.sync
        def _(sp):
            def load_weights(first, last):
                for n in range(first, last + 1):
                    if n >= WSLOTS:
                        sp.wait_ge(w_used, n - WSLOTS + 1)
                    sp.dma_start(ring[n % WSLOTS], weights[n]).then_inc(w_loaded[n % WSLOTS], 16)

            def load_gain(i):
                if i >= 2:
                    sp.wait_ge(rows_normed, 2 * (i - 1))
                sp.dma_start(gain_row[i % 2], row_gains[i:i + 1].partition_broadcast(P)).then_inc(gain_loaded[i % 2], 16)

            sp.dma_start(h[:, 0, :], x[0:P]).then_inc(loaded_x[0], 16)
            load_gain(X_ROWS)
            sp.dma_start(h[:, 1, :], x[P:SEQ]).then_inc(loaded_x[1], 16)
            load_weights(0, 1)
            sp.dma_start(rows2, mem.rearrange("(t p) n -> p t n", p=P)).then_inc(loaded_mem, 16)
            load_gain(MEM_ROWS)
            load_weights(2, 3)
            sp.dma_start(gain[:], cols).then_inc(loaded_c, 16)
            sp.dma_start(hgain, head_gains.partition_broadcast(P)).then_inc(loaded_c, 16)
            sp.dma_start(posi[:], pos).then_inc(loaded_c, 16)
            load_weights(4, 9)
            load_gain(MIXED_ROWS)
            load_weights(10, 12)
            load_gain(QUERY_ROWS)
            load_weights(13, 21)
            load_gain(FFN_ROWS)
            load_weights(22, KEYS_HALF)

            sp.wait_ge(x_psum, 4 * (FFN_ROWS + 1))
            for s in range(4):
                sp.dma_start(raw[:, s, :], u_t[s]).then_inc(raw_loaded[s], 16)
            sp.wait_ge(h_ready, 4)
            sp.wait_ge(rows_normed, 2 * (FFN_ROWS + 1))
            sp.dma_start(h_kept, h_room).then_inc(h_stored, 16)

            def load(table, g, s, chunk):
                sp.wait_ge(part_lo_ready, g * 8 + 2 * (s - 3))
                sp.dma_start(raw[:, s, :], table[chunk]).then_inc(raw_loaded[s], 16)

            def store_gelu(i, s):
                sp.wait_ge(gelu_done, i + 1)
                sp.dma_start(gelu_kept[i], gelus[:, s, :]).then_inc(gelu_stored[s], 16)

            for g in (1, 2):
                for s in range(4):
                    load(u_t, g, s, g * 4 + s)
                    if g * 4 + s >= 6:
                        store_gelu(g * 4 + s - 6, (s + 2) % 4)
            with sp.Fori(3, GROUPS) as g:
                for s in range(4):
                    load(u_t, g, s, g * 4 + s)
                    store_gelu(g * 4 + (s - 6), (s + 2) % 4)
            for s in range(4):
                load(v_t, GROUPS, s, s)
                store_gelu(NKEY + s - 6, (s + 2) % 4)
                if s == 1:
                    sp.wait_ge(g_done, QUADS)
                    for n in range(4):
                        sp.wait_ge(gelu_stored[n], 32)
                    for n in range(2):
                        sp.dma_start(first_gelus[:, n], gelu_kept[4 * n:4 * n + 4].rearrange(
                            "s p t -> p s t")).then_inc(first_gelus_loaded[n], 16)
            for s in range(2, 4):
                store_gelu(NKEY - 4 + s, s)
            for s in range(4):
                load(v_t, GROUPS + 1, s, s + 4)
                sp.wait_ge(gelu_stored[s], 16 * GROUPS)
            with sp.Fori(GROUPS + 2, 2 * GROUPS) as g:
                for s in range(4):
                    load(v_t, g, s, g * 4 + (s - NKEY))
                    sp.wait_ge(acts_ready, g * 4 + (s - NKEY - 3))
                    sp.dma_start(gelus[:, s, :], gelu_kept[g * 4 + (s - NKEY)]).then_inc(gelu_loaded[s], 16)
            sp.wait_ge(h_stored, 16)
            sp.dma_start(h_back, h_kept).then_inc(h_back_loaded, 16)
            sp.wait_ge(out_ready, 1)
            sp.dma_start(out.rearrange("(t p) n -> p t n", p=P),
                         h_back.rearrange("p (t n) -> p t n", t=NT)).then_inc(stored, 16)
            sp.wait_ge(stored, 16)

        @block.gpsimd
        def _(pool):
            step = Signal(pool_step)

            def chain(ins):
                pool.wait_ge(pool_step, step.on(ins))

            chain(pool.memset(ident[:], 0.0))
            pool.affine_select(ident[:], ident[:], [[-1, P]], ALU.not_equal, 1.0, base=0,
                               channel_multiplier=1).then_inc(ident_ready, 1)
            pool.iota(untapped.bitcast(I32), [[-1, SEQ]], base=P, channel_multiplier=1).then_inc(masks_ready, 1)
            chain(pool.memset(tri_neg, -1.0))
            pool.affine_select(tri_neg, tri_neg, [[-1, P]], ALU.is_ge, 0.0, base=0,
                               channel_multiplier=1).then_inc(masks_ready, 1)
            pool.memset(ones_neg, -1.0).then_inc(masks_ready, 1)
            pool.iota(iota_key[:], [[1, P]], base=0, channel_multiplier=0,
                      allow_small_or_imprecise_dtypes=True).then_inc(masks_ready, 1)
            pool.iota(iota_cand[:], [[1, NCAND]], base=0, channel_multiplier=0,
                      allow_small_or_imprecise_dtypes=True).then_inc(masks_ready, 1)
            for g in range(2):
                soft = t2[:, 1536:3072]
                pool.wait_ge(b_soft, g + 1)
                for at, n in ((0, SEQ), (1024, P)):
                    part = soft[:, at:at + 4 * n].rearrange("p (h t) -> p h t", h=4)[:, :, 0:P]
                    pool.affine_select(part, part, [[0, 4], [1, P]], ALU.is_gt, 0.0, base=0,
                                       channel_multiplier=-1).then_inc(b_soft_masked, 1)
                pool.wait_ge(b_stick, 2 * (g + 1))
                for at in (0, SEQ):
                    part = sticks[:, 4 * g:4 * g + 4, at:at + P]
                    pool.affine_select(part, part, [[0, 4], [1, P]], ALU.is_gt, 0.0, base=0,
                                       channel_multiplier=-1).then_inc(b_stick_masked, 1)

            with pool.Fori(0, MATCH_GROUPS) as g:
                for n in range(2):
                    pool.wait_ge(matched, g * 2 + (n + 1))
                    ids = cand_id[:, bass.ds(g * 2 + n, 1), :].rearrange("p h c -> p (h c)")
                    pool.tensor_tensor(match[:, n], match[:, n], ids.unsqueeze(1).broadcast_to([P, TOPK, NCAND]),
                                       ALU.mult).then_inc(match_ids, 1)

        def b_head(g, j):
            return 4 * g + (0, 2, 1, 3)[j]

        @block.tensor
        def _(pe):
            def turn(i, t, b):
                pe.wait_ge(rows_normed, NT * i + t + 1)
                for k in range(KD):
                    ins = pe.transpose(ps[:, b + k // 4, (k % 4) * P:][:, 0:P], ROWS[i][:, t, k * P:(k + 1) * P],
                                       ident[:])
                    if k % 4 == 3:
                        ins.then_inc(x_psum, 1)

            def parts_ready(i, t, a):
                pe.wait_ge(x_lo_ready, 4 * i + 2 * t + a + 1)

            def rows_half(u, a, t, b, i):
                n = 2 * u + a
                pe.wait_ge(w_lo_ready, SPLIT.index(n) + 1)
                parts_ready(i, t, a)
                hi, lo = X_PARTS[i]
                for k in range(4):
                    for m, (x_, w) in enumerate(((hi, hi_of(n)), (hi, lo_of(n)), (lo, hi_of(n)))):
                        ins = pe.matmul(bank(b), x_[:, 4 * a + k, t * P:(t + 1) * P], w[:, k, :],
                                        start=(a == 0 and k == 0 and m == 0), stop=(a == 1 and k == 3 and m == 2))
                return ins

            def project_rows(u, b, i, bank_free=()):
                for a in range(2):
                    for t in range(NT):
                        if bank_free and a == 0:
                            pe.wait_ge(bank_free[t], 1)
                        ins = rows_half(u, a, t, b + t, i)
                    ins.then_inc(w_used, 1)

            def project_cols(u, b, i):
                hi, lo = X_PARTS[i]
                for a in range(2):
                    n = 2 * u + a
                    pe.wait_ge(w_lo_ready, SPLIT.index(n) + 1)
                    parts_ready(i, 1, a)
                    for c in range(4):
                        for k in range(4):
                            for m, (w, x_) in enumerate(((hi_of(n), hi), (hi_of(n), lo), (lo_of(n), hi))):
                                ins = pe.matmul(ps[:, b + c // 2, (c % 2) * SEQ:][:, 0:SEQ],
                                                w[:, k, c * P:(c + 1) * P], x_[:, 4 * a + k, :],
                                                start=(a == 0 and c % 2 == 0 and k == 0 and m == 0),
                                                stop=(a == 1 and k == 3 and m == 2), skip_group_check=True)
                    ins.then_inc(w_used, 1)

            def stick_scores(g):
                for j in range(4):
                    hh = b_head(g, j)
                    rows = slice(HD * (hh % 2), HD * (hh % 2) + HD)
                    if j == 2:
                        pe.wait_ge(b_evens, g + 1)
                    pe.matmul(ps[:, j // 2, (j % 2) * SEQ:][:, 0:SEQ], k_bt[rows, hh // 2, 0:P],
                              q_bt[rows, hh // 2, :], start=(j % 2 == 0), stop=True, skip_group_check=True)
                    ins = pe.matmul(ps[:, 2, j * P:(j + 1) * P], k_bt[rows, hh // 2, P:SEQ],
                                    q_bt[rows, hh // 2, P:SEQ], start=(j == 0), stop=True, skip_group_check=True)
                    if j == 1:
                        ins.then_inc(b_evens, 1)
                ins.then_inc(b_scores, 1)

            def stick_sums(g):
                soft = t2[:, 1536:3072]
                pe.wait_ge(b_soft_masked, 2 * (g + 1))
                for j in range(4):
                    s0 = soft[:, j * SEQ:(j + 1) * SEQ]
                    s1 = soft[:, 1024 + j * P:1024 + (j + 1) * P]
                    z0 = ps[:, j // 2, (j % 2) * SEQ:][:, 0:SEQ]
                    pe.matmul(z0, tri_neg, s0, start=False, stop=False, skip_group_check=True)
                    pe.matmul(z0[:, P:SEQ], ones_neg, s1, start=False, stop=True, skip_group_check=True)
                    ins = pe.matmul(ps[:, 2, j * P:(j + 1) * P], tri_neg, s1, start=False, stop=True,
                                    skip_group_check=True)
                ins.then_inc(b_summed, 1)

            pe.wait_ge(ident_ready, 1)
            turn(X_ROWS, 0, 0)
            turn(X_ROWS, 1, 2)
            project_cols(Q_B, 4, X_ROWS)
            project_cols(K_B, 6, X_ROWS)
            turn(MEM_ROWS, 0, 0)
            turn(MEM_ROWS, 1, 2)
            pe.wait_ge(taken[Q_B], 1)
            project_rows(Q_A, 4, X_ROWS)
            parts_ready(MEM_ROWS, 1, 1)
            pe.wait_ge(taken[K_B], 1)
            pe.wait_ge(masks_ready, 5)
            stick_scores(0)
            project_rows(K_A, 6, X_ROWS)
            stick_sums(0)
            pe.wait_ge(taken[Q_A], 1)
            project_rows(V_B, 4, X_ROWS)
            pe.wait_ge(b_stick, 2)
            stick_scores(1)
            pe.wait_ge(taken[K_A], 1)
            project_rows(V_A, 6, X_ROWS)
            stick_sums(1)
            pe.wait_ge(taken[V_B], 1)
            project_rows(K_MEM, 4, MEM_ROWS)

            pe.wait_ge(b_stick, 4)
            pe.wait_ge(qk_normed, 1)
            for w in range(2):
                for c in range(4):
                    for t in range(NT):
                        ins = pe.transpose(ps[:, 2 * w + c // 2, (c % 2) * SEQ + t * P:][:, 0:P],
                                           qk_a[:, t, w, c * P:(c + 1) * P], ident[:])
                ins.then_inc(at_psum, 1)
            pe.wait_ge(taken[K_MEM], 1)
            pe.wait_ge(q_at_ready, 1)
            pe.wait_ge(k_at_ready, 1)
            for par in range(2):
                rows = slice(HD * par, HD * par + HD)
                for c in range(4):
                    ins = pe.matmul(ps[:, par, c * P:(c + 1) * P], q_at[rows, c, 0:P], k_at[rows, c, 0:P],
                                    start=True, stop=True)
            ins.then_inc(a_scores, 1)
            for par in range(2):
                rows = slice(HD * par, HD * par + HD)
                for c in range(4):
                    ins = pe.matmul(ps[:, 2 + 2 * par + c // 2, (c % 2) * SEQ:][:, 0:SEQ],
                                    q_at[rows, c, P:SEQ], k_at[rows, c, :], start=True, stop=True)
                ins.then_inc(a_scores, 1)

            pe.wait_ge(b_stick_masked, 4)
            pe.wait_ge(taken[V_A], 1)
            for t in range(NT):
                for hh in range(NH):
                    for sblk in range(t + 1):
                        g, j = hh // 4, (0, 2, 1, 3)[hh % 4]
                        st = sticks[:, 4 * g + j, :]
                        at = t * P if sblk == 0 else SEQ
                        ins = pe.matmul(ps[:, 6 + t, hh * HD:(hh + 1) * HD], st[:, at:at + P],
                                        v_b[:, sblk, hh * HD:(hh + 1) * HD], start=(sblk == 0), stop=(sblk == t))
                ins.then_inc(b_out, 1)
            project_rows(V_MEM, 6, MEM_ROWS, b_taken)

            for n in range(24):
                if n % 8 == 0:
                    pe.wait_ge(a_weighted, n // 8 + 1)
                ins = pe.transpose(ps[:, n // 4, (n % 4) * P:][:, 0:P], t2[:, n * P:(n + 1) * P], ident[:])
                if n % 8 == 7:
                    ins.then_inc(a_turned, 1)
            pe.wait_ge(taken[V_MEM], 1)
            for t in range(NT):
                pe.wait_ge(a_prob_t, (1, 3)[t])
                for hh in range(NH):
                    slot = (hh % 2) * 4 + hh // 2
                    for sblk in range(t + 1):
                        at = slot * P if t == 0 else 1024 + slot * SEQ + sblk * P
                        ins = pe.matmul(ps[:, 6 + t, hh * HD:(hh + 1) * HD], t1[:, at:at + P],
                                        v_a[:, sblk, hh * HD:(hh + 1) * HD], start=(sblk == 0), stop=(sblk == t))
                ins.then_inc(a_out, 1)

            pe.wait_ge(mk_normed, 1)
            for c in range(MH):
                for t in range(NT):
                    ins = pe.transpose(ps[:, 4 + c // 2, (c % 2) * SEQ + t * P:][:, 0:P],
                                       k_mem[:, t, c * P:(c + 1) * P], ident[:])
            ins.then_inc(mk_psum, 1)

            turn(MIXED_ROWS, 0, 0)
            pe.wait_ge(mk_ready, 1)
            for t in range(NT):
                for n in range(2):
                    if (t, n) == (0, 1):
                        turn(MIXED_ROWS, 1, 2)
                    for a in range(2):
                        ins = rows_half(OUT0 + n, a, t, 4 + 2 * t + n, MIXED_ROWS)
                        if t == 1 and (n, a) != (1, 1):
                            ins.then_inc(w_used, 1)
                if t == 0:
                    ins.then_inc(out_projected, 1)
            ins.then_inc(w_used, 1)

            def turn_queries(t):
                pe.wait_ge(mq_taken, t + 1)
                for c in range(MH):
                    ins = pe.transpose(ps[:, 5 + 2 * t, c * P:(c + 1) * P], q_mem[:, t, c * P:(c + 1) * P], ident[:])
                ins.then_inc(mq_psum, 1)

            for t in range(NT):
                turn(QUERY_ROWS, t, 2 * t)
                pe.wait_ge(h_ready, t + 1)
                if t == 1:
                    turn_queries(0)
                for a in range(2):
                    ins = rows_half(Q_MEM, a, t, 4 + 2 * t, QUERY_ROWS)
                    if t == 1 and a == 0:
                        ins.then_inc(w_used, 1)
                if t == 0:
                    ins.then_inc(mq_projected, 1)
            ins.then_inc(w_used, 1)
            for t in range(NT):
                if t == 1:
                    turn_queries(1)
                pe.wait_ge(mq_ready, t + 1)
                for c in range(MH):
                    ins = pe.matmul(ps[:, 2 * t + c // 2, (c % 2) * SEQ:][:, 0:SEQ],
                                    q_at[:, c, t * P:(t + 1) * P], k_memt[:, c, :], start=True, stop=True)
                ins.then_inc(m_scores, 1)
            for t in range(NT):
                pe.wait_ge(m_weighted, t + 1)
                for c in range(MH):
                    for m in range(2):
                        ins = pe.transpose(ps[:, 4 + 2 * t + c // 2, (c % 2) * SEQ + m * P:][:, 0:P],
                                           t2[:, (t * MH + c) * SEQ + m * P:][:, 0:P], ident[:])
                ins.then_inc(m_turned, 1)
            for t in range(NT):
                pe.wait_ge(m_prob_t[t], 1)
                for c in range(MH):
                    for m in range(2):
                        ins = pe.matmul(ps[:, t, c * P:(c + 1) * P], v_mem[:, m, c * P:(c + 1) * P],
                                        t1[:, t * D + (c * 2 + m) * P:][:, 0:P], start=(m == 0), stop=(m == 1))
                ins.then_inc(m_out, 1)
            for a in range(2):
                n = 2 * O_MEM + a
                pe.wait_ge(w_loaded[n % WSLOTS], 16 * (n // WSLOTS + 1))
            for t in range(NT):
                pe.wait_ge(m_out_ready, t + 1)
                for a in range(2):
                    w = ring[(2 * O_MEM + a) % WSLOTS].rearrange("p (k n) -> p k n", k=2)
                    for n in range(2):
                        for k in range(2):
                            ins = pe.matmul(bank(4 + 2 * t + n), k_at[:, 2 * a + k, t * P:(t + 1) * P],
                                            w[:, k, n * 512:(n + 1) * 512],
                                            start=(a == 0 and k == 0), stop=(a == 1 and k == 1))
                    if t == 1 and a == 0:
                        ins.then_inc(w_used, 1)
                if t == 0:
                    ins.then_inc(o_projected, 1)
            ins.then_inc(w_used, 1)

            turn(FFN_ROWS, 0, 0)
            turn(FFN_ROWS, 1, 2)
            for n in range(PEER_UNITS):
                project_cols(PEER0 + n, (4 + 2 * n) % 8, FFN_ROWS)
            pe.wait_ge(w_loaded[KEYS_HALF % WSLOTS], 16 * (KEYS_HALF // WSLOTS + 1))
            keys = ring[KEYS_HALF % WSLOTS].rearrange("p (b n) -> p b n", b=NBLK)
            for t in range(NT):
                for b in range(NBLK):
                    if t == 0 and b % 4 == 0:
                        pe.wait_ge(taken[PEER0 + b // 4], 1)
                        if b == 0:
                            pe.wait_ge(taken[PEER0 + 2], 1)
                            pe.wait_ge(taken[PEER0 + 3], 1)
                    ins = pe.matmul(ps[:, 4 * t + b // 4, (b % 4) * P:][:, 0:P], q_peert[:, b, t * P:(t + 1) * P],
                                    keys[:, b, :], start=True, stop=True)
                ins.then_inc(key_scores, 1)

            def hidden(g, s, a, first=False):
                c = g * 4 + s
                pe.wait_ge(part_lo_ready, 2 * c + (a + 1))
                if a == 0 and not first:
                    pe.wait_ge(gelu_done, c - 3)
                part = 2 * (s % 2) + a
                for k in range(4):
                    w = slice(k * P, (k + 1) * P)
                    for n, (u, r) in enumerate(((part_hi, x_hi), (part_hi, x_lo), (part_lo, x_hi))):
                        ins = pe.matmul(ps[:, s, 0:SEQ], u[:, part, w], r[:, 4 * a + k, :],
                                        start=(a == 0 and k == 0 and n == 0), stop=(a == 1 and k == 3 and n == 2))
                ins.then_inc(part_used, 1)

            def gate_matrix(n, b, first=False):
                pe.wait_ge(gated, n + 1)
                if not first:
                    pe.wait_ge(g_taken, n - 3)
                for q in range(4):
                    ins = pe.matmul(ps[:, 4 + b, q * P:(q + 1) * P], hot_j[:, b, q, :], hot_i[b][:, q, :],
                                    start=True, stop=True)
                ins.then_inc(g_done, 1)

            def plain_group(g, first=False):
                for s in range(4):
                    for a in range(2):
                        hidden(g, s, a, first)

            pe.wait_ge(key_scores_taken, 1)
            plain_group(0, True)
            with pe.Fori(1, G_ROUTE) as g:
                plain_group(g)
            pe.wait_ge(routed, 1)
            for w in range(3):
                for t in range(NT):
                    ins = pe.transpose(ps[:, 6 + w // 2, (w % 2) * SEQ + t * P:][:, 0:P], chosen[:, w * NT + t, :],
                                       ident[:])
            ins.then_inc(route_psum, 1)
            plain_group(G_ROUTE)

            def build_pair(g, n, first=False):
                for p in range(16):
                    hidden(g + p // 8, p // 2 % 4, p % 2)
                    if p in PLACES:
                        m = PLACES.index(p)
                        gate_matrix(n + m, m % 4, first and m < 4)

            pe.wait_ge(route_ready, 1)
            build_pair(G_BUILD, 0, True)
            with pe.Fori(1, PAIRS) as r:
                build_pair(r * 2 + G_BUILD, r * len(PLACES))
            for p in range(8):
                hidden(GROUPS - 1, p // 2, p % 2)
                if p < 4:
                    gate_matrix(QUADS - 4 + p, p)

            def mix(g, s, a, first=False):
                c = g * 4 + s
                pe.wait_ge(part_lo_ready, 2 * c + (a + 1))
                if a == 0:
                    pe.wait_ge(a_lo_ready, c - (NKEY - 1))
                b = s % 2
                hi, lo = v_hi[s // 2], v_lo[s // 2]
                for t in range(NT):
                    for n, (w, r) in enumerate(((a_hi, hi), (a_hi, lo), (a_lo, hi))):
                        ins = pe.matmul(bank(2 * t + a), w[:, b, t * P:(t + 1) * P], r[:, 2 * b + a, :],
                                        start=(first and n == 0), stop=False, skip_group_check=True)
                ins.then_inc(part_used, 1)

            for s in range(4):
                for a in range(2):
                    if s == 0:
                        pe.wait_ge(gelu_done, NKEY - 1 + a)
                    mix(GROUPS, s, a, s == 0)
            with pe.Fori(GROUPS + 1, 2 * GROUPS) as g:
                for s in range(4):
                    mix(g, s, 0)
                    mix(g, s, 1)

        @block.scalar
        def _(act):
            step = Signal(act_step)

            def chain(ins):
                act.wait_ge(act_step, step.on(ins))

            roots = [0]

            def root(cols):
                roots[0] += 1
                act.wait_ge(mean_ready, roots[0])
                act.activation(stat[:, 2, cols], stat[:, 1, cols], ACT.Sqrt).then_inc(root_ready, 1)

            def squares(junk, src, col):
                act.activation(junk, src, ACT.Square, accum_out=stat[:, 0, col:col + 1]).then_inc(sumsq, 1)

            def weights_hi(n):
                act.wait_ge(w_loaded[n % WSLOTS], 16 * (n // WSLOTS + 1))
                if hi_free(n):
                    act.wait_ge(w_used, hi_free(n))
                act.activation(hi_of(n), ring[n % WSLOTS].rearrange("p (k n) -> p k n", k=4),
                               ACT.Copy).then_inc(w_hi_ready, 1)

            def turned_hi(i, t, b):
                for a in range(2):
                    act.wait_ge(x_psum, 4 * i + 2 * t + a + 1)
                    act.activation(X_PARTS[i][0][:, 4 * a:4 * a + 4, t * P:(t + 1) * P],
                                   bank(b + a).rearrange("p (k t) -> p k t", k=4), ACT.Copy).then_inc(x_hi_ready, 1)

            def sticks_log(g):
                act.wait_ge(b_scores, g + 1)
                if g:
                    act.wait_ge(b_soft, g)
                e = t2[:, 0:1536]
                chain(act.activation(e, bank(0, 3), ACT.Abs))
                chain(act.activation(e, e, ACT.Exp, scale=-1.0))
                act.activation(e, e, ACT.Ln, bias=1.0).then_inc(b_log, 1)

            def sticks_exp(g):
                act.wait_ge(b_summed, g + 1)
                act.activation(sticks[:, 4 * g:4 * g + 4, 0:SEQ],
                               bank(0, 2).rearrange("p (h t) -> p h t", h=4), ACT.Exp).then_inc(b_stick, 1)
                act.activation(sticks[:, 4 * g:4 * g + 4, SEQ:SEQ + P],
                               bank(2).rearrange("p (h t) -> p h t", h=4), ACT.Exp).then_inc(b_stick, 1)

            def take_unit(u, dst, b, scale=1.0):
                act.wait_ge(w_used, 2 * (u + 1))
                act.activation(dst, bank(b, 2), ACT.Copy, scale=scale).then_inc(taken[u], 1)

            def take_qk(w, b):
                u = (Q_A, K_A)[w]
                act.wait_ge(w_used, 2 * (u + 1))
                act.activation(qk_a[:, :, w, :], ps[:, b:b + 2, :], ACT.Copy).then_inc(taken[u], 1)

            junk = scratch(15360, 2048).rearrange("p (t n) -> p t n", t=NT)
            act.wait_ge(one_ready, 1)
            act.activation(one[:], one[:], ACT.Sqrt)
            for t in range(NT):
                act.wait_ge(loaded_x[t], 16)
                squares(junk[:, t, :], h[:, t, :], t)
                root(slice(t, t + 1))
            turned_hi(X_ROWS, 0, 0)
            weights_hi(0)
            turned_hi(X_ROWS, 1, 2)
            weights_hi(1)
            act.wait_ge(loaded_mem, 16)
            act.wait_ge(sumsq, 2)
            for t in range(NT):
                squares(junk[:, t, :], rows2[:, t, :], 2 + t)
            root(slice(2, 4))
            for n in (2, 3, 4, 5):
                weights_hi(n)
            take_unit(Q_B, q_bt.rearrange("p b t -> p (b t)"), 4, HD ** -0.5)
            weights_hi(6)
            act.wait_ge(angles, 1)
            act.activation(cossin[:].rearrange("p w t f -> p (w t f)"),
                           cossin[:].rearrange("p w t f -> p (w t f)"), ACT.Sin).then_inc(sines, 1)
            turned_hi(MEM_ROWS, 0, 0)
            turned_hi(MEM_ROWS, 1, 2)
            weights_hi(7)
            weights_hi(8)
            take_qk(0, 4)
            weights_hi(9)
            sticks_log(0)
            weights_hi(10)
            take_qk(1, 6)
            weights_hi(11)
            sticks_exp(0)
            root(slice(0, 32))
            weights_hi(12)
            take_unit(V_B, v_b.rearrange("p t n -> p (t n)"), 4)
            weights_hi(13)
            sticks_log(1)
            weights_hi(14)
            sticks_exp(1)
            weights_hi(15)
            weights_hi(16)
            take_unit(K_MEM, k_mem.rearrange("p t n -> p (t n)"), 4)
            act.wait_ge(at_psum, 2)
            act.activation(k_at.rearrange("p b t -> p (b t)"), bank(2, 2), ACT.Copy).then_inc(k_at_ready, 1)
            weights_hi(17)
            for n in range(16):
                if n in (0, 8, 12):
                    act.wait_ge(a_max, (0, 8, 12).index(n) + 1)
                part = t2[:, n * P:(n + 1) * P] if n < 8 else t2[:, 1024 + (n - 8) * SEQ:][:, 0:SEQ]
                act.activation(part, part, ACT.Exp, bias=stat[:, 3, n:n + 1], scale=HD ** -0.5).then_inc(a_exp, 1)
            act.wait_ge(b_out, 2)
            act.activation(mixed[:, 1, 512:1024], bank(7), ACT.Copy).then_inc(b_taken[1], 1)
            for t in range(NT):
                act.wait_ge(b_taken[t], 1)
            for t in range(NT):
                squares(q_mem[:, t, :], mixed[:, t, 512:1024], t)
            root(slice(8, 16))
            root(slice(0, 2))
            weights_hi(18)
            take_unit(V_MEM, v_mem.rearrange("p t n -> p (t n)"), 6)
            for n in range(3):
                act.wait_ge(a_turned, n + 1)
                act.activation(t1[:, n * 1024:(n + 1) * 1024], bank(2 * n, 2), ACT.Copy).then_inc(a_prob_t, 1)
            act.wait_ge(sumsq, 6)
            for t in range(NT):
                act.wait_ge(a_mixed, t + 1)
                squares(q_mem[:, t, :], mixed[:, t, 0:512], 2 + t)
                root(slice(2 + t, 3 + t))
                if t == 0:
                    weights_hi(19)
                turned_hi(MIXED_ROWS, t, 2 * t)
            act.wait_ge(h_ready, 1)
            squares(t1[:, 0:D], h[:, 0, :], 4)
            root(slice(4, 5))
            weights_hi(20)
            weights_hi(21)
            turned_hi(QUERY_ROWS, 0, 0)
            act.wait_ge(h_ready, 2)
            squares(t1[:, D:2 * D], h[:, 1, :], 5)
            root(slice(5, 6))
            act.wait_ge(mq_projected, 1)
            act.activation(q_mem[:, 0, :], bank(4), ACT.Copy).then_inc(mq_taken, 1)
            turned_hi(QUERY_ROWS, 1, 2)
            root(slice(16, 20))
            act.wait_ge(w_used, 2 * Q_MEM + 2)
            act.activation(q_mem[:, 1, :], bank(6), ACT.Copy).then_inc(mq_taken, 1)
            root(slice(20, 24))
            for t in range(NT):
                act.wait_ge(m_max, t + 1)
                for n in range(4 * t, 4 * t + 4):
                    act.activation(t2[:, n * SEQ:(n + 1) * SEQ], bank(0, 4)[:, n * SEQ:(n + 1) * SEQ], ACT.Exp,
                                   bias=stat[:, 3, n:n + 1], scale=stat[:, 2, 16 + n:17 + n],
                                   accum_out=stat[:, 4, n:n + 1]).then_inc(m_exp, 1)
            act.wait_ge(m_turned, 1)
            act.activation(t1[:, 0:D], bank(4, 2), ACT.Copy).then_inc(m_prob_t[0], 1)
            for t in range(NT):
                act.wait_ge(m_out, t + 1)
                act.activation(k_at[:, :, t * P:(t + 1) * P], bank(t).rearrange("p (b t) -> p b t", b=MH),
                               ACT.Copy).then_inc(m_out_ready, 1)
            for n in (24, 25, 26):
                weights_hi(n)
            act.wait_ge(h_ready, 3)
            squares(t1[:, 0:D], h[:, 0, :], 6)
            root(slice(6, 7))
            act.wait_ge(h_ready, 4)
            squares(t1[:, D:2 * D], h[:, 1, :], 7)
            root(slice(7, 8))
            turned_hi(FFN_ROWS, 0, 0)
            turned_hi(FFN_ROWS, 1, 2)
            weights_hi(27)
            for n in range(PEER_UNITS):
                if n < PEER_UNITS - 2:
                    weights_hi(2 * (PEER0 + n) + 4)
                    weights_hi(2 * (PEER0 + n) + 5)
                take_unit(PEER0 + n, q_peert[:, 4 * n:4 * n + 4, :].rearrange("p b t -> p (b t)"), (4 + 2 * n) % 8)
            def high_part(g, s, a, first=False):
                c = g * 4 + s
                if a == 0:
                    act.wait_ge(raw_loaded[s], 16 * (g + 1))
                if not (first and s < 2):
                    act.wait_ge(part_used, 2 * c + (a - 3))
                act.activation(part_hi[:, 2 * (s % 2) + a, :], raw[:, s, a * 512:(a + 1) * 512],
                               ACT.Copy).then_inc(part_hi_ready, 1)

            def gelu(group, s, first=False):
                c = group * 4 + s
                """Of the chunk in bank s; two chunks behind the high parts."""
                act.wait_ge(part_used, 2 * c + 2)
                if not first:
                    act.wait_ge(gelu_stored[s], 16 * group)
                act.activation(gelus[:, s, :], ps[:, s, 0:SEQ], ACT.Gelu).then_inc(gelu_done, 1)

            def gate_rows(n, b):
                act.wait_ge(hots_ready, n + 1)
                for q in range(4):
                    ins = act.activation(hot_i[b][:, q, :], hot_i[b][:, q, :], ACT.Copy,
                                         scale=route_t[:, 2, bass.ds(n * 4 + q, 1)])
                ins.then_inc(gated, 1)

            by_token = big[:].rearrange("p (i t) -> p t i", t=SEQ)

            def take_g(n, b):
                act.wait_ge(g_done, n + 1)
                act.activation(by_token[:, bass.ds(n * 4, 4), :], bank(4 + b).rearrange("p (q i) -> p q i", q=4),
                               ACT.Copy).then_inc(g_taken, 1)

            def u_group(g):
                for s in range(4):
                    high_part(g, s, 0)
                    high_part(g, s, 1)
                    gelu(g + (s // 2 - 1), (s - 2) % 4)

            for s in range(4):
                high_part(0, s, 0, True)
                high_part(0, s, 1, True)
                if s == 1:
                    for t in range(NT):
                        act.wait_ge(key_scores, t + 1)
                        act.activation(scores[:, t * NBLK:(t + 1) * NBLK, :].rearrange("p b n -> p (b n)"), bank(4 * t, 4),
                                       ACT.Copy).then_inc(key_scores_taken, 1)
                    act.wait_ge(h_stored, 16)
                if s >= 2:
                    gelu(0, s - 2, True)
            for s in range(4):
                high_part(1, s, 0)
                high_part(1, s, 1)
                gelu(s // 2, (s - 2) % 4, s < 2)
            with act.Fori(2, G_MATCH + 1) as g:
                u_group(g)
            act.wait_ge(best_centred, 1)
            act.activation(chosen[:, 2 * NT:3 * NT, :], chosen[:, 2 * NT:3 * NT, :], ACT.Exp).then_inc(gates_exp, 1)
            u_group(G_MATCH + 1)
            with act.Fori(G_MATCH + 2, G_BUILD) as g:
                u_group(g)

            def build_pair(g, n, first=False):
                for p in range(16):
                    s = p // 2 % 4
                    high_part(g + p // 8, s, p % 2)
                    if p in PLACES:
                        m = PLACES.index(p)
                        if not (first and m < 2):
                            gate_rows(n + (m - 2), (m - 2) % 4)
                        if not (first and m < 4):
                            take_g(n + (m - 4), m % 4)
                    if p % 2:
                        gelu(g + (p // 8 + s // 2 - 1), (s - 2) % 4)

            build_pair(G_BUILD, 0, True)
            with act.Fori(1, PAIRS) as r:
                build_pair(r * 2 + G_BUILD, r * len(PLACES))
            for p in range(8):
                high_part(GROUPS - 1, p // 2, p % 2)
                if p < 6:
                    gate_rows(QUADS - 6 + p, (p - 2) % 4)
                if p < 7:
                    take_g(QUADS - 8 + p, p % 4)
                if p == 6:
                    take_g(QUADS - 1, 3)
                if p % 2:
                    gelu(GROUPS - 2 + p // 4, (p // 2 - 2) % 4)

            def high_v(g, s, a, first=False):
                c = g * 4 + s
                if a == 0:
                    act.wait_ge(raw_loaded[s], 16 * (g + 1))
                act.wait_ge(part_used, (2 * c - 3 + a if s < 2 else 2 * NKEY) if first else 2 * c + (a - 7))
                act.activation(v_hi[s // 2][:, 2 * (s % 2) + a, :], raw[:, s, a * 512:(a + 1) * 512],
                               ACT.Copy).then_inc(part_hi_ready, 1)

            def high_act(c, b, first=False):
                if not first:
                    act.wait_ge(part_used, 2 * c - 2)
                act.wait_ge(acts_ready, c - (NKEY - 1))
                act.activation(a_hi[:, b, :], big[:, bass.ds((c - NKEY) * SEQ, SEQ)],
                               ACT.Copy).then_inc(a_hi_ready, 1)

            gelu(GROUPS - 1, 2)
            for s in range(4):
                high_v(GROUPS, s, 0, True)
                if s == 1:
                    gelu(GROUPS - 1, 3)
                high_v(GROUPS, s, 1, True)
                if s < 2:
                    high_act(NKEY + s, s, True)
            with act.Fori(GROUPS + 1, 2 * GROUPS) as g:
                for s in range(4):
                    high_v(g, s, 0)
                    high_v(g, s, 1)
                    high_act(g * 4 + (s - 2), s % 2)
            high_act(2 * NKEY - 2, 0)
            high_act(2 * NKEY - 1, 1)

        @block.vector
        def _(dve):
            step = Signal(dve_step)

            def chain(ins):
                dve.wait_ge(dve_step, step.on(ins))

            dve.memset(one[:], 1.0).then_inc(one_ready, 1)
            means = [0]

            def mean(cols, width, sums=0):
                if sums:
                    dve.wait_ge(sumsq, sums)
                means[0] += 1
                dve.tensor_scalar(stat[:, 1, cols], stat[:, 0, cols], 1.0 / width, EPS, ALU.mult,
                                  ALU.add).then_inc(mean_ready, 1)

            def inverse(cols):
                dve.wait_ge(root_ready, means[0])
                chain(dve.reciprocal(stat[:, 2, cols], stat[:, 2, cols]))

            def norm_rows(i, src, t, col):
                if t == 0:
                    dve.wait_ge(gain_loaded[i % 2], 16 * (i // 2 + 1))
                dve.scalar_tensor_tensor(ROWS[i][:, t, :], src[:, t, :], stat[:, 2, col:col + 1], gain_row[i % 2],
                                         ALU.mult, ALU.mult).then_inc(rows_normed, 1)

            def weights_lo(n):
                dve.wait_ge(w_hi_ready, SPLIT.index(n) + 1)
                whole = ring[n % WSLOTS].rearrange("p (k n) -> p k n", k=4)
                dve.tensor_tensor(lo_of(n), whole, hi_of(n).bitcast(F32), ALU.subtract).then_inc(w_lo_ready, 1)

            def turned_lo(i, t, b):
                hi, lo = X_PARTS[i]
                for a in range(2):
                    dve.wait_ge(x_hi_ready, 4 * i + 2 * t + a + 1)
                    at_ = (slice(None), slice(4 * a, 4 * a + 4), slice(t * P, (t + 1) * P))
                    dve.tensor_tensor(lo[at_], bank(b + a).rearrange("p (k t) -> p k t", k=4), hi[at_].bitcast(F32),
                                      ALU.subtract).then_inc(x_lo_ready, 1)

            def sticks_soft(g):
                dve.wait_ge(b_log, g + 1)
                if g:
                    dve.wait_ge(b_summed, g)
                dve.scalar_tensor_tensor(t2[:, 1536:3072], bank(0, 3), 0.0, t2[:, 0:1536], ALU.max,
                                         ALU.add).then_inc(b_soft, 1)

            for t in range(NT):
                mean(slice(t, t + 1), D, t + 1)
                inverse(slice(t, t + 1))
                norm_rows(X_ROWS, h, t, t)
            turned_lo(X_ROWS, 0, 0)
            weights_lo(0)
            turned_lo(X_ROWS, 1, 2)
            weights_lo(1)
            mean(slice(2, 4), D, 4)
            inverse(slice(2, 4))
            for t in range(NT):
                norm_rows(MEM_ROWS, rows2, t, 2 + t)
            weights_lo(2)
            weights_lo(3)

            w = [t1[:, 2048 + n * SEQ:2048 + (n + 1) * SEQ] for n in range(4)]
            dve.wait_ge(loaded_c, 48)
            chain(dve.tensor_copy(posf[:], posi[:]))
            for f in range(HALF):
                ins = dve.memset(freq[:, f:f + 1], float(inv_freq[f]))
                step.on(ins)
            dve.wait_ge(dve_step, step.n)
            for t in range(NT):
                chain(dve.tensor_scalar(w[3][:, t * HALF:(t + 1) * HALF], freq[:], posf[:, t:t + 1], None, ALU.mult))
            a16, n16, m16 = w[3][:, 0:16], w[3][:, 16:32], w[3][:, 32:48]
            for c in range(2):
                chain(dve.tensor_scalar(n16, a16, float(1 / (2 * np.pi)), 0.25 * (1 - c), ALU.mult, ALU.add))
                chain(dve.tensor_scalar(n16, n16, MAGIC, None, ALU.add))
                chain(dve.tensor_scalar(n16, n16, MAGIC, None, ALU.subtract))
                chain(dve.scalar_tensor_tensor(m16, n16, -TWO_PI_PARTS[0], a16, ALU.mult, ALU.add))
                chain(dve.scalar_tensor_tensor(m16, n16, -TWO_PI_PARTS[1], m16, ALU.mult, ALU.add))
                chain(dve.scalar_tensor_tensor(m16, n16, -TWO_PI_PARTS[2], m16, ALU.mult, ALU.add))
                chain(dve.tensor_scalar(m16, m16, float(np.pi / 2) * (1 - c), PI_SAFE, ALU.add, ALU.min))
                ins = dve.tensor_scalar(cossin[:, c].rearrange("p t f -> p (t f)"), m16, -PI_SAFE, None, ALU.max)
                if c:
                    ins.then_inc(angles, 1)
                else:
                    chain(ins)
            weights_lo(4)
            weights_lo(5)
            weights_lo(6)
            dve.wait_ge(w_used, 2 * (K_B + 1))
            dve.tensor_copy(k_bt.rearrange("p b t -> p (b t)"), bank(6, 2)).then_inc(taken[K_B], 1)
            turned_lo(MEM_ROWS, 0, 0)
            turned_lo(MEM_ROWS, 1, 2)
            weights_lo(7)

            dve.wait_ge(masks_ready, 5)
            off_i = untapped.bitcast(I32)
            chain(dve.tensor_copy(w[0], off_i))
            chain(dve.tensor_scalar(taps, w[0], float(TAPS[0][0]), None, ALU.is_le))
            for window, dilation in zip(TAPS[0][1:], TAPS[1][1:]):
                assert window >= SEQ
                chain(dve.tensor_scalar(w[1].bitcast(I32), off_i, dilation - 1, None, ALU.bitwise_and))
                chain(dve.tensor_copy(w[2], w[1].bitcast(I32)))
                chain(dve.scalar_tensor_tensor(taps, w[2], 0.0, taps, ALU.is_equal, ALU.add))
            chain(dve.scalar_tensor_tensor(taps, w[0], 0.0, taps, ALU.is_ge, ALU.mult))
            chain(dve.tensor_scalar(untapped, taps, 0.0, MASKED, ALU.is_equal, ALU.mult))
            weights_lo(8)
            weights_lo(9)
            sticks_soft(0)
            weights_lo(10)

            dve.wait_ge(taken[Q_A], 1)
            dve.wait_ge(taken[K_A], 1)
            flat = qk_a.rearrange("p t w n -> p (t w n)")
            by_head = qk_a.rearrange("p t w (h d) -> p (t w h) d", d=HD)
            sq = t1[:, 0:2048]
            chain(dve.tensor_tensor(sq, flat, flat, ALU.mult))
            weights_lo(11)
            chain(dve.tensor_reduce(stat[:, 0, :], sq.rearrange("p (g d) -> p g d", d=HD), AX, ALU.add))
            mean(slice(0, 32), HD)
            inverse(slice(0, 32))
            chain(dve.tensor_tensor(by_head, by_head, stat[:, 2, :].unsqueeze(2).broadcast_to([P, 32, HD]), ALU.mult))
            weights_lo(12)
            for t in range(NT):
                for w_ in range(2):
                    part = qk_a[:, t, w_, :].rearrange("p (h d) -> p h d", d=HD)
                    ins = dve.tensor_tensor(part, part, hgain[:, w_, :].unsqueeze(1).broadcast_to([P, NH, HD]),
                                            ALU.mult)
                    step.on(ins)
            dve.wait_ge(dve_step, step.n)
            dve.wait_ge(sines, 1)
            for t in range(NT):
                part = qk_a[:, t].rearrange("p w (h d) -> p (w h) d", d=HD)
                x1, x2 = part[:, :, 0:HALF], part[:, :, HALF:ROPE]
                cos = cossin[:, 0, t, :].unsqueeze(1).broadcast_to([P, 2 * NH, HALF])
                sin = cossin[:, 1, t, :].unsqueeze(1).broadcast_to([P, 2 * NH, HALF])
                r = [t1[:, n * 128:(n + 1) * 128].rearrange("p (g f) -> p g f", f=HALF) for n in range(4 * t, 4 * t + 4)]
                for o, a, b in ((r[0], x1, cos), (r[1], x2, sin), (r[2], x2, cos), (r[3], x1, sin)):
                    step.on(dve.tensor_tensor(o, a, b, ALU.mult))
                dve.wait_ge(dve_step, step.n)
                step.on(dve.tensor_tensor(x1, r[0], r[1], ALU.subtract))
                ins = dve.tensor_tensor(x2, r[2], r[3], ALU.add)
            ins.then_inc(qk_normed, 1)
            weights_lo(13)
            sticks_soft(1)
            weights_lo(14)
            dve.wait_ge(w_used, 2 * (V_A + 1))
            dve.tensor_copy(v_a.rearrange("p t n -> p (t n)"), bank(6, 2)).then_inc(taken[V_A], 1)
            weights_lo(15)
            weights_lo(16)
            dve.wait_ge(at_psum, 1)
            dve.tensor_copy(q_at.rearrange("p b t -> p (b t)"), bank(0, 2)).then_inc(q_at_ready, 1)

            parts = [(t2[:, n * 1024:(n + 1) * 1024].rearrange("p (h s) -> p h s", h=(NH, 4, 4)[n]),
                      bank(2 * n, 2).rearrange("p (h s) -> p h s", h=(NH, 4, 4)[n]),
                      (P, 0, 0)[n], ((0, 8), (8, 12), (12, 16))[n]) for n in range(3)]
            for n, (p_, z, s0, (lo_, hi_)) in enumerate(parts):
                dve.wait_ge(a_scores, n + 1)
                chain(dve.tensor_tensor(p_, z, untapped[:, s0:SEQ].unsqueeze(1).broadcast_to([P, hi_ - lo_, SEQ - s0]),
                                        ALU.add))
                chain(dve.tensor_reduce(stat[:, 3, lo_:hi_], p_, AX, ALU.max))
                dve.tensor_scalar(stat[:, 3, lo_:hi_], stat[:, 3, lo_:hi_], -HD ** -0.5, None,
                                  ALU.mult).then_inc(a_max, 1)
            dve.wait_ge(b_out, 1)
            dve.tensor_copy(mixed[:, 0, 512:1024], bank(6)).then_inc(b_taken[0], 1)
            weights_lo(17)
            for n, (p_, z, s0, (lo_, hi_)) in enumerate(parts):
                dve.wait_ge(a_exp, hi_)
                dve.tensor_tensor(p_, p_, taps[:, s0:SEQ].unsqueeze(1).broadcast_to([P, hi_ - lo_, SEQ - s0]),
                                  ALU.mult).then_inc(a_weighted, 1)
            dve.wait_ge(taken[K_MEM], 1)
            by_head = k_mem.rearrange("p t (h d) -> p (t h) d", d=MHD)
            chain(dve.tensor_tensor(sq_mem, k_mem, k_mem, ALU.mult))
            chain(dve.tensor_reduce(stat[:, 0, 8:16], sq_mem.rearrange("p t (h d) -> p (t h) d", d=MHD), AX, ALU.add))
            mean(slice(8, 16), MHD)
            inverse(slice(8, 16))
            dve.tensor_tensor(by_head, by_head, stat[:, 2, 8:16].unsqueeze(2).broadcast_to([P, 8, MHD]),
                              ALU.mult).then_inc(mk_normed, 1)
            mean(slice(0, 2), 512, 6)
            inverse(slice(0, 2))
            dve.wait_ge(gain_loaded[MIXED_ROWS % 2], 16 * (MIXED_ROWS // 2 + 1))
            for t in range(NT):
                part = mixed[:, t, 512:1024]
                step.on(dve.scalar_tensor_tensor(part, part, stat[:, 2, t:t + 1], gain_row[MIXED_ROWS % 2][:, 512:1024],
                                                 ALU.mult, ALU.mult))
            for n, (p_, z, s0, (lo_, hi_)) in enumerate(parts):
                dve.wait_ge(a_weighted, n + 1)
                step.on(dve.tensor_reduce(stat[:, 4, lo_:hi_], p_, AX, ALU.add))
            dve.wait_ge(dve_step, step.n)
            chain(dve.reciprocal(stat[:, 4, 0:16], stat[:, 4, 0:16]))
            for t in range(NT):
                dve.wait_ge(a_out, t + 1)
                for par in range(2):
                    ins = dve.tensor_tensor(
                        mixed[:, t, 0:512].rearrange("p (a r d) -> p a r d", r=2, d=HD)[:, :, par, :],
                        bank(6 + t).rearrange("p (a r d) -> p a r d", r=2, d=HD)[:, :, par, :],
                        stat[:, 4, 8 * t + 4 * par:8 * t + 4 * par + 4].unsqueeze(2).broadcast_to([P, 4, HD]),
                        ALU.mult)
                    if par == 0:
                        step.on(ins)
                ins.then_inc(a_mixed, 1)
                if t == 1:
                    dve.wait_ge(mk_psum, 1)
                    dve.tensor_scalar(k_memt.rearrange("p b t -> p (b t)"), bank(4, 2), gain[:, G_KM:G_KM + 1], None,
                                      ALU.mult).then_inc(mk_ready, 1)
                    turned_lo(MIXED_ROWS, 0, 0)
                mean(slice(2 + t, 3 + t), 512, 7 + t)
                inverse(slice(2 + t, 3 + t))
                dve.wait_ge(a_mixed, t + 1)
                part = mixed[:, t, 0:512]
                dve.scalar_tensor_tensor(part, part, stat[:, 2, 2 + t:3 + t], gain_row[MIXED_ROWS % 2][:, 0:512],
                                         ALU.mult, ALU.mult).then_inc(rows_normed, 1)
                weights_lo(18 + t)
            turned_lo(MIXED_ROWS, 1, 2)

            def add_to_h(t):
                dve.tensor_tensor(h[:, t, :], h[:, t, :], bank(4 + 2 * t, 2), ALU.add).then_inc(h_ready, 1)

            dve.wait_ge(out_projected, 1)
            add_to_h(0)
            mean(slice(4, 5), D, 9)
            inverse(slice(4, 5))
            norm_rows(QUERY_ROWS, h, 0, 4)
            weights_lo(20)
            dve.wait_ge(w_used, 2 * (OUT1 + 1))
            add_to_h(1)
            turned_lo(QUERY_ROWS, 0, 0)
            weights_lo(21)
            mean(slice(5, 6), D, 10)
            inverse(slice(5, 6))
            norm_rows(QUERY_ROWS, h, 1, 5)
            turned_lo(QUERY_ROWS, 1, 2)

            def query_scale(t):
                cols4 = slice(16 + 4 * t, 20 + 4 * t)
                dve.wait_ge(mq_taken, t + 1)
                chain(dve.tensor_tensor(sq_mem[:, t, :], q_mem[:, t, :], q_mem[:, t, :], ALU.mult))
                chain(dve.tensor_reduce(stat[:, 0, cols4], sq_mem[:, t, :].rearrange("p (h d) -> p h d", d=MHD), AX,
                                        ALU.add))
                mean(cols4, MHD)
                inverse(cols4)
                chain(dve.tensor_scalar(stat[:, 2, cols4], stat[:, 2, cols4], MHD ** -0.5, None, ALU.mult))

            def take_queries(t):
                dve.wait_ge(mq_psum, t + 1)
                dve.tensor_scalar(q_at[:, :, t * P:(t + 1) * P], bank(5 + 2 * t).rearrange("p (b t) -> p b t", b=MH),
                                  gain[:, G_QM:G_QM + 1], None, ALU.mult).then_inc(mq_ready, 1)

            def greatest(t):
                four = slice(4 * t, 4 * t + 4)
                dve.wait_ge(m_scores, t + 1)
                chain(dve.tensor_reduce(stat[:, 3, four], bank(2 * t, 2).rearrange("p (g m) -> p g m", g=4), AX, ALU.max))
                dve.scalar_tensor_tensor(stat[:, 3, four], stat[:, 3, four], -1.0, stat[:, 2, 16 + 4 * t:20 + 4 * t],
                                         ALU.mult, ALU.mult).then_inc(m_max, 1)

            query_scale(0)
            take_queries(0)
            query_scale(1)
            greatest(0)
            take_queries(1)
            greatest(1)
            for t in range(NT):
                four = slice(4 * t, 4 * t + 4)
                dve.wait_ge(m_exp, 4 * t + 4)
                chain(dve.reciprocal(stat[:, 4, four], stat[:, 4, four]))
                part = t2[:, t * D:(t + 1) * D].rearrange("p (g m) -> p g m", g=4)
                dve.tensor_tensor(part, part, stat[:, 4, four].unsqueeze(2).broadcast_to([P, 4, SEQ]),
                                  ALU.mult).then_inc(m_weighted, 1)
            dve.wait_ge(m_turned, 2)
            dve.tensor_copy(t1[:, D:2 * D], bank(6, 2)).then_inc(m_prob_t[1], 1)
            for n in (24, 25, 26):
                weights_lo(n)
            dve.wait_ge(o_projected, 1)
            add_to_h(0)
            mean(slice(6, 7), D, 11)
            inverse(slice(6, 7))
            norm_rows(FFN_ROWS, h, 0, 6)
            dve.wait_ge(w_used, 2 * (O_MEM + 1))
            add_to_h(1)
            mean(slice(7, 8), D, 12)
            inverse(slice(7, 8))
            norm_rows(FFN_ROWS, h, 1, 7)
            turned_lo(FFN_ROWS, 0, 0)
            turned_lo(FFN_ROWS, 1, 2)
            weights_lo(27)
            for n in range(28, KEYS_HALF):
                weights_lo(n)

            def low_part(c, s, a):
                part = 2 * (s % 2) + a
                dve.wait_ge(part_hi_ready, 2 * c + (a + 1))
                dve.tensor_tensor(part_lo[:, part, :], raw[:, s, a * 512:(a + 1) * 512],
                                  part_hi[:, part, :].bitcast(F32), ALU.subtract).then_inc(part_lo_ready, 1)

            def beside(g, steps):
                done = 0
                for n in range(8):
                    low_part(g * 4 + n // 2, n // 2, n % 2)
                    upto = len(steps) * (n + 1) // 8
                    for emit in steps[done:upto]:
                        emit()
                    done = upto

            def top_list(b, n):
                val, pos_, row = (x[:, b, :] for x in (top_val, top_pos, scores))

                def link(k, ins):
                    ins.then_inc(top_step, 1)
                    dve.wait_ge(top_step, b * 5 + k)

                def first():
                    if b % NBLK == 0:
                        dve.wait_ge(key_scores_taken, b // NBLK + 1)
                    link(1, dve.max(val[:, 0:8], row))

                return [first,
                        lambda: link(2, dve.max_index(pos_[:, 0:8], val[:, 0:8], row)),
                        lambda: link(3, dve.match_replace(row, val[:, 0:8], row, LOWEST)),
                        lambda: link(4, dve.max(val[:, 8:16], row)),
                        lambda: link(5, dve.max_index(pos_[:, 8:16], val[:, 8:16], row))]

            for g in range(TOP_GROUPS):
                beside(g, [f for n in range(4) for f in top_list(g * 4 + n, n)])

            def candidates(dst, src):
                pair = src.rearrange("p (h w) k -> p h w k", w=2)
                c, emits = 0, []
                for a, n in enumerate(CAND):
                    if n == 1:
                        break
                    emits.append(lambda a=a, n=n, c=c: step.on(dve.tensor_tensor(
                        dst[:, :, c:c + n], pair[:, :, 0, a:a + 1].broadcast_to([P, NT * PH, n]),
                        pair[:, :, 1, 0:n], ALU.add)))
                    c += n
                emits.append(lambda: step.on(dve.tensor_tensor(
                    dst[:, :, c:NCAND], pair[:, :, 0, a:TOPK],
                    pair[:, :, 1, 0:1].broadcast_to([P, NT * PH, TOPK - a]), ALU.add)))
                return emits

            highs = top_id.rearrange("p (h w) k -> p h w k", w=2)[:, :, 0, :]
            beside(G_CAND, [lambda: chain(dve.tensor_copy(top_id, top_pos)),
                            lambda: chain(dve.tensor_scalar(highs, highs, float(NKEY), None, ALU.mult))]
                   + candidates(cand_val, top_val) + candidates(cand_id, top_id))
            dve.wait_ge(dve_step, step.n)

            def best_list(m):
                val, pos_, row = (x[:, m, :] for x in (best, best_pos, cand_val))

                def link(k, ins):
                    ins.then_inc(best_step, 1)
                    dve.wait_ge(best_step, m * 5 + k)

                return [lambda: link(1, dve.max(val[:, 0:8], row)),
                        lambda: link(2, dve.max_index(pos_[:, 0:8], val[:, 0:8], row)),
                        lambda: link(3, dve.match_replace(row, val[:, 0:8], row, LOWEST)),
                        lambda: link(4, dve.max(val[:, 8:16], row)),
                        lambda: link(5, dve.max_index(pos_[:, 8:16], val[:, 8:16], row))]

            for g in range(BEST_GROUPS):
                beside(g + G_BEST, [f for n in range(8) for f in best_list(g * 8 + n)])
            gate = chosen[:, 2 * NT:3 * NT, :].rearrange("p t (h k) -> p (t h) k", k=TOPK)
            dve.tensor_tensor(gate, best, best[:, :, 0:1].broadcast_to([P, NT * PH, TOPK]),
                              ALU.subtract).then_inc(best_centred, 1)
            dve.tensor_copy(best_at, best_pos).then_inc(at_ready, 1)
            dve.wait_ge(at_ready, 1)

            def match_list(g, n):
                at_, got = (x[:, bass.ds(g * 2 + n, 1), :].rearrange("p h k -> p (h k)") for x in (best_at, expert))

                def compare():
                    dve.tensor_tensor(match[:, n], iota_cand[:].unsqueeze(1).broadcast_to([P, TOPK, NCAND]),
                                      at_.unsqueeze(2).broadcast_to([P, TOPK, NCAND]), ALU.is_equal).then_inc(matched, 1)

                def gather():
                    dve.wait_ge(match_ids, g * 2 + (n + 1))
                    dve.tensor_reduce(got, match[:, n], AX, ALU.add).then_inc(match_summed, 1)

                return compare, gather

            def match_group(g):
                (compare0, gather0), (compare1, gather1) = match_list(g, 0), match_list(g, 1)
                beside(g + G_MATCH, [compare0, compare1, lambda: None, lambda: None, gather0, lambda: None, gather1,
                                     lambda: None])

            match_group(0)
            with dve.Fori(1, MATCH_GROUPS) as g:
                dve.wait_ge(match_summed, g * 2)
                match_group(g)
            dve.wait_ge(match_summed, 2 * MATCH_GROUPS)

            total = stat[:, 0, 0:NT * PH]

            def end_of_routing():
                dve.wait_ge(gates_exp, 1)
                chain(dve.tensor_reduce(total, gate, AX, ALU.add))

            beside(G_GATES, [
                lambda: chain(dve.tensor_copy(expert_i, expert.rearrange("p h k -> p (h k)"))),
                lambda: step.on(dve.tensor_scalar(digit[:, 0:2 * P], expert_i, 7, None, ALU.arith_shift_right)),
                lambda: chain(dve.tensor_scalar(digit[:, 2 * P:4 * P], expert_i, NKEY - 1, None, ALU.bitwise_and)),
                lambda: chain(dve.tensor_copy(chosen[:, 0:2 * NT, :].rearrange("p n k -> p (n k)"), digit)),
                end_of_routing,
                lambda: chain(dve.reciprocal(total, total)),
                lambda: dve.tensor_tensor(gate, gate, total.unsqueeze(2).broadcast_to([P, NT * PH, TOPK]),
                                          ALU.mult).then_inc(routed, 1),
                lambda: None])
            def take_route():
                dve.wait_ge(route_psum, 1)
                dve.tensor_copy(route_t.rearrange("p n t -> p (n t)"), bank(6, 2)[:, 0:3 * SEQ]).then_inc(route_ready, 1)

            beside(G_ROUTE, [lambda: None] * 7 + [take_route])
            dve.wait_ge(route_ready, 1)

            def hot_rows(n, b, first=False):
                if not first:
                    dve.wait_ge(g_done, n - 3)
                for w, rows in ((1, hot_j[:, b]), (0, hot_i[b])):
                    ins = dve.tensor_tensor(rows, iota_key[:].unsqueeze(1).broadcast_to([P, 4, P]),
                                            route_t[:, w, bass.ds(n * 4, 4)].unsqueeze(2).broadcast_to([P, 4, P]),
                                            ALU.is_equal)
                ins.then_inc(hots_ready, 1)

            def build_pair(g, n, first=False):
                for p in range(16):
                    low_part((g + p // 8) * 4 + p // 2 % 4, p // 2 % 4, p % 2)
                    if p in PLACES:
                        m = PLACES.index(p)
                        hot_rows(n + m, m % 4, first and m < 4)

            dve.wait_ge(h_stored, 16)
            build_pair(G_BUILD, 0, True)
            with dve.Fori(1, PAIRS) as r:
                build_pair(r * 2 + G_BUILD, r * len(PLACES))
            for p in range(8):
                low_part(NKEY - 4 + p // 2, p // 2, p % 2)
                if p < 4:
                    hot_rows(QUADS - 4 + p, p)

            def multiply(g, s, first=False):
                c = g * 4 + s
                if first:
                    dve.wait_ge(first_gelus_loaded[g - GROUPS], 16)
                else:
                    dve.wait_ge(gelu_loaded[s], 16 * (g - (GROUPS + 1)))
                part = big[:, bass.ds((c - NKEY) * SEQ, SEQ)]
                dve.tensor_tensor(part, part, first_gelus[:, g - GROUPS, s, :] if first else gelus[:, s, :], ALU.mult).then_inc(acts_ready, 1)

            def low_v(g, s):
                for a in range(2):
                    part = 2 * (s % 2) + a
                    dve.wait_ge(part_hi_ready, 2 * (g * 4 + s) + (a + 1))
                    dve.tensor_tensor(v_lo[s // 2][:, part, :], raw[:, s, a * 512:(a + 1) * 512],
                                      v_hi[s // 2][:, part, :].bitcast(F32), ALU.subtract).then_inc(part_lo_ready, 1)

            def low_act(c, b):
                dve.wait_ge(a_hi_ready, c - (NKEY - 1))
                dve.tensor_tensor(a_lo[:, b, :], big[:, bass.ds((c - NKEY) * SEQ, SEQ)],
                                  a_hi[:, b, :].bitcast(F32), ALU.subtract).then_inc(a_lo_ready, 1)

            dve.wait_ge(g_taken, QUADS)
            for s in range(4):
                multiply(GROUPS, s, True)
                low_v(GROUPS, s)
                if s < 2:
                    low_act(NKEY + s, s)
            for s in range(4):
                multiply(GROUPS + 1, s, True)
                low_v(GROUPS + 1, s)
                low_act((GROUPS + 1) * 4 + s - 2, s % 2)
            with dve.Fori(GROUPS + 2, 2 * GROUPS) as g:
                for s in range(4):
                    multiply(g, s)
                    low_v(g, s)
                    low_act(g * 4 + (s - 2), s % 2)
            low_act(2 * NKEY - 2, 0)
            low_act(2 * NKEY - 1, 1)
            dve.wait_ge(part_used, 4 * NKEY)
            dve.wait_ge(h_back_loaded, 16)
            dve.tensor_tensor(h_back, h_back, bank(0, 4), ALU.add).then_inc(out_ready, 1)


def kernel(x, mem, positions, norm_mix_g, w_in, qnorm_g_dil, knorm_g_dil, out_norm_g_dil, out_norm_g_sb, w_out,
           norm_mem_g, norm_memtok_g, w_q_mem, w_kv_mem, qnorm_g_mem, knorm_g_mem, w_o_mem, norm_ffn_g, w_q_peer,
           peer_sub_keys, peer_u, peer_v):
    import concourse.bacc as bacc
    from concourse.bass_utils import run_bass_kernel_spmd

    def blocks(w, n):
        k, c = w.shape[0] // P, w.shape[1] // n
        return np.ascontiguousarray(w.reshape(k, P, n, c).transpose(2, 1, 0, 3))

    def halves(units):
        n, p, k, c = units.shape
        return units.reshape(n, p, 2, k // 2, c).transpose(0, 2, 1, 3, 4).reshape(2 * n, p, k * c // 2)

    w_in, w_out, w_q_peer = np.asarray(w_in)[0], np.asarray(w_out)[0], np.asarray(w_q_peer)[0]
    w_kv = np.asarray(w_kv_mem)[0]
    mix = blocks(w_in, 6)
    keys = np.asarray(peer_sub_keys)[0].reshape(NBLK, NKEY, P).transpose(2, 0, 1).reshape(1, P, WHALF)
    weights = np.concatenate(
        [halves(mix[[3, 4, 0, 1, 5, 2]]), halves(blocks(w_kv, 2)), halves(blocks(w_out, 2)),
         halves(blocks(np.asarray(w_q_mem)[0], 1)), halves(blocks(np.asarray(w_o_mem)[0], 1)),
         halves(blocks(w_q_peer, PEER_UNITS)), keys], axis=0)
    row_gains = np.stack([np.asarray(norm_mix_g)[0], np.asarray(norm_memtok_g)[0],
                          np.concatenate([np.asarray(out_norm_g_dil)[0], np.asarray(out_norm_g_sb)[0]]),
                          np.asarray(norm_mem_g)[0], np.asarray(norm_ffn_g)[0]])
    cols = np.ascontiguousarray(np.stack([np.asarray(qnorm_g_mem)[0], np.asarray(knorm_g_mem)[0]], axis=1))
    head_gains = np.concatenate([np.asarray(qnorm_g_dil), np.asarray(knorm_g_dil)], axis=0)
    u_t = np.ascontiguousarray(np.asarray(peer_u)[0].reshape(NKEY, NKEY, KD, P).transpose(0, 3, 2, 1)).reshape(NKEY, P, D)
    v_t = np.asarray(peer_v)[0].reshape(NKEY, P, D)
    pos = np.ascontiguousarray(np.asarray(positions).reshape(NT, P).T)
    arrays = {"x": np.asarray(x)[0], "mem": np.asarray(mem)[0], "pos": pos, "weights": weights, "row_gains": row_gains, "cols": cols,
              "head_gains": head_gains, "u_t": u_t, "v_t": v_t}
    nc = bacc.Bacc("TRN2", target_bir_lowering=False, num_devices=1)
    args = [nc.dram_tensor(n, a.shape, mybir.dt.from_np(a.dtype), kind="ExternalInput").ap() for n, a in arrays.items()]
    out = nc.dram_tensor("out", (SEQ, D), F32, kind="ExternalOutput").ap()
    h_kept = nc.dram_tensor("h_kept", (P, NT * D), F32).ap()
    gelu_kept = nc.dram_tensor("gelu_kept", (NKEY, P, SEQ), F32).ap()
    hybrid_layer(nc, *args, out, h_kept, gelu_kept)
    r = run_bass_kernel_spmd(nc, [arrays], core_ids=[0])
    return r.results[0]["out"].reshape(1, SEQ, D)
```

```python
from contextlib import ExitStack

import numpy as np
import concourse.bass as bass
import concourse.mybir as mybir

F32 = mybir.dt.float32
F32R = mybir.dt.float32r
I32 = mybir.dt.int32
U32 = mybir.dt.uint32
ALU = mybir.AluOpType
ACT = mybir.ActivationFunctionType
AX = mybir.AxisListType.X

P = 128
D = 1024
SEQ = 256
NT = SEQ // P
KD = D // P
HD = 64
NH = 8
ROPE = HD // 4
HALF = ROPE // 2
MH, MHD = 4, 128
PH, TOPK = 8, 16
NKEY = 128
NBLK = 2 * PH
EPS = 1e-6
CAND = [TOPK // (a + 1) for a in range(TOPK)]
NCAND = sum(CAND)
TAPS = (128, 512, 2048), (1, 4, 16)
WSLOTS = 5
WHALF = 2048
HI_SLOTS = 4
(Q_B, K_B, Q_A, K_A, V_B, V_A, K_MEM, OUT0, OUT1, Q_MEM, V_MEM, O_MEM, PEER0) = range(13)
PEER_UNITS = 4
KEYS_HALF = 2 * (PEER0 + PEER_UNITS)
(X_ROWS, MEM_ROWS, MIXED_ROWS, QUERY_ROWS, FFN_ROWS) = range(5)
GROUPS = NKEY // 4
TOP_PAIRS = (4, 3, 3, 3, 3)
BEST_PAIRS = (2, 3, 3)
MATCH_ROUNDS = 4
G_CAND = len(TOP_PAIRS)
G_MATCH = G_CAND + len(BEST_PAIRS)
G_GATES = G_MATCH + 3 * MATCH_ROUNDS
G_BUILD = G_GATES + 1
QUADS = SEQ // 4
PAIRS = (GROUPS - 1 - G_BUILD) // 2
PLACES = [p for p in range(16) if p % 4 != 3]
assert 2 * sum(TOP_PAIRS) == NT * NBLK and 2 * sum(BEST_PAIRS) == NT * PH == 4 * MATCH_ROUNDS
assert G_BUILD + 2 * PAIRS + 1 == GROUPS and PAIRS * len(PLACES) + 4 == QUADS
LOWEST = -3.0e38
MASKED = -1.0e30
TWO_PI_PARTS = (6.28125, 0.0019340515136718750, float(2 * np.pi - 6.28125 - 0.0019340515136718750))
MAGIC = 1.5 * 2.0 ** 23
PI_SAFE = 3.1415925


class Signal:

    def __init__(self, sem):
        self.sem, self.n = sem, 0

    def on(self, ins, by=1):
        ins.then_inc(self.sem, by)
        self.n += by
        return self.n


def hybrid_layer(nc, x, mem, pos, weights, row_gains, cols, head_gains, u_t, v_t, out, h_kept, gelu_kept):
    inv_freq = np.float32(500000.0) ** (-np.arange(0, ROPE, 2, dtype=np.float32) / np.float32(ROPE))
    with ExitStack() as ctx:
        def sb(name, shape, dt=F32):
            return ctx.enter_context(nc.sbuf_tensor(name, shape, dt))

        def sem(name):
            return ctx.enter_context(nc.semaphore(name))

        def room_twice(name, shape, parts):
            typed, end = [], 0
            with ExitStack() as room:
                for part, first, n in parts:
                    if first > end:
                        room.enter_context(nc.sbuf_tensor(f"before_{part}", [P, first - end], F32))
                    typed.append(room.enter_context(nc.sbuf_tensor(part, [P, n], F32R)))
                    end = first + n
            return sb(name, shape), typed

        S0 = WSLOTS * WHALF
        big, (*ring_lo, mem_hi, mem_lo, hi_slot) = room_twice(
            "big", [P, NKEY * SEQ],
            [(f"ring_lo{s}", s * WHALF, WHALF) for s in range(WSLOTS)]
            + [("mem_hi", S0, 2048), ("mem_lo", S0 + 2048, 2048), ("hi_slot", NKEY * SEQ - WHALF, WHALF)])
        ring = [big[:, s * WHALF:(s + 1) * WHALF] for s in range(WSLOTS)]

        def scratch(at, n):
            return big[:, S0 + at:S0 + at + n]

        mem_hi = mem_hi[:].rearrange("p (k t) -> p k t", k=KD)
        mem_lo = mem_lo[:].rearrange("p (k t) -> p k t", k=KD)
        mixed = scratch(4096, 2048).rearrange("p (t n) -> p t n", t=NT)
        qk_a = scratch(4096, 2048).rearrange("p (t w n) -> p t w n", t=NT, w=2)
        q_at = scratch(6144, 1024).rearrange("p (b t) -> p b t", b=4)
        k_at = scratch(7168, 1024).rearrange("p (b t) -> p b t", b=4)
        q_bt = scratch(8192, 1024).rearrange("p (b t) -> p b t", b=4)
        k_bt = scratch(9216, 1024).rearrange("p (b t) -> p b t", b=4)
        q_mem = scratch(8192, 1024).rearrange("p (t n) -> p t n", t=NT)
        sq_mem = scratch(9216, 1024).rearrange("p (t n) -> p t n", t=NT)
        v_a = scratch(10240, 1024).rearrange("p (t n) -> p t n", t=NT)
        v_b = scratch(11264, 1024).rearrange("p (t n) -> p t n", t=NT)
        k_mem = scratch(12288, 1024).rearrange("p (t n) -> p t n", t=NT)
        v_mem = scratch(13312, 1024).rearrange("p (t n) -> p t n", t=NT)
        k_memt = scratch(14336, 1024).rearrange("p (b t) -> p b t", b=4)
        sticks = scratch(15360, 3072).rearrange("p (h c) -> p h c", h=NH)
        taps = scratch(18432, SEQ)
        untapped = scratch(18688, SEQ)
        tri_neg = scratch(18944, P)
        ones_neg = scratch(19072, P)
        hgain = scratch(19200, 2 * HD).rearrange("p (w d) -> p w d", w=2)
        gain_row0 = scratch(19328, D)
        q_peert = scratch(2048, 4096).rearrange("p (b t) -> p b t", b=NBLK)

        at = [NKEY * SEQ]

        def tail(n):
            at[0] -= n
            return big[:, at[0]:at[0] + n]

        scores = tail(4096).rearrange("p (b n) -> p b n", b=NT * NBLK)
        top_val = tail(512).rearrange("p (b k) -> p b k", b=NT * NBLK)
        top_pos = tail(512).bitcast(U32).rearrange("p (b k) -> p b k", b=NT * NBLK)
        top_id = tail(512).rearrange("p (b k) -> p b k", b=NT * NBLK)
        cand_val = tail(NT * PH * NCAND).rearrange("p (h c) -> p h c", c=NCAND)
        cand_id = tail(NT * PH * NCAND).rearrange("p (h c) -> p h c", c=NCAND)
        best = tail(2 * P).rearrange("p (h k) -> p h k", k=TOPK)
        best_pos = tail(2 * P).bitcast(U32).rearrange("p (h k) -> p h k", k=TOPK)
        best_at = tail(2 * P).rearrange("p (h k) -> p h k", k=TOPK)
        expert = tail(2 * P).rearrange("p (h k) -> p h k", k=TOPK)
        expert_i = tail(2 * P).bitcast(I32)
        digit = tail(4 * P).bitcast(I32)
        chosen = tail(6 * P).rearrange("p (n k) -> p n k", n=6)
        match = tail(TOPK * NCAND).rearrange("p (k c) -> p k c", k=TOPK)

        h = sb("h", [P, NT, D])
        tmp = sb("tmp", [P, 6144])
        t1, t2 = tmp[:, 0:3072], tmp[:, 3072:6144]
        raw = tmp[:, 0:4096].rearrange("p (s n) -> p s n", s=4)
        h_room = h[:].rearrange("p t n -> p (t n)")
        gelus = h_room[:, 0:1024].rearrange("p (s t) -> p s t", s=4)
        hot_i = [part[:, n * 512:(n + 1) * 512].rearrange("p (q n) -> p q n", q=4)
                 for part in (h_room[:, 1024:2048], tmp[:, 4096:5120]) for n in range(2)]
        hot_j, (hot_j_parts,) = room_twice("hot_j", [P, 4, 4, P], [("hot_j_parts", 0, WHALF)])
        h_back = hot_j[:].rearrange("p b q n -> p (b q n)")
        first_gelus = h_back.rearrange("p (g s t) -> p g s t", g=2, s=4)
        route_t = tmp[:, 5376:6144].rearrange("p (n t) -> p n t", n=3)
        part_hi = sb("part_hi", [P, 4, 512], F32R)
        part_lo = sb("part_lo", [P, 4, 512], F32R)
        x_hi = sb("x_hi", [P, KD, SEQ], F32R)
        x_lo = sb("x_lo", [P, KD, SEQ], F32R)
        v_hi = [part_hi, x_hi[:].rearrange("p (m k) t -> p m (k t)", m=4)]
        v_lo = [part_lo, x_lo[:].rearrange("p (m k) t -> p m (k t)", m=4)]
        acts_room, (acts_split,) = room_twice("acts_room", [P, 4, SEQ], [("acts_split", 0, 4 * SEQ)])
        a_hi, a_lo = (acts_split[:, w * 2 * SEQ:(w + 1) * 2 * SEQ].rearrange("p (b t) -> p b t", b=2) for w in range(2))
        gain_row = [gain_row0, acts_room[:].rearrange("p b t -> p (b t)")]
        hi_slots = [part_hi[:], part_lo[:], hot_j_parts[:].rearrange("p (k n) -> p k n", k=4),
                    hi_slot[:].rearrange("p (k n) -> p k n", k=4)]
        ident = sb("ident", [P, P])
        iota_key = sb("iota_key", [P, P])
        iota_cand = sb("iota_cand", [P, NCAND])
        gain = sb("gain", [P, 2])
        posi = sb("posi", [P, NT], I32)
        posf = sb("posf", [P, NT])
        freq = sb("freq", [P, HALF])
        cossin = sb("cossin", [P, 2, NT, HALF])
        one = sb("one", [P, 1])
        stat = sb("stat", [P, 5, 32])
        ps = ctx.enter_context(nc.psum_tensor("ps", [P, 8, 512], F32))

        def bank(b, n=1):
            return ps[:, b:b + n, :].rearrange("p b n -> p (b n)")

        loaded_x = [sem(f"loaded_x{t}") for t in range(NT)]
        loaded_mem, loaded_c = sem("loaded_mem"), sem("loaded_c")
        gain_loaded = [sem("gain_loaded0"), sem("gain_loaded1")]
        w_loaded = [sem(f"w_loaded{s}") for s in range(WSLOTS)]
        w_hi_ready, w_lo_ready = sem("w_hi_ready"), sem("w_lo_ready")
        w_used = sem("w_used")
        ident_ready, masks_ready = sem("ident_ready"), sem("masks_ready")
        pool_step, one_ready = sem("pool_step"), sem("one_ready")
        sumsq, mean_ready, root_ready = sem("sumsq"), sem("mean_ready"), sem("root_ready")
        rows_normed, x_psum = sem("rows_normed"), sem("x_psum")
        x_hi_ready, x_lo_ready = sem("x_hi_ready"), sem("x_lo_ready")
        b_taken = [sem(f"b_taken{t}") for t in range(NT)]
        a_mixed, out_projected, h_ready = sem("a_mixed"), sem("out_projected"), sem("h_ready")
        taken = [sem(f"taken{u}") for u in range(PEER0 + PEER_UNITS)]
        qk_normed, at_psum, q_at_ready, k_at_ready = (
            sem("qk_normed"), sem("at_psum"), sem("q_at_ready"), sem("k_at_ready"))
        a_scores, a_max, a_exp, a_weighted, a_turned, a_out = (
            sem("a_scores"), sem("a_max"), sem("a_exp"), sem("a_weighted"), sem("a_turned"), sem("a_out"))
        a_prob_t = sem("a_prob_t")
        b_scores, b_log, b_soft, b_soft_masked, b_summed, b_stick, b_stick_masked, b_out = (
            sem("b_scores"), sem("b_log"), sem("b_soft"), sem("b_soft_masked"), sem("b_summed"),
            sem("b_stick"), sem("b_stick_masked"), sem("b_out"))
        b_evens = sem("b_evens")
        mk_normed, mk_psum, mk_ready = sem("mk_normed"), sem("mk_psum"), sem("mk_ready")
        mq_projected, mq_taken = sem("mq_projected"), sem("mq_taken")
        mq_psum, mq_ready = sem("mq_psum"), sem("mq_ready")
        m_scores, m_max, m_exp, m_weighted, m_turned, m_out, m_out_hi, m_out_lo, o_projected = (
            sem("m_scores"), sem("m_max"), sem("m_exp"), sem("m_weighted"), sem("m_turned"),
            sem("m_out"), sem("m_out_hi"), sem("m_out_lo"), sem("o_projected"))
        m_prob_t = [sem(f"m_prob_t{t}") for t in range(NT)]
        angles, sines = sem("angles"), sem("sines")
        key_scores, key_scores_taken = sem("key_scores"), sem("key_scores_taken")
        best_centred, gates_exp = sem("best_centred"), sem("gates_exp")
        routed, route_psum, route_ready = sem("routed"), sem("route_psum"), sem("route_ready")
        raw_loaded = [sem(f"raw_loaded{s}") for s in range(4)]
        part_hi_ready, part_lo_ready, part_used = sem("part_hi_ready"), sem("part_lo_ready"), sem("part_used")
        gelu_done = sem("gelu_done")
        hots_ready, gated = sem("hots_ready"), sem("gated")
        g_done, g_taken, acts_ready = sem("g_done"), sem("g_taken"), sem("acts_ready")
        h_stored, h_back_loaded = sem("h_stored"), sem("h_back_loaded")
        gelu_stored = [sem(f"gelu_stored{s}") for s in range(4)]
        first_gelus_loaded = [sem("first_gelus_loaded0"), sem("first_gelus_loaded1")]
        gelu_loaded = [sem(f"gelu_loaded{s}") for s in range(4)]
        a_hi_ready, a_lo_ready = sem("a_hi_ready"), sem("a_lo_ready")
        top_step, best_step, match_step = sem("top_step"), sem("best_step"), sem("match_step")
        out_ready, stored = sem("out_ready"), sem("stored")
        dve_step, act_step = sem("dve_step"), sem("act_step")

        block = ctx.enter_context(nc.Block())

        G_QM, G_KM = 0, 1
        rows1, rows2 = (part[:, 0:2048].rearrange("p (t n) -> p t n", t=NT) for part in (t1, t2))
        ROWS = rows1, rows2, mixed, rows1, rows1
        o_hi, o_lo = mem_hi, mem_lo
        X_PARTS = (x_hi, x_lo), (mem_hi, mem_lo), (x_hi, x_lo), (x_hi, x_lo), (x_hi, x_lo)

        def hi_of(n):
            return hi_slots[n % HI_SLOTS]

        def lo_of(n):
            return ring_lo[n % WSLOTS][:].rearrange("p (k n) -> p k n", k=4)

        def hi_free(n):
            return max(n - HI_SLOTS + 1, 0)

        @block.sync
        def _(sp):
            def load_weights(first, last):
                for n in range(first, last + 1):
                    if n >= WSLOTS:
                        sp.wait_ge(w_used, n - WSLOTS + 1)
                    sp.dma_start(ring[n % WSLOTS], weights[n]).then_inc(w_loaded[n % WSLOTS], 16)

            def load_gain(i):
                if i >= 2:
                    sp.wait_ge(rows_normed, 2 * (i - 1))
                sp.dma_start(gain_row[i % 2], row_gains[i:i + 1].partition_broadcast(P)).then_inc(gain_loaded[i % 2], 16)

            sp.dma_start(h[:, 0, :], x[0:P]).then_inc(loaded_x[0], 16)
            load_gain(X_ROWS)
            sp.dma_start(h[:, 1, :], x[P:SEQ]).then_inc(loaded_x[1], 16)
            load_weights(0, 1)
            sp.dma_start(rows2, mem.rearrange("(t p) n -> p t n", p=P)).then_inc(loaded_mem, 16)
            load_gain(MEM_ROWS)
            load_weights(2, 3)
            sp.dma_start(gain[:], cols).then_inc(loaded_c, 16)
            sp.dma_start(hgain, head_gains.partition_broadcast(P)).then_inc(loaded_c, 16)
            sp.dma_start(posi[:], pos).then_inc(loaded_c, 16)
            load_weights(4, 9)
            load_gain(MIXED_ROWS)
            load_weights(10, 12)
            load_gain(QUERY_ROWS)
            load_weights(13, 21)
            load_gain(FFN_ROWS)
            load_weights(22, KEYS_HALF)

            sp.wait_ge(x_psum, 4 * (FFN_ROWS + 1))
            for s in range(4):
                sp.dma_start(raw[:, s, :], u_t[s]).then_inc(raw_loaded[s], 16)
            sp.wait_ge(h_ready, 4)
            sp.wait_ge(rows_normed, 2 * (FFN_ROWS + 1))
            sp.dma_start(h_kept, h_room).then_inc(h_stored, 16)

            def load(table, g, s, chunk):
                sp.wait_ge(part_lo_ready, g * 8 + 2 * (s - 3))
                sp.dma_start(raw[:, s, :], table[chunk]).then_inc(raw_loaded[s], 16)

            def store_gelu(i, s):
                sp.wait_ge(gelu_done, i + 1)
                sp.dma_start(gelu_kept[i], gelus[:, s, :]).then_inc(gelu_stored[s], 16)

            def load_first_gelus(g):
                for s in range(4):
                    sp.wait_ge(gelu_stored[s], 16 * (g + 1))
                sp.dma_start(first_gelus[:, g], gelu_kept[4 * g:4 * g + 4].rearrange(
                    "s p t -> p s t")).then_inc(first_gelus_loaded[g], 16)

            for g in (1, 2):
                for s in range(4):
                    load(u_t, g, s, g * 4 + s)
                    if g * 4 + s >= 6:
                        store_gelu(g * 4 + s - 6, (s + 2) % 4)
            with sp.Fori(3, GROUPS) as g:
                for s in range(4):
                    load(u_t, g, s, g * 4 + s)
                    store_gelu(g * 4 + (s - 6), (s + 2) % 4)
            for s in range(4):
                load(v_t, GROUPS, s, s)
                store_gelu(NKEY + s - 6, (s + 2) % 4)
                if s == 1:
                    sp.wait_ge(g_done, QUADS)
                    load_first_gelus(0)
            for s in range(4):
                if s >= 2:
                    store_gelu(NKEY - 4 + s, s)
                load(v_t, GROUPS + 1, s, s + 4)
                if s == 1:
                    load_first_gelus(1)
            for s in range(4):
                sp.wait_ge(gelu_stored[s], 16 * GROUPS)
            with sp.Fori(GROUPS + 2, 2 * GROUPS) as g:
                for s in range(4):
                    load(v_t, g, s, g * 4 + (s - NKEY))
                    sp.wait_ge(acts_ready, g * 4 + (s - NKEY - 3))
                    sp.dma_start(gelus[:, s, :], gelu_kept[g * 4 + (s - NKEY)]).then_inc(gelu_loaded[s], 16)
            sp.wait_ge(h_stored, 16)
            sp.dma_start(h_back, h_kept).then_inc(h_back_loaded, 16)
            for a in range(2):
                sp.wait_ge(out_ready, NT * (a + 1))
                half = slice(a * 512, (a + 1) * 512)
                sp.dma_start(out.rearrange("(t p) n -> p t n", p=P)[:, :, half],
                             h_back.rearrange("p (t n) -> p t n", t=NT)[:, :, half]).then_inc(stored, 16)
            sp.wait_ge(stored, 32)

        @block.gpsimd
        def _(pool):
            step = Signal(pool_step)

            def chain(ins):
                pool.wait_ge(pool_step, step.on(ins))

            chain(pool.memset(ident[:], 0.0))
            pool.affine_select(ident[:], ident[:], [[-1, P]], ALU.not_equal, 1.0, base=0,
                               channel_multiplier=1).then_inc(ident_ready, 1)
            pool.iota(untapped.bitcast(I32), [[-1, SEQ]], base=P, channel_multiplier=1).then_inc(masks_ready, 1)
            chain(pool.memset(tri_neg, -1.0))
            pool.affine_select(tri_neg, tri_neg, [[-1, P]], ALU.is_ge, 0.0, base=0,
                               channel_multiplier=1).then_inc(masks_ready, 1)
            pool.memset(ones_neg, -1.0).then_inc(masks_ready, 1)
            pool.iota(iota_key[:], [[1, P]], base=0, channel_multiplier=0,
                      allow_small_or_imprecise_dtypes=True).then_inc(masks_ready, 1)
            pool.iota(iota_cand[:], [[1, NCAND]], base=0, channel_multiplier=0,
                      allow_small_or_imprecise_dtypes=True).then_inc(masks_ready, 1)
            for g in range(2):
                soft = t2[:, 1536:3072]
                pool.wait_ge(b_soft, g + 1)
                for at, n in ((0, SEQ), (1024, P)):
                    part = soft[:, at:at + 4 * n].rearrange("p (h t) -> p h t", h=4)[:, :, 0:P]
                    pool.affine_select(part, part, [[0, 4], [1, P]], ALU.is_gt, 0.0, base=0,
                                       channel_multiplier=-1).then_inc(b_soft_masked, 1)
                pool.wait_ge(b_stick, 2 * (g + 1))
                for at in (0, SEQ):
                    part = sticks[:, 4 * g:4 * g + 4, at:at + P]
                    pool.affine_select(part, part, [[0, 4], [1, P]], ALU.is_gt, 0.0, base=0,
                                       channel_multiplier=-1).then_inc(b_stick_masked, 1)

        def b_head(g, j):
            return 4 * g + (0, 2, 1, 3)[j]

        @block.tensor
        def _(pe):
            def turn(i, t, b):
                pe.wait_ge(rows_normed, NT * i + t + 1)
                for k in range(KD):
                    ins = pe.transpose(ps[:, b + k // 4, (k % 4) * P:][:, 0:P], ROWS[i][:, t, k * P:(k + 1) * P],
                                       ident[:])
                    if k % 4 == 3:
                        ins.then_inc(x_psum, 1)

            def parts_ready(i, t, a):
                pe.wait_ge(x_lo_ready, 4 * i + 2 * t + a + 1)

            def rows_half(u, a, t, b, i):
                n = 2 * u + a
                pe.wait_ge(w_lo_ready, n + 1)
                parts_ready(i, t, a)
                hi, lo = X_PARTS[i]
                for k in range(4):
                    for m, (x_, w) in enumerate(((hi, hi_of(n)), (hi, lo_of(n)), (lo, hi_of(n)))):
                        ins = pe.matmul(bank(b), x_[:, 4 * a + k, t * P:(t + 1) * P], w[:, k, :],
                                        start=(a == 0 and k == 0 and m == 0), stop=(a == 1 and k == 3 and m == 2))
                return ins

            def project_rows(u, b, i, bank_free=()):
                for a in range(2):
                    for t in range(NT):
                        if bank_free and a == 0:
                            pe.wait_ge(bank_free[t], 1)
                        ins = rows_half(u, a, t, b + t, i)
                    ins.then_inc(w_used, 1)

            def project_cols(u, b, i):
                hi, lo = X_PARTS[i]
                for a in range(2):
                    n = 2 * u + a
                    pe.wait_ge(w_lo_ready, n + 1)
                    parts_ready(i, 1, a)
                    for c in range(4):
                        for k in range(4):
                            for m, (w, x_) in enumerate(((hi_of(n), hi), (hi_of(n), lo), (lo_of(n), hi))):
                                ins = pe.matmul(ps[:, b + c // 2, (c % 2) * SEQ:][:, 0:SEQ],
                                                w[:, k, c * P:(c + 1) * P], x_[:, 4 * a + k, :],
                                                start=(a == 0 and c % 2 == 0 and k == 0 and m == 0),
                                                stop=(a == 1 and k == 3 and m == 2), skip_group_check=True)
                    ins.then_inc(w_used, 1)

            def stick_scores(g):
                for j in range(4):
                    hh = b_head(g, j)
                    rows = slice(HD * (hh % 2), HD * (hh % 2) + HD)
                    if j == 2:
                        pe.wait_ge(b_evens, g + 1)
                    pe.matmul(ps[:, j // 2, (j % 2) * SEQ:][:, 0:SEQ], k_bt[rows, hh // 2, 0:P],
                              q_bt[rows, hh // 2, :], start=(j % 2 == 0), stop=True, skip_group_check=True)
                    ins = pe.matmul(ps[:, 2, j * P:(j + 1) * P], k_bt[rows, hh // 2, P:SEQ],
                                    q_bt[rows, hh // 2, P:SEQ], start=(j == 0), stop=True, skip_group_check=True)
                    if j == 1:
                        ins.then_inc(b_evens, 1)
                ins.then_inc(b_scores, 1)

            def stick_sums(g):
                soft = t2[:, 1536:3072]
                pe.wait_ge(b_soft_masked, 2 * (g + 1))
                for j in range(4):
                    s0 = soft[:, j * SEQ:(j + 1) * SEQ]
                    s1 = soft[:, 1024 + j * P:1024 + (j + 1) * P]
                    z0 = ps[:, j // 2, (j % 2) * SEQ:][:, 0:SEQ]
                    pe.matmul(z0, tri_neg, s0, start=False, stop=False, skip_group_check=True)
                    pe.matmul(z0[:, P:SEQ], ones_neg, s1, start=False, stop=True, skip_group_check=True)
                    ins = pe.matmul(ps[:, 2, j * P:(j + 1) * P], tri_neg, s1, start=False, stop=True,
                                    skip_group_check=True)
                ins.then_inc(b_summed, 1)

            def keep_warm(n, b):
                for _ in range(n):
                    pe.matmul(ps[:, b, 0:P], ident[:], ident[:], start=True, stop=True)

            pe.wait_ge(ident_ready, 1)
            keep_warm(20, 7)
            turn(X_ROWS, 0, 0)
            keep_warm(3, 7)
            turn(X_ROWS, 1, 2)
            keep_warm(11, 7)
            project_cols(Q_B, 4, X_ROWS)
            project_cols(K_B, 6, X_ROWS)
            turn(MEM_ROWS, 0, 0)
            turn(MEM_ROWS, 1, 2)
            pe.wait_ge(taken[Q_B], 1)
            project_rows(Q_A, 4, X_ROWS)
            parts_ready(MEM_ROWS, 1, 1)
            pe.wait_ge(taken[K_B], 1)
            pe.wait_ge(masks_ready, 5)
            stick_scores(0)
            project_rows(K_A, 6, X_ROWS)
            stick_sums(0)
            pe.wait_ge(taken[Q_A], 1)
            project_rows(V_B, 4, X_ROWS)
            pe.wait_ge(b_stick, 2)
            stick_scores(1)
            pe.wait_ge(taken[K_A], 1)
            project_rows(V_A, 6, X_ROWS)

            def turn_qk(w):
                for c in range(4):
                    for t in range(NT):
                        ins = pe.transpose(ps[:, 4 + 2 * w + c // 2, (c % 2) * SEQ + t * P:][:, 0:P],
                                           qk_a[:, t, w, c * P:(c + 1) * P], ident[:])
                ins.then_inc(at_psum, 1)

            pe.wait_ge(taken[V_B], 1)
            pe.wait_ge(qk_normed, 1)
            turn_qk(0)
            stick_sums(1)
            pe.wait_ge(taken[V_A], 1)
            turn_qk(1)
            keep_warm(6, 3)
            pe.wait_ge(b_stick, 4)
            pe.wait_ge(q_at_ready, 1)
            pe.wait_ge(k_at_ready, 1)
            for par in range(2):
                rows = slice(HD * par, HD * par + HD)
                for c in range(4):
                    ins = pe.matmul(ps[:, par, c * P:(c + 1) * P], q_at[rows, c, 0:P], k_at[rows, c, 0:P],
                                    start=True, stop=True)
            ins.then_inc(a_scores, 1)
            for par in range(2):
                rows = slice(HD * par, HD * par + HD)
                for c in range(4):
                    ins = pe.matmul(ps[:, 2 + 2 * par + c // 2, (c % 2) * SEQ:][:, 0:SEQ],
                                    q_at[rows, c, P:SEQ], k_at[rows, c, :], start=True, stop=True)
                ins.then_inc(a_scores, 1)

            pe.wait_ge(b_stick_masked, 4)
            for t in range(NT):
                for hh in range(NH):
                    for sblk in range(t + 1):
                        g, j = hh // 4, (0, 2, 1, 3)[hh % 4]
                        st = sticks[:, 4 * g + j, :]
                        at = t * P if sblk == 0 else SEQ
                        ins = pe.matmul(ps[:, 6 + t, hh * HD:(hh + 1) * HD], st[:, at:at + P],
                                        v_b[:, sblk, hh * HD:(hh + 1) * HD], start=(sblk == 0), stop=(sblk == t))
                ins.then_inc(b_out, 1)
            project_rows(K_MEM, 6, MEM_ROWS, b_taken)

            for n in range(24):
                if n % 8 == 0:
                    pe.wait_ge(a_weighted, n // 8 + 1)
                ins = pe.transpose(ps[:, n // 4, (n % 4) * P:][:, 0:P], t2[:, n * P:(n + 1) * P], ident[:])
                if n % 8 == 7:
                    ins.then_inc(a_turned, 1)
            pe.wait_ge(taken[K_MEM], 1)
            for t in range(NT):
                pe.wait_ge(a_prob_t, (1, 3)[t])
                for hh in range(NH):
                    slot = (hh % 2) * 4 + hh // 2
                    for sblk in range(t + 1):
                        at = slot * P if t == 0 else 1024 + slot * SEQ + sblk * P
                        ins = pe.matmul(ps[:, 6 + t, hh * HD:(hh + 1) * HD], t1[:, at:at + P],
                                        v_a[:, sblk, hh * HD:(hh + 1) * HD], start=(sblk == 0), stop=(sblk == t))
                ins.then_inc(a_out, 1)

            turn(MIXED_ROWS, 0, 0)
            keep_warm(8, 4)
            pe.wait_ge(a_mixed, 2)
            for t in range(NT):
                for n in range(2):
                    if (t, n) == (0, 1):
                        turn(MIXED_ROWS, 1, 2)
                    for a in range(2):
                        ins = rows_half(OUT0 + n, a, t, 6 - 2 * t + n, MIXED_ROWS)
                        if t == 1 and (n, a) != (1, 1):
                            ins.then_inc(w_used, 1)
                if t == 0:
                    ins.then_inc(out_projected, 1)
                    pe.wait_ge(mk_normed, 1)
                    for c in range(MH):
                        for m in range(NT):
                            ins = pe.transpose(ps[:, c // 2, (c % 2) * SEQ + m * P:][:, 0:P],
                                               k_mem[:, m, c * P:(c + 1) * P], ident[:])
                    ins.then_inc(mk_psum, 1)
            ins.then_inc(w_used, 1)
            pe.wait_ge(mk_ready, 1)

            def turn_queries(t):
                pe.wait_ge(mq_taken, t + 1)
                for c in range(MH):
                    ins = pe.transpose(ps[:, 7 - 2 * t, c * P:(c + 1) * P], q_mem[:, t, c * P:(c + 1) * P], ident[:])
                ins.then_inc(mq_psum, 1)

            for t in range(NT):
                turn(QUERY_ROWS, t, 2 * t)
                pe.wait_ge(h_ready, t + 1)
                if t == 1:
                    turn_queries(0)
                for a in range(2):
                    ins = rows_half(Q_MEM, a, t, 6 - 2 * t, QUERY_ROWS)
                    if t == 1 and a == 0:
                        ins.then_inc(w_used, 1)
                if t == 0:
                    ins.then_inc(mq_projected, 1)
            ins.then_inc(w_used, 1)

            def memory_scores(t):
                pe.wait_ge(mq_ready, t + 1)
                for c in range(MH):
                    ins = pe.matmul(ps[:, 2 * t + c // 2, (c % 2) * SEQ:][:, 0:SEQ],
                                    q_at[:, c, t * P:(t + 1) * P], k_memt[:, c, :], start=True, stop=True)
                ins.then_inc(m_scores, 1)

            def memory_values(a):
                for t in range(NT):
                    ins = rows_half(V_MEM, a, t, 6 + t, MEM_ROWS)
                ins.then_inc(w_used, 1)

            memory_scores(0)
            memory_values(0)
            turn_queries(1)
            memory_scores(1)
            memory_values(1)
            for t in range(NT):
                pe.wait_ge(m_weighted, t + 1)
                if t == 1:
                    pe.wait_ge(taken[V_MEM], 1)
                for c in range(MH):
                    for m in range(2):
                        ins = pe.transpose(ps[:, 4 + 2 * t + c // 2, (c % 2) * SEQ + m * P:][:, 0:P],
                                           t2[:, (t * MH + c) * SEQ + m * P:][:, 0:P], ident[:])
                ins.then_inc(m_turned, 1)
            for t in range(NT):
                pe.wait_ge(m_prob_t[t], 1)
                for c in range(MH):
                    for m in range(2):
                        ins = pe.matmul(ps[:, t, c * P:(c + 1) * P], v_mem[:, m, c * P:(c + 1) * P],
                                        t1[:, t * D + (c * 2 + m) * P:][:, 0:P], start=(m == 0), stop=(m == 1))
                ins.then_inc(m_out, 1)
            for t in range(NT):
                for a in range(2):
                    pe.wait_ge(w_lo_ready, 2 * O_MEM + a + 1)
                    pe.wait_ge(m_out_lo, t + 1)
                    hi, lo = (f(2 * O_MEM + a) for f in (hi_of, lo_of))
                    for n in range(2):
                        for k in range(2):
                            for m, (o, w) in enumerate(((o_hi, hi), (o_hi, lo), (o_lo, hi))):
                                ins = pe.matmul(bank(4 + 2 * t + n), o[:, 2 * a + k, t * P:(t + 1) * P],
                                                w[:, 2 * k + n, :], start=(a == 0 and k == 0 and m == 0),
                                                stop=(a == 1 and k == 1 and m == 2))
                    if t == 1 and a == 0:
                        ins.then_inc(w_used, 1)
                if t == 0:
                    ins.then_inc(o_projected, 1)
            ins.then_inc(w_used, 1)

            turn(FFN_ROWS, 0, 0)
            keep_warm(12, 3)
            turn(FFN_ROWS, 1, 2)
            keep_warm(4, 4)
            for n in range(PEER_UNITS):
                project_cols(PEER0 + n, (4 + 2 * n) % 8, FFN_ROWS)
            pe.wait_ge(w_loaded[KEYS_HALF % WSLOTS], 16 * (KEYS_HALF // WSLOTS + 1))
            keys = ring[KEYS_HALF % WSLOTS].rearrange("p (b n) -> p b n", b=NBLK)
            for t in range(NT):
                for b in range(NBLK):
                    if t == 0 and b % 4 == 0:
                        pe.wait_ge(taken[PEER0 + b // 4], 1)
                        if b == 0:
                            pe.wait_ge(taken[PEER0 + 2], 1)
                            pe.wait_ge(taken[PEER0 + 3], 1)
                    ins = pe.matmul(ps[:, 4 * t + b // 4, (b % 4) * P:][:, 0:P], q_peert[:, b, t * P:(t + 1) * P],
                                    keys[:, b, :], start=True, stop=True)
                ins.then_inc(key_scores, 1)

            def hidden(g, s, a, first=False):
                c = g * 4 + s
                pe.wait_ge(part_lo_ready, 2 * c + (a + 1))
                if a == 0 and not first:
                    pe.wait_ge(gelu_done, c - 3)
                part = 2 * (s % 2) + a
                for k in range(4):
                    w = slice(k * P, (k + 1) * P)
                    for n, (u, r) in enumerate(((part_hi, x_hi), (part_hi, x_lo), (part_lo, x_hi))):
                        ins = pe.matmul(ps[:, s, 0:SEQ], u[:, part, w], r[:, 4 * a + k, :],
                                        start=(a == 0 and k == 0 and n == 0), stop=(a == 1 and k == 3 and n == 2))
                ins.then_inc(part_used, 1)

            def gate_matrix(n, b, first=False):
                pe.wait_ge(gated, n + 1)
                if not first:
                    pe.wait_ge(g_taken, n - 3)
                for q in range(4):
                    ins = pe.matmul(ps[:, 4 + b, q * P:(q + 1) * P], hot_j[:, b, q, :], hot_i[b][:, q, :],
                                    start=True, stop=True)
                ins.then_inc(g_done, 1)

            def plain_group(g, first=False):
                for s in range(4):
                    for a in range(2):
                        hidden(g, s, a, first)

            pe.wait_ge(key_scores_taken, 1)
            plain_group(0, True)
            with pe.Fori(1, G_GATES) as g:
                plain_group(g)
            for p in range(8):
                hidden(G_GATES, p // 2, p % 2)
                if p == 5:
                    pe.wait_ge(routed, 1)
                    for w in range(3):
                        for t in range(NT):
                            ins = pe.transpose(ps[:, 6 + w // 2, (w % 2) * SEQ + t * P:][:, 0:P],
                                               chosen[:, w * NT + t, :], ident[:])
                    ins.then_inc(route_psum, 1)

            def build_pair(g, n, first=False):
                for p in range(16):
                    hidden(g + p // 8, p // 2 % 4, p % 2)
                    if p in PLACES:
                        m = PLACES.index(p)
                        gate_matrix(n + m, m % 4, first and m < 4)

            pe.wait_ge(route_ready, 1)
            build_pair(G_BUILD, 0, True)
            with pe.Fori(1, PAIRS) as r:
                build_pair(r * 2 + G_BUILD, r * len(PLACES))
            for p in range(8):
                hidden(GROUPS - 1, p // 2, p % 2)
                if p < 4:
                    gate_matrix(QUADS - 4 + p, p)

            def mix(g, s, a, first=False):
                c = g * 4 + s
                pe.wait_ge(part_lo_ready, 2 * c + (a + 1))
                if a == 0:
                    pe.wait_ge(a_lo_ready, c - (NKEY - 1))
                b = s % 2
                hi, lo = v_hi[s // 2], v_lo[s // 2]
                for t in range(NT):
                    for n, (w, r) in enumerate(((a_hi, hi), (a_hi, lo), (a_lo, hi))):
                        ins = pe.matmul(bank(2 * t + a), w[:, b, t * P:(t + 1) * P], r[:, 2 * b + a, :],
                                        start=(first and n == 0), stop=False, skip_group_check=True)
                ins.then_inc(part_used, 1)

            for s in range(4):
                for a in range(2):
                    if s == 0:
                        pe.wait_ge(gelu_done, NKEY - 1 + a)
                    mix(GROUPS, s, a, s == 0)
            with pe.Fori(GROUPS + 1, 2 * GROUPS) as g:
                for s in range(4):
                    mix(g, s, 0)
                    mix(g, s, 1)

        @block.scalar
        def _(act):
            step = Signal(act_step)

            def chain(ins):
                act.wait_ge(act_step, step.on(ins))

            roots = [0]

            def root(cols):
                roots[0] += 1
                act.wait_ge(mean_ready, roots[0])
                act.activation(stat[:, 2, cols], stat[:, 1, cols], ACT.Sqrt).then_inc(root_ready, 1)

            def squares(junk, src, col):
                act.activation(junk, src, ACT.Square, accum_out=stat[:, 0, col:col + 1]).then_inc(sumsq, 1)

            def weights_hi(n):
                act.wait_ge(w_loaded[n % WSLOTS], 16 * (n // WSLOTS + 1))
                if hi_free(n):
                    act.wait_ge(w_used, hi_free(n))
                act.activation(hi_of(n), ring[n % WSLOTS].rearrange("p (k n) -> p k n", k=4),
                               ACT.Copy).then_inc(w_hi_ready, 1)

            def turned_hi(i, t, b):
                for a in range(2):
                    act.wait_ge(x_psum, 4 * i + 2 * t + a + 1)
                    act.activation(X_PARTS[i][0][:, 4 * a:4 * a + 4, t * P:(t + 1) * P],
                                   bank(b + a).rearrange("p (k t) -> p k t", k=4), ACT.Copy).then_inc(x_hi_ready, 1)

            def sticks_log(g):
                act.wait_ge(b_scores, g + 1)
                if g:
                    act.wait_ge(b_soft, g)
                e = t2[:, 0:1536]
                chain(act.activation(e, bank(0, 3), ACT.Abs))
                chain(act.activation(e, e, ACT.Exp, scale=-1.0))
                act.activation(e, e, ACT.Ln, bias=1.0).then_inc(b_log, 1)

            def sticks_exp(g):
                act.wait_ge(b_summed, g + 1)
                act.activation(sticks[:, 4 * g:4 * g + 4, 0:SEQ],
                               bank(0, 2).rearrange("p (h t) -> p h t", h=4), ACT.Exp).then_inc(b_stick, 1)
                act.activation(sticks[:, 4 * g:4 * g + 4, SEQ:SEQ + P],
                               bank(2).rearrange("p (h t) -> p h t", h=4), ACT.Exp).then_inc(b_stick, 1)

            def take_unit(u, dst, b, scale=1.0):
                act.wait_ge(w_used, 2 * (u + 1))
                act.activation(dst, bank(b, 2), ACT.Copy, scale=scale).then_inc(taken[u], 1)

            def take_qk(w, b):
                u = (Q_A, K_A)[w]
                act.wait_ge(w_used, 2 * (u + 1))
                act.activation(qk_a[:, :, w, :], ps[:, b:b + 2, :], ACT.Copy).then_inc(taken[u], 1)

            junk = scratch(15360, 2048).rearrange("p (t n) -> p t n", t=NT)
            act.wait_ge(one_ready, 1)
            act.activation(one[:], one[:], ACT.Sqrt)
            for t in range(NT):
                act.wait_ge(loaded_x[t], 16)
                squares(junk[:, t, :], h[:, t, :], t)
                root(slice(t, t + 1))
            turned_hi(X_ROWS, 0, 0)
            weights_hi(0)
            turned_hi(X_ROWS, 1, 2)
            weights_hi(1)
            act.wait_ge(loaded_mem, 16)
            act.wait_ge(sumsq, 2)
            for t in range(NT):
                squares(junk[:, t, :], rows2[:, t, :], 2 + t)
            root(slice(2, 4))
            for n in (2, 3, 4, 5):
                weights_hi(n)
            take_unit(Q_B, q_bt.rearrange("p b t -> p (b t)"), 4, HD ** -0.5)
            weights_hi(6)
            act.wait_ge(angles, 1)
            act.activation(cossin[:].rearrange("p w t f -> p (w t f)"),
                           cossin[:].rearrange("p w t f -> p (w t f)"), ACT.Sin).then_inc(sines, 1)
            turned_hi(MEM_ROWS, 0, 0)
            turned_hi(MEM_ROWS, 1, 2)
            weights_hi(7)
            weights_hi(8)
            take_qk(0, 4)
            weights_hi(9)
            sticks_log(0)
            weights_hi(10)
            take_qk(1, 6)
            weights_hi(11)
            sticks_exp(0)
            root(slice(0, 32))
            weights_hi(12)
            take_unit(V_B, v_b.rearrange("p t n -> p (t n)"), 4)
            weights_hi(13)
            sticks_log(1)
            weights_hi(14)
            sticks_exp(1)
            act.wait_ge(at_psum, 2)
            act.activation(k_at.rearrange("p b t -> p (b t)"), bank(6, 2), ACT.Copy).then_inc(k_at_ready, 1)
            weights_hi(15)
            for n in range(16):
                if n in (0, 8, 12):
                    act.wait_ge(a_max, (0, 8, 12).index(n) + 1)
                part = t2[:, n * P:(n + 1) * P] if n < 8 else t2[:, 1024 + (n - 8) * SEQ:][:, 0:SEQ]
                act.activation(part, part, ACT.Exp, bias=stat[:, 3, n:n + 1], scale=HD ** -0.5).then_inc(a_exp, 1)
            act.wait_ge(b_out, 2)
            act.activation(mixed[:, 1, 512:1024], bank(7), ACT.Copy).then_inc(b_taken[1], 1)
            for t in range(NT):
                act.wait_ge(b_taken[t], 1)
            for t in range(NT):
                squares(q_mem[:, t, :], mixed[:, t, 512:1024], t)
            root(slice(0, 2))
            weights_hi(16)
            take_unit(K_MEM, k_mem.rearrange("p t n -> p (t n)"), 6)
            for n in range(3):
                act.wait_ge(a_turned, n + 1)
                act.activation(t1[:, n * 1024:(n + 1) * 1024], bank(2 * n, 2), ACT.Copy).then_inc(a_prob_t, 1)
            act.wait_ge(sumsq, 6)
            for t in range(NT):
                act.wait_ge(a_mixed, t + 1)
                squares(q_mem[:, t, :], mixed[:, t, 0:512], 2 + t)
                root(slice(2 + t, 3 + t))
                if t == 0:
                    weights_hi(17)
                else:
                    root(slice(8, 16))
                turned_hi(MIXED_ROWS, t, 2 * t)
            act.wait_ge(h_ready, 1)
            squares(t1[:, 0:D], h[:, 0, :], 4)
            root(slice(4, 5))
            weights_hi(18)
            weights_hi(19)
            turned_hi(QUERY_ROWS, 0, 0)
            act.wait_ge(h_ready, 2)
            squares(t1[:, D:2 * D], h[:, 1, :], 5)
            root(slice(5, 6))
            weights_hi(20)
            act.wait_ge(mq_projected, 1)
            act.activation(q_mem[:, 0, :], bank(6), ACT.Copy).then_inc(mq_taken, 1)
            turned_hi(QUERY_ROWS, 1, 2)
            root(slice(16, 20))
            weights_hi(21)
            act.wait_ge(w_used, 2 * Q_MEM + 2)
            act.activation(q_mem[:, 1, :], bank(4), ACT.Copy).then_inc(mq_taken, 1)
            root(slice(20, 24))
            weights_hi(22)
            for t in range(NT):
                if t == 1:
                    weights_hi(23)
                act.wait_ge(m_max, t + 1)
                for n in range(4 * t, 4 * t + 4):
                    act.activation(t2[:, n * SEQ:(n + 1) * SEQ], bank(0, 4)[:, n * SEQ:(n + 1) * SEQ], ACT.Exp,
                                   bias=stat[:, 3, n:n + 1], scale=stat[:, 2, 16 + n:17 + n],
                                   accum_out=stat[:, 4, n:n + 1]).then_inc(m_exp, 1)
            take_unit(V_MEM, v_mem.rearrange("p t n -> p (t n)"), 6)
            act.wait_ge(m_turned, 1)
            act.activation(t1[:, 0:D], bank(4, 2), ACT.Copy).then_inc(m_prob_t[0], 1)
            for t in range(NT):
                act.wait_ge(m_out, t + 1)
                act.activation(o_hi[:, 0:MH, t * P:(t + 1) * P], bank(t).rearrange("p (b t) -> p b t", b=MH),
                               ACT.Copy).then_inc(m_out_hi, 1)
            for n in (24, 25):
                weights_hi(n)
            act.wait_ge(h_ready, 3)
            squares(t1[:, 0:D], h[:, 0, :], 6)
            root(slice(6, 7))
            act.wait_ge(h_ready, 4)
            squares(t1[:, D:2 * D], h[:, 1, :], 7)
            root(slice(7, 8))
            turned_hi(FFN_ROWS, 0, 0)
            turned_hi(FFN_ROWS, 1, 2)
            weights_hi(26)
            weights_hi(27)
            for n in range(PEER_UNITS):
                if n < PEER_UNITS - 2:
                    weights_hi(2 * (PEER0 + n) + 4)
                    weights_hi(2 * (PEER0 + n) + 5)
                take_unit(PEER0 + n, q_peert[:, 4 * n:4 * n + 4, :].rearrange("p b t -> p (b t)"), (4 + 2 * n) % 8)
            def high_part(g, s, a, first=False):
                c = g * 4 + s
                if a == 0:
                    act.wait_ge(raw_loaded[s], 16 * (g + 1))
                if not (first and s < 2):
                    act.wait_ge(part_used, 2 * c + (a - 3))
                act.activation(part_hi[:, 2 * (s % 2) + a, :], raw[:, s, a * 512:(a + 1) * 512],
                               ACT.Copy).then_inc(part_hi_ready, 1)

            def gelu(group, s, first=False):
                c = group * 4 + s
                act.wait_ge(part_used, 2 * c + 2)
                if not first:
                    act.wait_ge(gelu_stored[s], 16 * group)
                act.activation(gelus[:, s, :], ps[:, s, 0:SEQ], ACT.Gelu).then_inc(gelu_done, 1)

            def gate_rows(n, b):
                act.wait_ge(hots_ready, n + 1)
                for q in range(4):
                    ins = act.activation(hot_i[b][:, q, :], hot_i[b][:, q, :], ACT.Copy,
                                         scale=route_t[:, 2, bass.ds(n * 4 + q, 1)])
                ins.then_inc(gated, 1)

            by_token = big[:].rearrange("p (i t) -> p t i", t=SEQ)

            def take_g(n, b):
                act.wait_ge(g_done, n + 1)
                act.activation(by_token[:, bass.ds(n * 4, 4), :], bank(4 + b).rearrange("p (q i) -> p q i", q=4),
                               ACT.Copy).then_inc(g_taken, 1)

            def u_group(g):
                for s in range(4):
                    high_part(g, s, 0)
                    high_part(g, s, 1)
                    gelu(g + (s // 2 - 1), (s - 2) % 4)

            for s in range(4):
                high_part(0, s, 0, True)
                high_part(0, s, 1, True)
                if s == 1:
                    for t in range(NT):
                        act.wait_ge(key_scores, t + 1)
                        act.activation(scores[:, t * NBLK:(t + 1) * NBLK, :].rearrange("p b n -> p (b n)"), bank(4 * t, 4),
                                       ACT.Copy).then_inc(key_scores_taken, 1)
                    act.wait_ge(h_stored, 16)
                if s >= 2:
                    gelu(0, s - 2, True)
            for s in range(4):
                high_part(1, s, 0)
                high_part(1, s, 1)
                gelu(s // 2, (s - 2) % 4, s < 2)
            with act.Fori(2, G_MATCH + 1) as g:
                u_group(g)
            act.wait_ge(best_centred, 1)
            act.activation(chosen[:, 2 * NT:3 * NT, :], chosen[:, 2 * NT:3 * NT, :], ACT.Exp).then_inc(gates_exp, 1)
            u_group(G_MATCH + 1)
            with act.Fori(G_MATCH + 2, G_BUILD) as g:
                u_group(g)

            def build_pair(g, n, first=False):
                for p in range(16):
                    s = p // 2 % 4
                    high_part(g + p // 8, s, p % 2)
                    if p in PLACES:
                        m = PLACES.index(p)
                        if not (first and m < 2):
                            gate_rows(n + (m - 2), (m - 2) % 4)
                        if not (first and m < 4):
                            take_g(n + (m - 4), m % 4)
                    if p % 2:
                        gelu(g + (p // 8 + s // 2 - 1), (s - 2) % 4)

            build_pair(G_BUILD, 0, True)
            with act.Fori(1, PAIRS) as r:
                build_pair(r * 2 + G_BUILD, r * len(PLACES))
            for p in range(8):
                high_part(GROUPS - 1, p // 2, p % 2)
                if p < 6:
                    gate_rows(QUADS - 6 + p, (p - 2) % 4)
                if p < 7:
                    take_g(QUADS - 8 + p, p % 4)
                if p == 6:
                    take_g(QUADS - 1, 3)
                if p % 2:
                    gelu(GROUPS - 2 + p // 4, (p // 2 - 2) % 4)

            def high_v(g, s, a, first=False):
                c = g * 4 + s
                if a == 0:
                    act.wait_ge(raw_loaded[s], 16 * (g + 1))
                act.wait_ge(part_used, (2 * c - 3 + a if s < 2 else 2 * NKEY) if first else 2 * c + (a - 7))
                act.activation(v_hi[s // 2][:, 2 * (s % 2) + a, :], raw[:, s, a * 512:(a + 1) * 512],
                               ACT.Copy).then_inc(part_hi_ready, 1)

            def high_act(c, b, first=False):
                if not first:
                    act.wait_ge(part_used, 2 * c - 2)
                act.wait_ge(acts_ready, c - (NKEY - 1))
                act.activation(a_hi[:, b, :], big[:, bass.ds((c - NKEY) * SEQ, SEQ)],
                               ACT.Copy).then_inc(a_hi_ready, 1)

            gelu(GROUPS - 1, 2)
            for s in range(4):
                high_v(GROUPS, s, 0, True)
                if s == 1:
                    gelu(GROUPS - 1, 3)
                high_v(GROUPS, s, 1, True)
                if s < 2:
                    high_act(NKEY + s, s, True)
            with act.Fori(GROUPS + 1, 2 * GROUPS) as g:
                for s in range(4):
                    high_v(g, s, 0)
                    high_v(g, s, 1)
                    high_act(g * 4 + (s - 2), s % 2)
            high_act(2 * NKEY - 2, 0)
            high_act(2 * NKEY - 1, 1)

        @block.vector
        def _(dve):
            step = Signal(dve_step)

            def chain(ins):
                dve.wait_ge(dve_step, step.on(ins))

            dve.memset(one[:], 1.0).then_inc(one_ready, 1)
            means = [0]

            def mean(cols, width, sums=0):
                if sums:
                    dve.wait_ge(sumsq, sums)
                means[0] += 1
                dve.tensor_scalar(stat[:, 1, cols], stat[:, 0, cols], 1.0 / width, EPS, ALU.mult,
                                  ALU.add).then_inc(mean_ready, 1)

            def inverse(cols):
                dve.wait_ge(root_ready, means[0])
                chain(dve.reciprocal(stat[:, 2, cols], stat[:, 2, cols]))

            def norm_rows(i, src, t, col):
                if t == 0:
                    dve.wait_ge(gain_loaded[i % 2], 16 * (i // 2 + 1))
                dve.scalar_tensor_tensor(ROWS[i][:, t, :], src[:, t, :], stat[:, 2, col:col + 1], gain_row[i % 2],
                                         ALU.mult, ALU.mult).then_inc(rows_normed, 1)

            def weights_lo(n):
                dve.wait_ge(w_hi_ready, n + 1)
                whole = ring[n % WSLOTS].rearrange("p (k n) -> p k n", k=4)
                dve.tensor_tensor(lo_of(n), whole, hi_of(n).bitcast(F32), ALU.subtract).then_inc(w_lo_ready, 1)

            def turned_lo(i, t, b):
                hi, lo = X_PARTS[i]
                for a in range(2):
                    dve.wait_ge(x_hi_ready, 4 * i + 2 * t + a + 1)
                    at_ = (slice(None), slice(4 * a, 4 * a + 4), slice(t * P, (t + 1) * P))
                    dve.tensor_tensor(lo[at_], bank(b + a).rearrange("p (k t) -> p k t", k=4), hi[at_].bitcast(F32),
                                      ALU.subtract).then_inc(x_lo_ready, 1)

            def sticks_soft(g):
                dve.wait_ge(b_log, g + 1)
                if g:
                    dve.wait_ge(b_summed, g)
                dve.scalar_tensor_tensor(t2[:, 1536:3072], bank(0, 3), 0.0, t2[:, 0:1536], ALU.max,
                                         ALU.add).then_inc(b_soft, 1)

            for t in range(NT):
                mean(slice(t, t + 1), D, t + 1)
                inverse(slice(t, t + 1))
                norm_rows(X_ROWS, h, t, t)
            turned_lo(X_ROWS, 0, 0)
            weights_lo(0)
            turned_lo(X_ROWS, 1, 2)
            weights_lo(1)
            mean(slice(2, 4), D, 4)
            inverse(slice(2, 4))
            for t in range(NT):
                norm_rows(MEM_ROWS, rows2, t, 2 + t)
            weights_lo(2)
            weights_lo(3)

            w = [t1[:, 2048 + n * SEQ:2048 + (n + 1) * SEQ] for n in range(4)]
            dve.wait_ge(loaded_c, 48)
            chain(dve.tensor_copy(posf[:], posi[:]))
            for f in range(HALF):
                ins = dve.memset(freq[:, f:f + 1], float(inv_freq[f]))
                step.on(ins)
            dve.wait_ge(dve_step, step.n)
            for t in range(NT):
                chain(dve.tensor_scalar(w[3][:, t * HALF:(t + 1) * HALF], freq[:], posf[:, t:t + 1], None, ALU.mult))
            a16, n16, m16 = w[3][:, 0:16], w[3][:, 16:32], w[3][:, 32:48]
            for c in range(2):
                chain(dve.tensor_scalar(n16, a16, float(1 / (2 * np.pi)), 0.25 * (1 - c), ALU.mult, ALU.add))
                chain(dve.tensor_scalar(n16, n16, MAGIC, None, ALU.add))
                chain(dve.tensor_scalar(n16, n16, MAGIC, None, ALU.subtract))
                chain(dve.scalar_tensor_tensor(m16, n16, -TWO_PI_PARTS[0], a16, ALU.mult, ALU.add))
                chain(dve.scalar_tensor_tensor(m16, n16, -TWO_PI_PARTS[1], m16, ALU.mult, ALU.add))
                chain(dve.scalar_tensor_tensor(m16, n16, -TWO_PI_PARTS[2], m16, ALU.mult, ALU.add))
                chain(dve.tensor_scalar(m16, m16, float(np.pi / 2) * (1 - c), PI_SAFE, ALU.add, ALU.min))
                ins = dve.tensor_scalar(cossin[:, c].rearrange("p t f -> p (t f)"), m16, -PI_SAFE, None, ALU.max)
                if c:
                    ins.then_inc(angles, 1)
                else:
                    chain(ins)
            weights_lo(4)
            weights_lo(5)
            weights_lo(6)
            dve.wait_ge(w_used, 2 * (K_B + 1))
            dve.tensor_copy(k_bt.rearrange("p b t -> p (b t)"), bank(6, 2)).then_inc(taken[K_B], 1)
            turned_lo(MEM_ROWS, 0, 0)
            turned_lo(MEM_ROWS, 1, 2)
            weights_lo(7)

            dve.wait_ge(masks_ready, 5)
            off_i = untapped.bitcast(I32)
            chain(dve.tensor_copy(w[0], off_i))
            chain(dve.tensor_scalar(taps, w[0], float(TAPS[0][0]), None, ALU.is_le))
            for window, dilation in zip(TAPS[0][1:], TAPS[1][1:]):
                assert window >= SEQ
                chain(dve.tensor_scalar(w[1].bitcast(I32), off_i, dilation - 1, None, ALU.bitwise_and))
                chain(dve.tensor_copy(w[2], w[1].bitcast(I32)))
                chain(dve.scalar_tensor_tensor(taps, w[2], 0.0, taps, ALU.is_equal, ALU.add))
            chain(dve.scalar_tensor_tensor(taps, w[0], 0.0, taps, ALU.is_ge, ALU.mult))
            chain(dve.tensor_scalar(untapped, taps, 0.0, MASKED, ALU.is_equal, ALU.mult))
            weights_lo(8)
            weights_lo(9)
            sticks_soft(0)
            weights_lo(10)

            dve.wait_ge(taken[Q_A], 1)
            dve.wait_ge(taken[K_A], 1)
            flat = qk_a.rearrange("p t w n -> p (t w n)")
            by_head = qk_a.rearrange("p t w (h d) -> p (t w h) d", d=HD)
            sq = t1[:, 0:2048]
            chain(dve.tensor_tensor(sq, flat, flat, ALU.mult))
            weights_lo(11)
            chain(dve.tensor_reduce(stat[:, 0, :], sq.rearrange("p (g d) -> p g d", d=HD), AX, ALU.add))
            mean(slice(0, 32), HD)
            inverse(slice(0, 32))
            chain(dve.tensor_tensor(by_head, by_head, stat[:, 2, :].unsqueeze(2).broadcast_to([P, 32, HD]), ALU.mult))
            weights_lo(12)
            for t in range(NT):
                for w_ in range(2):
                    part = qk_a[:, t, w_, :].rearrange("p (h d) -> p h d", d=HD)
                    ins = dve.tensor_tensor(part, part, hgain[:, w_, :].unsqueeze(1).broadcast_to([P, NH, HD]),
                                            ALU.mult)
                    step.on(ins)
            dve.wait_ge(dve_step, step.n)
            dve.wait_ge(sines, 1)
            for t in range(NT):
                part = qk_a[:, t].rearrange("p w (h d) -> p (w h) d", d=HD)
                x1, x2 = part[:, :, 0:HALF], part[:, :, HALF:ROPE]
                cos = cossin[:, 0, t, :].unsqueeze(1).broadcast_to([P, 2 * NH, HALF])
                sin = cossin[:, 1, t, :].unsqueeze(1).broadcast_to([P, 2 * NH, HALF])
                r = [t1[:, n * 128:(n + 1) * 128].rearrange("p (g f) -> p g f", f=HALF) for n in range(4 * t, 4 * t + 4)]
                for o, a, b in ((r[0], x1, cos), (r[1], x2, sin), (r[2], x2, cos), (r[3], x1, sin)):
                    step.on(dve.tensor_tensor(o, a, b, ALU.mult))
                dve.wait_ge(dve_step, step.n)
                step.on(dve.tensor_tensor(x1, r[0], r[1], ALU.subtract))
                ins = dve.tensor_tensor(x2, r[2], r[3], ALU.add)
            ins.then_inc(qk_normed, 1)
            weights_lo(13)
            sticks_soft(1)
            weights_lo(14)
            dve.wait_ge(w_used, 2 * (V_A + 1))
            dve.tensor_copy(v_a.rearrange("p t n -> p (t n)"), bank(6, 2)).then_inc(taken[V_A], 1)
            dve.wait_ge(at_psum, 1)
            dve.tensor_copy(q_at.rearrange("p b t -> p (b t)"), bank(4, 2)).then_inc(q_at_ready, 1)

            parts = [(t2[:, n * 1024:(n + 1) * 1024].rearrange("p (h s) -> p h s", h=(NH, 4, 4)[n]),
                      bank(2 * n, 2).rearrange("p (h s) -> p h s", h=(NH, 4, 4)[n]),
                      (P, 0, 0)[n], ((0, 8), (8, 12), (12, 16))[n]) for n in range(3)]
            for n, (p_, z, s0, (lo_, hi_)) in enumerate(parts):
                dve.wait_ge(a_scores, n + 1)
                chain(dve.tensor_tensor(p_, z, untapped[:, s0:SEQ].unsqueeze(1).broadcast_to([P, hi_ - lo_, SEQ - s0]),
                                        ALU.add))
                chain(dve.tensor_reduce(stat[:, 3, lo_:hi_], p_, AX, ALU.max))
                dve.tensor_scalar(stat[:, 3, lo_:hi_], stat[:, 3, lo_:hi_], -HD ** -0.5, None,
                                  ALU.mult).then_inc(a_max, 1)
            dve.wait_ge(b_out, 1)
            dve.tensor_copy(mixed[:, 0, 512:1024], bank(6)).then_inc(b_taken[0], 1)
            weights_lo(15)
            for n, (p_, z, s0, (lo_, hi_)) in enumerate(parts):
                dve.wait_ge(a_exp, hi_)
                dve.tensor_tensor(p_, p_, taps[:, s0:SEQ].unsqueeze(1).broadcast_to([P, hi_ - lo_, SEQ - s0]),
                                  ALU.mult).then_inc(a_weighted, 1)
            mean(slice(0, 2), 512, 6)
            inverse(slice(0, 2))
            dve.wait_ge(gain_loaded[MIXED_ROWS % 2], 16 * (MIXED_ROWS // 2 + 1))
            for t in range(NT):
                part = mixed[:, t, 512:1024]
                step.on(dve.scalar_tensor_tensor(part, part, stat[:, 2, t:t + 1], gain_row[MIXED_ROWS % 2][:, 512:1024],
                                                 ALU.mult, ALU.mult))
            for n, (p_, z, s0, (lo_, hi_)) in enumerate(parts):
                dve.wait_ge(a_weighted, n + 1)
                step.on(dve.tensor_reduce(stat[:, 4, lo_:hi_], p_, AX, ALU.add))
            dve.wait_ge(dve_step, step.n)
            chain(dve.reciprocal(stat[:, 4, 0:16], stat[:, 4, 0:16]))
            for t in range(NT):
                dve.wait_ge(a_out, t + 1)
                for par in range(2):
                    ins = dve.tensor_tensor(
                        mixed[:, t, 0:512].rearrange("p (a r d) -> p a r d", r=2, d=HD)[:, :, par, :],
                        bank(6 + t).rearrange("p (a r d) -> p a r d", r=2, d=HD)[:, :, par, :],
                        stat[:, 4, 8 * t + 4 * par:8 * t + 4 * par + 4].unsqueeze(2).broadcast_to([P, 4, HD]),
                        ALU.mult)
                    if par == 0:
                        step.on(ins)
                ins.then_inc(a_mixed, 1)
                if t == 1:
                    turned_lo(MIXED_ROWS, 0, 0)
                mean(slice(2 + t, 3 + t), 512, 7 + t)
                inverse(slice(2 + t, 3 + t))
                dve.wait_ge(a_mixed, t + 1)
                part = mixed[:, t, 0:512]
                dve.scalar_tensor_tensor(part, part, stat[:, 2, 2 + t:3 + t], gain_row[MIXED_ROWS % 2][:, 0:512],
                                         ALU.mult, ALU.mult).then_inc(rows_normed, 1)
                weights_lo(16 + t)
            dve.wait_ge(taken[K_MEM], 1)
            by_head = k_mem.rearrange("p t (h d) -> p (t h) d", d=MHD)
            chain(dve.tensor_tensor(sq_mem, k_mem, k_mem, ALU.mult))
            chain(dve.tensor_reduce(stat[:, 0, 8:16], sq_mem.rearrange("p t (h d) -> p (t h) d", d=MHD), AX, ALU.add))
            mean(slice(8, 16), MHD)
            inverse(slice(8, 16))
            dve.tensor_tensor(by_head, by_head, stat[:, 2, 8:16].unsqueeze(2).broadcast_to([P, 8, MHD]),
                              ALU.mult).then_inc(mk_normed, 1)
            turned_lo(MIXED_ROWS, 1, 2)

            def add_to_h(t, b):
                dve.tensor_tensor(h[:, t, :], h[:, t, :], bank(b, 2), ALU.add).then_inc(h_ready, 1)

            dve.wait_ge(out_projected, 1)
            add_to_h(0, 6)
            mean(slice(4, 5), D, 9)
            inverse(slice(4, 5))
            norm_rows(QUERY_ROWS, h, 0, 4)
            dve.wait_ge(mk_psum, 1)
            dve.tensor_scalar(k_memt.rearrange("p b t -> p (b t)"), bank(0, 2), gain[:, G_KM:G_KM + 1], None,
                              ALU.mult).then_inc(mk_ready, 1)
            weights_lo(18)
            dve.wait_ge(w_used, 2 * (OUT1 + 1))
            add_to_h(1, 4)
            turned_lo(QUERY_ROWS, 0, 0)
            weights_lo(19)
            mean(slice(5, 6), D, 10)
            inverse(slice(5, 6))
            norm_rows(QUERY_ROWS, h, 1, 5)
            weights_lo(20)
            turned_lo(QUERY_ROWS, 1, 2)

            def query_scale(t):
                cols4 = slice(16 + 4 * t, 20 + 4 * t)
                dve.wait_ge(mq_taken, t + 1)
                chain(dve.tensor_tensor(sq_mem[:, t, :], q_mem[:, t, :], q_mem[:, t, :], ALU.mult))
                chain(dve.tensor_reduce(stat[:, 0, cols4], sq_mem[:, t, :].rearrange("p (h d) -> p h d", d=MHD), AX,
                                        ALU.add))
                mean(cols4, MHD)
                inverse(cols4)
                chain(dve.tensor_scalar(stat[:, 2, cols4], stat[:, 2, cols4], MHD ** -0.5, None, ALU.mult))

            def take_queries(t):
                dve.wait_ge(mq_psum, t + 1)
                dve.tensor_scalar(q_at[:, :, t * P:(t + 1) * P], bank(7 - 2 * t).rearrange("p (b t) -> p b t", b=MH),
                                  gain[:, G_QM:G_QM + 1], None, ALU.mult).then_inc(mq_ready, 1)

            def greatest(t):
                four = slice(4 * t, 4 * t + 4)
                dve.wait_ge(m_scores, t + 1)
                chain(dve.tensor_reduce(stat[:, 3, four], bank(2 * t, 2).rearrange("p (g m) -> p g m", g=4), AX, ALU.max))
                dve.scalar_tensor_tensor(stat[:, 3, four], stat[:, 3, four], -1.0, stat[:, 2, 16 + 4 * t:20 + 4 * t],
                                         ALU.mult, ALU.mult).then_inc(m_max, 1)

            query_scale(0)
            take_queries(0)
            weights_lo(21)
            query_scale(1)
            greatest(0)
            take_queries(1)
            weights_lo(22)
            greatest(1)
            for t in range(NT):
                four = slice(4 * t, 4 * t + 4)
                dve.wait_ge(m_exp, 4 * t + 4)
                chain(dve.reciprocal(stat[:, 4, four], stat[:, 4, four]))
                part = t2[:, t * D:(t + 1) * D].rearrange("p (g m) -> p g m", g=4)
                dve.tensor_tensor(part, part, stat[:, 4, four].unsqueeze(2).broadcast_to([P, 4, SEQ]),
                                  ALU.mult).then_inc(m_weighted, 1)
            weights_lo(23)
            dve.wait_ge(m_turned, 2)
            dve.tensor_copy(t1[:, D:2 * D], bank(6, 2)).then_inc(m_prob_t[1], 1)
            for t in range(NT):
                dve.wait_ge(m_out_hi, t + 1)
                at_ = (slice(None), slice(0, MH), slice(t * P, (t + 1) * P))
                dve.tensor_tensor(o_lo[at_], bank(t).rearrange("p (b t) -> p b t", b=MH), o_hi[at_].bitcast(F32),
                                  ALU.subtract).then_inc(m_out_lo, 1)
            for n in (24, 25):
                weights_lo(n)
            dve.wait_ge(o_projected, 1)
            add_to_h(0, 4)
            mean(slice(6, 7), D, 11)
            inverse(slice(6, 7))
            norm_rows(FFN_ROWS, h, 0, 6)
            dve.wait_ge(w_used, 2 * (O_MEM + 1))
            add_to_h(1, 6)
            mean(slice(7, 8), D, 12)
            inverse(slice(7, 8))
            norm_rows(FFN_ROWS, h, 1, 7)
            turned_lo(FFN_ROWS, 0, 0)
            turned_lo(FFN_ROWS, 1, 2)
            weights_lo(26)
            weights_lo(27)
            for n in range(28, KEYS_HALF):
                weights_lo(n)

            def low_part(c, s, a):
                part = 2 * (s % 2) + a
                dve.wait_ge(part_hi_ready, 2 * c + (a + 1))
                dve.tensor_tensor(part_lo[:, part, :], raw[:, s, a * 512:(a + 1) * 512],
                                  part_hi[:, part, :].bitcast(F32), ALU.subtract).then_inc(part_lo_ready, 1)

            def beside(c, steps, halves=8):
                done = 0
                for n in range(halves):
                    low_part(c + n // 2, n // 2 % 4, n % 2)
                    upto = len(steps) * (n + 1) // halves
                    for emit in steps[done:upto]:
                        emit()
                    done = upto

            def largest(pair, tensors, sem_, ready=None):
                def emit(n):
                    val, pos_, row = (x[:, 2 * pair + n % 2, :] for x in tensors)
                    if ready and n == 0:
                        dve.wait_ge(*ready)
                    if n >= 2:
                        dve.wait_ge(sem_, 10 * pair + n - 1)
                    lo8, hi8 = slice(0, 8), slice(8, 16)
                    ins = (lambda: dve.max(val[:, lo8], row),
                           lambda: dve.max_index(pos_[:, lo8], val[:, lo8], row),
                           lambda: dve.match_replace(row, val[:, lo8], row, LOWEST),
                           lambda: dve.max(val[:, hi8], row),
                           lambda: dve.max_index(pos_[:, hi8], val[:, hi8], row))[n // 2]()
                    ins.then_inc(sem_, 1)

                return [lambda n=n: emit(n) for n in range(10)]

            pair = 0
            for g, pairs in enumerate(TOP_PAIRS):
                beside(4 * g, [f for n in range(pair, pair + pairs)
                               for f in largest(n, (top_val, top_pos, scores), top_step,
                                                (key_scores_taken, 2 * n // NBLK + 1) if 2 * n % NBLK == 0 else None)])
                pair += pairs
            dve.wait_ge(top_step, 5 * NT * NBLK)

            def candidates(dst, src):
                pair = src.rearrange("p (h w) k -> p h w k", w=2)
                c, emits = 0, []
                for a, n in enumerate(CAND):
                    if n == 1:
                        break
                    emits.append(lambda a=a, n=n, c=c: step.on(dve.tensor_tensor(
                        dst[:, :, c:c + n], pair[:, :, 0, a:a + 1].broadcast_to([P, NT * PH, n]),
                        pair[:, :, 1, 0:n], ALU.add)))
                    c += n
                emits.append(lambda: step.on(dve.tensor_tensor(
                    dst[:, :, c:NCAND], pair[:, :, 0, a:TOPK],
                    pair[:, :, 1, 0:1].broadcast_to([P, NT * PH, TOPK - a]), ALU.add)))
                return emits

            highs = top_id.rearrange("p (h w) k -> p h w k", w=2)[:, :, 0, :]
            numbers = [lambda: chain(dve.tensor_copy(top_id, top_pos)),
                       lambda: chain(dve.tensor_scalar(highs, highs, float(NKEY), None, ALU.mult))]
            pair = 0
            for g, pairs in enumerate(BEST_PAIRS):
                steps = [f for n in range(pair, pair + pairs) for f in largest(n, (best, best_pos, cand_val), best_step)]
                if g == 0:
                    steps = candidates(cand_val, top_val) + [lambda: dve.wait_ge(dve_step, step.n)] + steps
                if g == len(BEST_PAIRS) - 1:
                    steps = numbers + candidates(cand_id, top_id) + steps
                beside(4 * (G_CAND + g), steps)
                pair += pairs
            dve.wait_ge(best_step, 5 * NT * PH)
            dve.wait_ge(dve_step, step.n)
            gate = chosen[:, 2 * NT:3 * NT, :].rearrange("p t (h k) -> p (t h) k", k=TOPK)
            dve.tensor_tensor(gate, best, best[:, :, 0:1].broadcast_to([P, NT * PH, TOPK]),
                              ALU.subtract).then_inc(best_centred, 1)
            chain(dve.tensor_copy(best_at, best_pos))

            def match_list(m, first=False):
                at_, ids, got = (x[:, bass.ds(m, 1), :].rearrange("p h k -> p (h k)") for x in (best_at, cand_id, expert))

                def after(k, emit):
                    if not (first and k == 0):
                        dve.wait_ge(match_step, m * 3 + k)
                    emit().then_inc(match_step, 1)

                return [lambda: after(0, lambda: dve.tensor_tensor(
                            match, iota_cand[:].unsqueeze(1).broadcast_to([P, TOPK, NCAND]),
                            at_.unsqueeze(2).broadcast_to([P, TOPK, NCAND]), ALU.is_equal)),
                        lambda: after(1, lambda: dve.tensor_tensor(
                            match, match, ids.unsqueeze(1).broadcast_to([P, TOPK, NCAND]), ALU.mult)),
                        lambda: after(2, lambda: dve.tensor_reduce(got, match, AX, ALU.add))]

            def match_round(r, first=False):
                beside(r * 12 + 4 * G_MATCH, [f for n in range(4) for f in match_list(r * 4 + n, first and n == 0)], 24)

            match_round(0, True)
            with dve.Fori(1, MATCH_ROUNDS) as r:
                match_round(r)
            dve.wait_ge(match_step, 3 * NT * PH)

            total = stat[:, 0, 0:NT * PH]

            def take_digits():
                chain(dve.tensor_copy(expert_i, expert.rearrange("p h k -> p (h k)")))
                step.on(dve.tensor_scalar(digit[:, 0:2 * P], expert_i, 7, None, ALU.arith_shift_right))
                chain(dve.tensor_scalar(digit[:, 2 * P:4 * P], expert_i, NKEY - 1, None, ALU.bitwise_and))

            def sum_gates():
                dve.wait_ge(gates_exp, 1)
                chain(dve.tensor_reduce(total, gate, AX, ALU.add))
                chain(dve.reciprocal(total, total))

            def take_route():
                dve.wait_ge(route_psum, 1)
                dve.tensor_copy(route_t.rearrange("p n t -> p (n t)"), bank(6, 2)[:, 0:3 * SEQ]).then_inc(route_ready, 1)

            beside(4 * G_GATES, [
                sum_gates,
                take_digits,
                lambda: chain(dve.tensor_copy(chosen[:, 0:2 * NT, :].rearrange("p n k -> p (n k)"), digit)),
                lambda: dve.tensor_tensor(gate, gate, total.unsqueeze(2).broadcast_to([P, NT * PH, TOPK]),
                                          ALU.mult).then_inc(routed, 1),
                lambda: None,
                lambda: None,
                lambda: None,
                take_route])
            dve.wait_ge(route_ready, 1)

            def hot_rows(n, b, first=False):
                if not first:
                    dve.wait_ge(g_done, n - 3)
                for w, rows in ((1, hot_j[:, b]), (0, hot_i[b])):
                    ins = dve.tensor_tensor(rows, iota_key[:].unsqueeze(1).broadcast_to([P, 4, P]),
                                            route_t[:, w, bass.ds(n * 4, 4)].unsqueeze(2).broadcast_to([P, 4, P]),
                                            ALU.is_equal)
                ins.then_inc(hots_ready, 1)

            def build_pair(g, n, first=False):
                for p in range(16):
                    low_part((g + p // 8) * 4 + p // 2 % 4, p // 2 % 4, p % 2)
                    if p in PLACES:
                        m = PLACES.index(p)
                        hot_rows(n + m, m % 4, first and m < 4)

            dve.wait_ge(h_stored, 16)
            build_pair(G_BUILD, 0, True)
            with dve.Fori(1, PAIRS) as r:
                build_pair(r * 2 + G_BUILD, r * len(PLACES))
            for p in range(8):
                low_part(NKEY - 4 + p // 2, p // 2, p % 2)
                if p < 4:
                    hot_rows(QUADS - 4 + p, p)

            def multiply(g, s, first=False):
                c = g * 4 + s
                if first:
                    dve.wait_ge(first_gelus_loaded[g - GROUPS], 16)
                else:
                    dve.wait_ge(gelu_loaded[s], 16 * (g - (GROUPS + 1)))
                part = big[:, bass.ds((c - NKEY) * SEQ, SEQ)]
                kept = first_gelus[:, g - GROUPS, s, :] if first else gelus[:, s, :]
                dve.tensor_tensor(part, part, kept, ALU.mult).then_inc(acts_ready, 1)

            def low_v(g, s):
                for a in range(2):
                    part = 2 * (s % 2) + a
                    dve.wait_ge(part_hi_ready, 2 * (g * 4 + s) + (a + 1))
                    dve.tensor_tensor(v_lo[s // 2][:, part, :], raw[:, s, a * 512:(a + 1) * 512],
                                      v_hi[s // 2][:, part, :].bitcast(F32), ALU.subtract).then_inc(part_lo_ready, 1)

            def low_act(c, b):
                dve.wait_ge(a_hi_ready, c - (NKEY - 1))
                dve.tensor_tensor(a_lo[:, b, :], big[:, bass.ds((c - NKEY) * SEQ, SEQ)],
                                  a_hi[:, b, :].bitcast(F32), ALU.subtract).then_inc(a_lo_ready, 1)

            dve.wait_ge(g_taken, QUADS)
            for s in range(4):
                multiply(GROUPS, s, True)
                low_v(GROUPS, s)
                if s < 2:
                    low_act(NKEY + s, s)
            for s in range(4):
                low_v(GROUPS + 1, s)
                low_act((GROUPS + 1) * 4 + s - 2, s % 2)
                multiply(GROUPS + 1, s, True)
            with dve.Fori(GROUPS + 2, 2 * GROUPS) as g:
                for s in range(4):
                    low_v(g, s)
                    low_act(g * 4 + (s - 2), s % 2)
                    multiply(g, s)
            low_act(2 * NKEY - 2, 0)
            low_act(2 * NKEY - 1, 1)
            dve.wait_ge(h_back_loaded, 16)
            for a in range(2):
                dve.wait_ge(part_used, 4 * NKEY - 1 + a)
                for t in range(NT):
                    part = h_back[:, (2 * t + a) * 512:(2 * t + a + 1) * 512]
                    dve.tensor_tensor(part, part, bank(2 * t + a), ALU.add).then_inc(out_ready, 1)


def kernel(x, mem, positions, norm_mix_g, w_in, qnorm_g_dil, knorm_g_dil, out_norm_g_dil, out_norm_g_sb, w_out,
           norm_mem_g, norm_memtok_g, w_q_mem, w_kv_mem, qnorm_g_mem, knorm_g_mem, w_o_mem, norm_ffn_g, w_q_peer,
           peer_sub_keys, peer_u, peer_v):
    import concourse.bacc as bacc
    from concourse.bass_utils import run_bass_kernel_spmd

    def blocks(w, n):
        k, c = w.shape[0] // P, w.shape[1] // n
        return np.ascontiguousarray(w.reshape(k, P, n, c).transpose(2, 1, 0, 3))

    def halves(units):
        n, p, k, c = units.shape
        return units.reshape(n, p, 2, k // 2, c).transpose(0, 2, 1, 3, 4).reshape(2 * n, p, k * c // 2)

    w_in, w_out, w_q_peer = np.asarray(w_in)[0], np.asarray(w_out)[0], np.asarray(w_q_peer)[0]
    w_kv = np.asarray(w_kv_mem)[0]
    mix = blocks(w_in, 6)
    keys = np.asarray(peer_sub_keys)[0].reshape(NBLK, NKEY, P).transpose(2, 0, 1).reshape(1, P, WHALF)
    weights = np.concatenate(
        [halves(mix[[3, 4, 0, 1, 5, 2]]), halves(blocks(w_kv, 2)[:1]), halves(blocks(w_out, 2)),
         halves(blocks(np.asarray(w_q_mem)[0], 1)), halves(blocks(w_kv, 2)[1:]),
         halves(blocks(np.asarray(w_o_mem)[0], 1)),
         halves(blocks(w_q_peer, PEER_UNITS)), keys], axis=0)
    row_gains = np.stack([np.asarray(norm_mix_g)[0], np.asarray(norm_memtok_g)[0],
                          np.concatenate([np.asarray(out_norm_g_dil)[0], np.asarray(out_norm_g_sb)[0]]),
                          np.asarray(norm_mem_g)[0], np.asarray(norm_ffn_g)[0]])
    cols = np.ascontiguousarray(np.stack([np.asarray(qnorm_g_mem)[0], np.asarray(knorm_g_mem)[0]], axis=1))
    head_gains = np.concatenate([np.asarray(qnorm_g_dil), np.asarray(knorm_g_dil)], axis=0)
    u_t = np.ascontiguousarray(np.asarray(peer_u)[0].reshape(NKEY, NKEY, KD, P).transpose(0, 3, 2, 1)).reshape(NKEY, P, D)
    v_t = np.asarray(peer_v)[0].reshape(NKEY, P, D)
    pos = np.ascontiguousarray(np.asarray(positions).reshape(NT, P).T)
    arrays = {"x": np.asarray(x)[0], "mem": np.asarray(mem)[0], "pos": pos, "weights": weights,
              "row_gains": row_gains, "cols": cols,
              "head_gains": head_gains, "u_t": u_t, "v_t": v_t}
    nc = bacc.Bacc("TRN2", target_bir_lowering=False, num_devices=1)
    args = [nc.dram_tensor(n, a.shape, mybir.dt.from_np(a.dtype), kind="ExternalInput").ap() for n, a in arrays.items()]
    out = nc.dram_tensor("out", (SEQ, D), F32, kind="ExternalOutput").ap()
    h_kept = nc.dram_tensor("h_kept", (P, NT * D), F32).ap()
    gelu_kept = nc.dram_tensor("gelu_kept", (NKEY, P, SEQ), F32).ap()
    hybrid_layer(nc, *args, out, h_kept, gelu_kept)
    r = run_bass_kernel_spmd(nc, [arrays], core_ids=[0])
    return r.results[0]["out"].reshape(1, SEQ, D)
```
